# Optimizing a Trainium2 kernel written in Bass

```python
import jax, jax.numpy as jnp
from jax import lax
import numpy as np

D_MODEL = 1024
BATCH = 1
SEQ = 128
DEPTH = 2
DEC_BATCH = 1
DEC_SEQ = 128
PAST_LEN = 128

GRID_W = 64
A_HEADS = 8
A_KV_HEADS = 2
A_HEAD_DIM = 64
A_WINDOW = 128
A_BLOCK = 128
ROPE_BASE = 10000.0
B_HEADS = 4
B_HEAD_DIM = 64
B_DECAY_RANK = 64
B_AAA_RANK = 64
B_GATE_RANK = 128
B_GN_EPS = 64e-5
C_HEADS = 4
C_KEY_DIM = 32
C_VAL_DIM = 64
C_GATE_RANK = 16
C_GATE_NORM = 16.0
C_CHUNK = 64
D_FF = 2816
N_EXPERTS = 8
TOP_K = 2
D_FF_EXPERT = 3584
LN_EPS = 1e-5
DN_ALPHA = (2.0 * DEPTH) ** 0.25
DN_BETA = (8.0 * DEPTH) ** -0.25

A_Q_W = A_HEADS * A_HEAD_DIM
A_KV_W = A_KV_HEADS * A_HEAD_DIM
B_W = B_HEADS * B_HEAD_DIM
C_K_W = C_HEADS * C_KEY_DIM
C_V_W = C_HEADS * C_VAL_DIM
IN_SPLITS = (A_Q_W, A_KV_W, A_KV_W, B_W, B_W, B_W, C_K_W, C_K_W, C_V_W, C_V_W, D_MODEL, D_MODEL, D_MODEL)
IN_W = sum(IN_SPLITS)
NEG_INF = -1e30
F32 = jnp.float32

kernel_name = "hybrid_prefix_swa_rwkv7_gla_diffusion_step"

def _layer_norm(x, g, b):
    xf = x.astype(F32)
    mu = jnp.mean(xf, -1, keepdims=True)
    var = jnp.mean(jnp.square(xf - mu), -1, keepdims=True)
    return ((xf - mu) * lax.rsqrt(var + LN_EPS) * g.astype(F32) + b.astype(F32)).astype(x.dtype)

def _sink_softmax(logits, sink):
    m = jnp.maximum(jnp.max(logits, -1, keepdims=True), sink)
    e = jnp.exp(logits - m)
    return e / (jnp.sum(e, -1, keepdims=True) + jnp.exp(sink - m))

def _flip(t):
    return t[:, ::-1]

def _axial_rope(x):
    T = x.shape[1]
    n_rows = T // GRID_W
    rows = jnp.repeat(jnp.arange(n_rows, dtype=F32), GRID_W)
    cols = jnp.tile(jnp.arange(GRID_W, dtype=F32), n_rows)
    half = A_HEAD_DIM // 2
    inv_freq = ROPE_BASE ** (-jnp.arange(0, half, 2, dtype=F32) / half)

    def rot(xa, pos):
        ang = pos[:, None] * inv_freq[None, :]
        cos = jnp.cos(ang)[None, :, None, :]
        sin = jnp.sin(ang)[None, :, None, :]
        x1, x2 = xa[..., :half // 2], xa[..., half // 2:]
        return jnp.concatenate([x1 * cos - x2 * sin, x1 * sin + x2 * cos], -1)

    xf = x.astype(F32)
    return jnp.concatenate([rot(xf[..., :half], rows), rot(xf[..., half:], cols)], -1).astype(x.dtype)

def _attn_context(q, k, v, sink):
    B, S = q.shape[:2]
    G = A_HEADS // A_KV_HEADS
    qg = q.reshape(B, S, A_KV_HEADS, G, A_HEAD_DIM)
    s = jnp.einsum('bqkgd,bskd->bkgqs', qg, k).astype(F32) * (A_HEAD_DIM ** -0.5)
    p = _sink_softmax(s, sink.astype(F32).reshape(1, A_KV_HEADS, G, 1, 1))
    o = jnp.einsum('bkgqs,bskd->bqkgd', p.astype(v.dtype), v)
    return o.reshape(B, S, A_Q_W)

def _attn_latent(q, k, v, k_ctx, v_ctx, sink):
    B, T = q.shape[:2]
    nb = T // A_BLOCK
    G = A_HEADS // A_KV_HEADS
    q = _axial_rope(q)
    k = _axial_rope(k)
    qb = q.reshape(B, nb, A_BLOCK, A_KV_HEADS, G, A_HEAD_DIM)
    pad = ((0, 0), (A_BLOCK, A_BLOCK), (0, 0), (0, 0))
    kp = jnp.pad(k, pad).reshape(B, nb + 2, A_BLOCK, A_KV_HEADS, A_HEAD_DIM)
    vp = jnp.pad(v, pad).reshape(B, nb + 2, A_BLOCK, A_KV_HEADS, A_HEAD_DIM)
    kband = jnp.concatenate([kp[:, :-2], kp[:, 1:-1], kp[:, 2:]], axis=2)
    vband = jnp.concatenate([vp[:, :-2], vp[:, 1:-1], vp[:, 2:]], axis=2)
    scale = A_HEAD_DIM ** -0.5
    s_loc = jnp.einsum('bnqkgd,bnskd->bnkgqs', qb, kband).astype(F32) * scale
    qi = jnp.arange(A_BLOCK)[:, None]
    kj = jnp.arange(3 * A_BLOCK)[None, :]
    rel = kj - A_BLOCK - qi
    kpos = (jnp.arange(nb)[:, None, None] - 1) * A_BLOCK + kj[None]
    valid = (jnp.abs(rel)[None] <= A_WINDOW) & (kpos >= 0) & (kpos < T)
    s_loc = jnp.where(valid[None, :, None, None], s_loc, NEG_INF)
    s_ctx = jnp.einsum('bnqkgd,bpkd->bnkgqp', qb, k_ctx).astype(F32) * scale
    s = jnp.concatenate([s_loc, s_ctx], -1)
    p = _sink_softmax(s, sink.astype(F32).reshape(1, 1, A_KV_HEADS, G, 1, 1))
    p_loc = p[..., :3 * A_BLOCK].astype(v.dtype)
    p_ctx = p[..., 3 * A_BLOCK:].astype(v.dtype)
    o = (jnp.einsum('bnkgqs,bnskd->bnqkgd', p_loc, vband)
         + jnp.einsum('bnkgqp,bpkd->bnqkgd', p_ctx, v_ctx))
    return o.reshape(B, T, A_Q_W)

def _rwkv_scan(r, w, kk, a, v, kt, s0):
    def step(S, xs):
        r_t, w_t, kk_t, a_t, v_t, k_t = xs
        sk = jnp.einsum('bhvk,bhk->bhv', S, kk_t)
        S = S * w_t[:, :, None, :] - sk[..., None] * (a_t * kk_t)[:, :, None, :] + v_t[..., :, None] * k_t[..., None, :]
        return S, jnp.einsum('bhvk,bhk->bhv', S, r_t)

    xs = tuple(jnp.moveaxis(t, 1, 0) for t in (r, w, kk, a, v, kt))
    S, y = lax.scan(step, s0, xs)
    return jnp.moveaxis(y, 0, 1), S

def _rwkv_branch(h, r, k, v, P, l, s0):
    B, T, _ = h.shape
    hs = (B, T, B_HEADS, B_HEAD_DIM)
    rf = r.astype(F32).reshape(hs)
    kf = k.astype(F32).reshape(hs)
    vf = v.astype(F32).reshape(hs)
    kk = kf * P['rwkv_k_k'][l].astype(F32).reshape(B_HEADS, B_HEAD_DIM)
    kk = kk * lax.rsqrt(jnp.sum(kk * kk, -1, keepdims=True) + 1e-12)
    k_a = P['rwkv_k_a'][l].astype(F32).reshape(B_HEADS, B_HEAD_DIM)
    r_k = P['rwkv_r_k'][l].astype(F32)
    y = jnp.zeros(hs, F32)
    bonus = jnp.zeros(hs, F32)
    finals = []
    for d in range(2):
        z = (P['rwkv_w0'][l, d] + jnp.tanh(h @ P['rwkv_w_a'][l, d]) @ P['rwkv_w_b'][l, d]).astype(F32)
        w = jnp.exp(-jnp.exp(-jax.nn.softplus(-z) - 0.5)).reshape(hs)
        a = jax.nn.sigmoid((P['rwkv_a0'][l, d] + (h @ P['rwkv_a_a'][l, d]) @ P['rwkv_a_b'][l, d]).astype(F32)).reshape(hs)
        kt = kf * (1.0 + (a - 1.0) * k_a)
        seq = (rf, w, kk, a, vf, kt)
        if d == 1:
            seq = tuple(_flip(t) for t in seq)
        yd, sd = _rwkv_scan(*seq, s0[:, d].astype(F32))
        if d == 1:
            yd = _flip(yd)
        y = y + yd
        bonus = bonus + jnp.sum(rf * kt * r_k, -1, keepdims=True) * vf
        finals.append(sd)
    mu = jnp.mean(y, -1, keepdims=True)
    var = jnp.mean(jnp.square(y - mu), -1, keepdims=True)
    y = ((y - mu) * lax.rsqrt(var + B_GN_EPS)).reshape(B, T, B_W)
    y = y * P['rwkv_ln_g'][l].astype(F32) + P['rwkv_ln_b'][l].astype(F32) + bonus.reshape(B, T, B_W)
    g = jax.nn.sigmoid(h @ P['rwkv_g_a'][l]) @ P['rwkv_g_b'][l]
    return y.astype(h.dtype) * g, jnp.stack(finals, 1)

def _gla_chunked(q, k, v, log_a, s0):
    B, T, H, K = q.shape
    V = v.shape[-1]
    n = T // C_CHUNK
    q = q.reshape(B, n, C_CHUNK, H, K)
    k = k.reshape(B, n, C_CHUNK, H, K)
    v = v.reshape(B, n, C_CHUNK, H, V)
    b = jnp.cumsum(log_a.reshape(B, n, C_CHUNK, H, K), axis=2)
    causal = jnp.tril(jnp.ones((C_CHUNK, C_CHUNK), bool))[None, None, :, :, None, None]
    dec = jnp.exp(jnp.where(causal, b[:, :, :, None] - b[:, :, None, :], -jnp.inf))
    att = jnp.einsum('bnthk,bnshk,bntshk->bnhts', q, k, dec)
    o = jnp.einsum('bnhts,bnshv->bnthv', att, v)
    b_last = b[:, :, -1]
    u = jnp.einsum('bnshk,bnshv->bnhkv', k * jnp.exp(b_last[:, :, None] - b), v)

    def step(S, xs):
        d_last, u_n = xs
        return d_last[..., None] * S + u_n, S

    S_fin, S_start = lax.scan(step, s0, (jnp.moveaxis(jnp.exp(b_last), 1, 0), jnp.moveaxis(u, 1, 0)))
    o = o + jnp.einsum('bnthk,bnhkv->bnthv', q * jnp.exp(b), jnp.moveaxis(S_start, 0, 1))
    return o.reshape(B, T, H, V), S_fin

def _gla_branch(h, q, k, v, og, P, l, s0):
    B, T, _ = h.shape
    qf = q.astype(F32).reshape(B, T, C_HEADS, C_KEY_DIM) * (C_KEY_DIM ** -0.5)
    kf = k.astype(F32).reshape(B, T, C_HEADS, C_KEY_DIM)
    vf = v.astype(F32).reshape(B, T, C_HEADS, C_VAL_DIM)
    o = jnp.zeros((B, T, C_HEADS, C_VAL_DIM), F32)
    finals = []
    for d in range(2):
        gl = (h @ P['gla_gate_a'][l, d]) @ P['gla_gate_b'][l, d] + P['gla_gate_bias'][l, d]
        log_a = (jax.nn.log_sigmoid(gl.astype(F32)) / C_GATE_NORM).reshape(B, T, C_HEADS, C_KEY_DIM)
        seq = (qf, kf, vf, log_a)
        if d == 1:
            seq = tuple(_flip(t) for t in seq)
        od, sd = _gla_chunked(*seq, s0[:, d].astype(F32))
        if d == 1:
            od = _flip(od)
        o = o + od
        finals.append(sd)
    o = o * lax.rsqrt(jnp.mean(o * o, -1, keepdims=True) + LN_EPS) * P['gla_norm_g'][l].astype(F32)
    return o.reshape(B, T, C_V_W).astype(h.dtype) * jax.nn.silu(og), jnp.stack(finals, 1)

def _token_mixer(h, P, l, ctx):
    B, T, _ = h.shape
    idx = np.cumsum(IN_SPLITS)[:-1]
    aq, ak, av, br, bk, bv, cq, ck, cv, cog, ga, gb, gc = jnp.split(h @ P['w_in'][l], idx, axis=-1)
    aq = aq.reshape(B, T, A_HEADS, A_HEAD_DIM)
    ak = ak.reshape(B, T, A_KV_HEADS, A_HEAD_DIM)
    av = av.reshape(B, T, A_KV_HEADS, A_HEAD_DIM)
    if ctx is None:
        o_a = _attn_context(aq, ak, av, P['attn_sink'][l])
        s_r0 = jnp.zeros((B, 2, B_HEADS, B_HEAD_DIM, B_HEAD_DIM), F32)
        s_g0 = jnp.zeros((B, 2, C_HEADS, C_KEY_DIM, C_VAL_DIM), F32)
    else:
        k_ctx, v_ctx, s_r0, s_g0 = ctx
        o_a = _attn_latent(aq, ak, av, k_ctx.astype(h.dtype), v_ctx.astype(h.dtype), P['attn_sink'][l])
    o_b, s_r = _rwkv_branch(h, br, bk, bv, P, l, s_r0)
    o_c, s_g = _gla_branch(h, cq, ck, cv, cog, P, l, s_g0)
    merged = (jax.nn.sigmoid(ga) * (o_a @ P['w_up_a'][l])
              + jax.nn.sigmoid(gb) * (o_b @ P['w_up_b'][l])
              + jax.nn.sigmoid(gc) * (o_c @ P['w_up_c'][l]))
    return merged @ P['w_out'][l], (ak, av, s_r, s_g)

def _dense_ffn(h, P, i):
    return (jax.nn.silu(h @ P['ffn_w_gate'][i]) * (h @ P['ffn_w_up'][i])) @ P['ffn_w_down'][i]

def _moe_ffn(h, P, i):
    B, T, D = h.shape
    xt = h.reshape(B * T, D)
    logits = (xt @ P['moe_router'][i]).astype(F32)
    top_v, top_i = lax.top_k(logits, TOP_K)
    w = jax.nn.softmax(top_v, axis=-1)
    gates = jnp.sum(w[..., None] * jax.nn.one_hot(top_i, N_EXPERTS, dtype=F32), axis=1).astype(h.dtype)
    out = jnp.zeros_like(xt)
    for e in range(N_EXPERTS):
        y = (jax.nn.silu(xt @ P['moe_w_gate'][i, e]) * (xt @ P['moe_w_up'][i, e])) @ P['moe_w_down'][i, e]
        out = out + gates[:, e:e + 1] * y
    return out.reshape(B, T, D)

def _trunk(x, cvec, P, caches):
    kept = []
    for l in range(DEPTH):
        mod = (jax.nn.silu(cvec) @ P['w_ada'][l] + P['b_ada'][l])[:, None, :]
        sh1, sc1, g1, sh2, sc2, g2 = jnp.split(mod, 6, axis=-1)
        ctx = None if caches is None else tuple(t[:, l] for t in caches)
        mix, ctx_tensors = _token_mixer(x * (1.0 + sc1) + sh1, P, l, ctx)
        x = _layer_norm(DN_ALPHA * x + g1 * mix, P['ln1_g'][l], P['ln1_b'][l])
        h = x * (1.0 + sc2) + sh2
        f = _dense_ffn(h, P, l // 2) if l % 2 == 0 else _moe_ffn(h, P, l // 2)
        x = _layer_norm(DN_ALPHA * x + g2 * f, P['ln2_g'][l], P['ln2_b'][l])
        kept.append(ctx_tensors)
    return x, kept

def setup_inputs(seed: int = 0) -> dict:
    key = jax.random.key(seed)
    ks = iter(jax.random.split(key, 64))

    def nrm(shape, scale=1.0):
        return jax.random.normal(next(ks), shape, F32) * scale

    L = DEPTH
    nd = (DEPTH + 1) // 2
    nm = DEPTH // 2
    D = D_MODEL
    return {
        'x_prompt': nrm((BATCH, SEQ, D)),
        'x_sample': nrm((DEC_BATCH, DEC_SEQ, D)),
        'cache_attn_k': nrm((DEC_BATCH, L, PAST_LEN, A_KV_HEADS, A_HEAD_DIM)),
        'cache_attn_v': nrm((DEC_BATCH, L, PAST_LEN, A_KV_HEADS, A_HEAD_DIM)),
        'state_rwkv': nrm((DEC_BATCH, L, 2, B_HEADS, B_HEAD_DIM, B_HEAD_DIM), 0.3),
        'state_gla': nrm((DEC_BATCH, L, 2, C_HEADS, C_KEY_DIM, C_VAL_DIM), 0.3),
        'c': nrm((DEC_BATCH, D)),
        'c_ctx': nrm((D,)),
        'w_ada': nrm((L, D, 6 * D), D ** -0.5),
        'b_ada': nrm((L, 6 * D), 0.02),
        'w_in': nrm((L, D, IN_W), D ** -0.5),
        'attn_sink': nrm((L, A_HEADS), 0.5),
        'rwkv_w0': nrm((L, 2, B_W), 0.5),
        'rwkv_w_a': nrm((L, 2, D, B_DECAY_RANK), D ** -0.5),
        'rwkv_w_b': nrm((L, 2, B_DECAY_RANK, B_W), 0.5 * B_DECAY_RANK ** -0.5),
        'rwkv_a0': nrm((L, 2, B_W), 0.5),
        'rwkv_a_a': nrm((L, 2, D, B_AAA_RANK), D ** -0.5),
        'rwkv_a_b': nrm((L, 2, B_AAA_RANK, B_W), 0.5 * B_AAA_RANK ** -0.5),
        'rwkv_g_a': nrm((L, D, B_GATE_RANK), D ** -0.5),
        'rwkv_g_b': nrm((L, B_GATE_RANK, B_W), B_GATE_RANK ** -0.5),
        'rwkv_k_k': 0.85 + nrm((L, B_W), 0.05),
        'rwkv_k_a': 1.0 + nrm((L, B_W), 0.05),
        'rwkv_r_k': nrm((L, B_HEADS, B_HEAD_DIM), 0.1),
        'rwkv_ln_g': 1.0 + nrm((L, B_W), 0.02),
        'rwkv_ln_b': nrm((L, B_W), 0.02),
        'gla_gate_a': nrm((L, 2, D, C_GATE_RANK), D ** -0.5),
        'gla_gate_b': nrm((L, 2, C_GATE_RANK, C_K_W), C_GATE_RANK ** -0.5),
        'gla_gate_bias': 1.0 + nrm((L, 2, C_K_W), 0.5),
        'gla_norm_g': 1.0 + nrm((L, C_VAL_DIM), 0.02),
        'w_up_a': nrm((L, A_Q_W, D), A_Q_W ** -0.5),
        'w_up_b': nrm((L, B_W, D), B_W ** -0.5),
        'w_up_c': nrm((L, C_V_W, D), C_V_W ** -0.5),
        'w_out': nrm((L, D, D), DN_BETA * D ** -0.5),
        'ln1_g': 1.0 + nrm((L, D), 0.02),
        'ln1_b': nrm((L, D), 0.02),
        'ln2_g': 1.0 + nrm((L, D), 0.02),
        'ln2_b': nrm((L, D), 0.02),
        'ffn_w_gate': nrm((nd, D, D_FF), D ** -0.5),
        'ffn_w_up': nrm((nd, D, D_FF), D ** -0.5),
        'ffn_w_down': nrm((nd, D_FF, D), DN_BETA * D_FF ** -0.5),
        'moe_router': nrm((nm, D, N_EXPERTS), D ** -0.5),
        'moe_w_gate': nrm((nm, N_EXPERTS, D, D_FF_EXPERT), D ** -0.5),
        'moe_w_up': nrm((nm, N_EXPERTS, D, D_FF_EXPERT), D ** -0.5),
        'moe_w_down': nrm((nm, N_EXPERTS, D_FF_EXPERT, D), DN_BETA * D_FF_EXPERT ** -0.5),
    }

def reference(x_prompt, x_sample, cache_attn_k, cache_attn_v, state_rwkv, state_gla, c, c_ctx,
              w_ada, b_ada, w_in, attn_sink,
              rwkv_w0, rwkv_w_a, rwkv_w_b, rwkv_a0, rwkv_a_a, rwkv_a_b, rwkv_g_a, rwkv_g_b,
              rwkv_k_k, rwkv_k_a, rwkv_r_k, rwkv_ln_g, rwkv_ln_b,
              gla_gate_a, gla_gate_b, gla_gate_bias, gla_norm_g,
              w_up_a, w_up_b, w_up_c, w_out, ln1_g, ln1_b, ln2_g, ln2_b,
              ffn_w_gate, ffn_w_up, ffn_w_down, moe_router, moe_w_gate, moe_w_up, moe_w_down):
    P = dict(w_ada=w_ada, b_ada=b_ada, w_in=w_in, attn_sink=attn_sink,
             rwkv_w0=rwkv_w0, rwkv_w_a=rwkv_w_a, rwkv_w_b=rwkv_w_b, rwkv_a0=rwkv_a0,
             rwkv_a_a=rwkv_a_a, rwkv_a_b=rwkv_a_b, rwkv_g_a=rwkv_g_a, rwkv_g_b=rwkv_g_b,
             rwkv_k_k=rwkv_k_k, rwkv_k_a=rwkv_k_a, rwkv_r_k=rwkv_r_k,
             rwkv_ln_g=rwkv_ln_g, rwkv_ln_b=rwkv_ln_b,
             gla_gate_a=gla_gate_a, gla_gate_b=gla_gate_b, gla_gate_bias=gla_gate_bias, gla_norm_g=gla_norm_g,
             w_up_a=w_up_a, w_up_b=w_up_b, w_up_c=w_up_c, w_out=w_out,
             ln1_g=ln1_g, ln1_b=ln1_b, ln2_g=ln2_g, ln2_b=ln2_b,
             ffn_w_gate=ffn_w_gate, ffn_w_up=ffn_w_up, ffn_w_down=ffn_w_down,
             moe_router=moe_router, moe_w_gate=moe_w_gate, moe_w_up=moe_w_up, moe_w_down=moe_w_down)
    y_prompt, kept = _trunk(x_prompt, c_ctx[None, :], P, None)
    y_sample, _ = _trunk(x_sample, c, P, (cache_attn_k, cache_attn_v, state_rwkv, state_gla))
    new_attn_k = jnp.stack([t[0] for t in kept], axis=1)
    new_attn_v = jnp.stack([t[1] for t in kept], axis=1)
    new_state_rwkv = jnp.stack([t[2] for t in kept], axis=1)
    new_state_gla = jnp.stack([t[3] for t in kept], axis=1)
    return (y_prompt, y_sample, new_attn_k, new_attn_v, new_state_rwkv, new_state_gla)


_drawn_inputs = setup_inputs


def setup_inputs(seed=0):
    import zlib

    import numpy as np

    out = dict(_drawn_inputs(seed))
    spreads = {}
    factors = {'cache_attn_k': 2.678,
     'state_rwkv': 8.0,
     'state_gla': 5.664,
     'attn_sink': 21.907,
     'rwkv_k_k': 10.118,
     'rwkv_ln_g': 25.637,
     'rwkv_ln_b': 26.616,
     'gla_norm_g': 21.583}
    for name, (base, spread) in spreads.items():
        noise = np.random.default_rng([zlib.crc32(name.encode()), seed]).standard_normal(out[name].shape)
        drawn = base * np.exp(spread * noise) if base else spread * noise
        out[name] = __import__('jax').numpy.asarray(drawn.astype(out[name].dtype))
    for name, factor in factors.items():
        out[name] = (out[name] * factor).astype(out[name].dtype)
    return out
```

```python
from contextlib import ExitStack

import numpy as np

import concourse.bass as bass
from concourse import mybir

ALU = mybir.AluOpType
ACT = mybir.ActivationFunctionType
AX = mybir.AxisListType
F32 = mybir.dt.float32
U32 = mybir.dt.uint32

P = 128
D = 1024
KC = D // P
TOK = 2 * P
L = 2
TW = 256
RING = 6
FF = 2816
FFE = 3584
NE = 8
DENSE_UNITS = FF // TW
EXPERT_UNITS = FFE // TW
MOE_UNITS = NE * EXPERT_UNITS
ADA_TILES = 6 * D // TW
LN_EPS = 1e-5
GN_EPS = 64e-5
ALPHA = (2.0 * L) ** 0.25
LEVELS = 6

SMALL = ["decay_rate", "gate_gla"]
FIRST = SMALL + ["q0", "q1", "kv", "br", "bk", "bv", "cqk", "cv", "cog"]
GATES = [f"gate{i}" for i in range(12)]
PROJ = FIRST + GATES
MIX = PROJ + ["up_a0", "up_a1", "up_b", "up_c"] + [f"out{i}" for i in range(4)]
MIX_DMAS = {"q0": 4, "q1": 4, "decay_rate": 4, "gate_gla": 3, "up_a0": 2, "up_a1": 2}
MIX_TILES = len(MIX)

CST = {}


def build_constants():
    t = np.arange(P)
    row, col = t[:, None], t[None, :]
    parts = []

    def add(name, a):
        CST[name] = (sum(x.shape[1] for x in parts), a.shape[1])
        parts.append(a.astype(np.float32))

    add("ident", row == col)
    add("ones", np.ones((P, P)))
    add("mean_d", np.full((P, P), 1.0 / D))
    add("blk", row // 64 == col // 64)
    add("blkm", (row // 64 == col // 64) / 64.0)
    decay = -np.exp(-0.5)
    le, lt, ge, gt = row <= col, row < col, row >= col, row > col
    first, second = row < 64, row >= 64
    for d, (inc, exc, cen) in enumerate([(le, lt, first), (ge, gt, second)]):
        add(f"tri{d}", np.concatenate([inc * 1.0 - cen, exc * 1.0 - cen], 1) * decay)
        add(f"trig{d}", (inc * 1.0 - cen) / 16.0)
        add(f"cen{d}", cen * decay)
        add(f"ceng{d}", cen / 16.0)
        add(f"mask{d}", np.concatenate([exc, exc, inc, inc], 1))
        pair = (row // 2 == col // 2) & (row != col)
        add(f"lv0T{d}", -1.0 * (exc & pair))
        add(f"lv0{d}", -1.0 * (exc.T & pair))
    for j in range(1, LEVELS + 1):
        add(f"lv{j}", (row // 2 ** (j + 1) == col // 2 ** (j + 1)) & (row // 2 ** j != col // 2 ** j))
    inv = (10000.0 ** (-np.arange(0, 32, 2, dtype=np.float32) / 32)).astype(np.float32)
    pos = np.stack([t // 64, t % 64]).astype(np.float32)
    dim = t % 64
    ang = (pos[dim // 32][:, :] * inv[dim % 16][:, None]).astype(np.float32)
    add("cos", np.cos(ang))
    add("sin", np.sin(ang))
    same = row // 32 == col // 32
    add("rot", 1.0 * (same & (row + 16 == col)) - 1.0 * (same & (row == col + 16)))
    add("hm64", (t[:, None] // 64 == np.arange(2)[None]))
    add("hm32", (t[:, None] // 32 == np.arange(4)[None]))
    add("iota8", np.broadcast_to(np.arange(8), (P, 8)))
    return np.concatenate(parts, 1)


NCST = build_constants().shape[1]


def build_program(nc, ins, outs):
    ctx = ExitStack()
    with ctx:
        def sb(name, shape, dt=F32):
            return ctx.enter_context(nc.sbuf_tensor(name, shape, dt))

        used_names = {}

        def sem(name):
            if name not in used_names:
                used_names[name] = ctx.enter_context(nc.semaphore(name))
            return used_names[name]

        ring = sb("ring", [P, RING, KC * TW])
        cst = sb("cst", [P, NCST])
        xT = sb("xT", [P, KC, TOK])
        hT = sb("hT", [P, KC, TOK])
        cT = sb("cT", [P, KC, 2])
        cS = sb("cS", [P, KC, 2])
        bada = sb("bada", [P, L, 48])
        mod = sb("mod", [P, L, 48, 2])
        lnp = sb("lnp", [P, L, 4, KC])
        rv = sb("rv", [P, L, 15])
        omk = sb("omk", [P, L, 2])
        w0row = sb("w0row", [1, L, 512])
        glbrow = sb("glbrow", [1, L, 256])
        sinkB = sb("sinkB", [P, L, 8])
        wbB = sb("wbB", [P, 512])
        abB = sb("abB", [P, 512])
        gbw = sb("gbw", [P, 256])
        glb = sb("glb", [32, 256])
        s0r = sb("s0r", [P, 4, 64])
        s0g = sb("s0g", [P, 2, 64])
        kcT = sb("kcT", [P, P])
        vc = sb("vc", [P, P])
        router = sb("router", [P, KC, NE])
        tanhT = sb("tanhT", [P, TOK])
        aaT = sb("aaT", [P, TOK])
        sgaT = sb("sgaT", [P, TOK])
        glaT = sb("glaT", [32, TOK])
        qT = sb("qT", [P, 4, TOK])
        kT = sb("kT", [P, TOK])
        av = sb("av", [P, 2, P])
        rT = sb("rT", [P, 2, TOK])
        kfT = sb("kfT", [P, 2, TOK])
        vT = sb("vT", [P, 2, TOK])
        cqT = sb("cqT", [P, TOK])
        ckT = sb("ckT", [P, TOK])
        cv = sb("cv", [P, 2, 256])
        ogs = sb("ogs", [P, 2, TOK])
        oaT = sb("oaT", [P, 4, TOK])
        obT = sb("obT", [P, 2, TOK])
        ocT = sb("ocT", [P, 2, TOK])
        WORK, WIDE = 8832, 9600
        work = sb("work", [P, WORK])
        wide = sb("wide", [P, WIDE])
        small = sb("small", [P, 64])
        zeros = sb("zeros", [P, 512])
        idxu = sb("idxu", [P, 2, 8], U32)
        fstate = sb("fstate", [P, 2, 2, P])
        gstate = sb("gstate", [P, 2, 256])
        bank = [ctx.enter_context(nc.psum_tensor(f"bank{i}", [P, 512], F32)) for i in range(8)]

        def C(name):
            a, n = CST[name]
            return cst[:, a:a + n]

        def shaped(v, shape):
            names = "abcd"[:len(shape)]
            if len(shape) < 2:
                return v
            return v.rearrange(f"p ({' '.join(names)}) -> p {' '.join(names)}",
                               **{k: n for k, n in zip(names[:-1], shape[:-1])})

        def carver(area, size, start=0):
            at = [start]

            def cut(*shape):
                a, n = at[0], int(np.prod(shape))
                assert a + n <= size, (a, n, size)
                at[0] = a + n
                return shaped(area[:, a:a + n], shape)
            return cut

        def bk(i, *shape):
            return shaped(bank[i][:, 0:int(np.prod(shape))], shape)

        cut = carver(work, WORK)
        qL, kxL, kxP = cut(4, P), cut(2, 256), cut(2, P)
        pL, pP, pT = cut(8, 256), cut(8, P), cut(24, P)
        mneg, den, esink = cut(16), cut(16), cut(16)
        atmp, krot, rtmp_k = cut(4, P), cut(P), cut(P)
        cut = carver(work, WORK)
        sigz = cut(2, 512)
        aT, kapT, akT, ktT = cut(2, 2, TOK), cut(2, TOK), cut(2, 2, TOK), cut(2, 2, TOK)
        gT, bonT, Vn, yT, rtmp, rtmp2 = (cut(2, TOK) for _ in range(6))
        Bc, KcR = [cut(2, P) for _ in range(2)], [cut(2, P) for _ in range(2)]
        cut = carver(wide, WIDE)
        KR = [cut(2, 2, 2, P) for _ in range(2)]
        MTQ = [cut(2, 2, 2, P) for _ in range(2)]
        AKQ = [cut(2, 2, 2, P) for _ in range(2)]
        shared = 1024 * 6
        Tm, TmT = [cut(4, P) for _ in range(2)], [cut(4, P) for _ in range(2)]
        Xs, nU = [cut(256) for _ in range(2)], [cut(256) for _ in range(2)]
        s0c, ecr, elast = cut(4, 64), cut(4), cut(4)
        P1 = [qT[:, 2 * d:2 * d + 2, :].rearrange("p a (b t) -> p (a b) t", b=2) for d in range(2)]
        cut = carver(wide, WIDE, shared)
        Ep, En = [cut(2, 2, P) for _ in range(2)], [cut(2, P) for _ in range(2)]
        K2T = carver(wide, WIDE, shared)(2, 4, P)
        K2n = P1
        cut = carver(work, WORK)
        glog, gtm = cut(512), cut(512)
        EG, EGn, Qh = cut(4, P), cut(4, P), cut(P)
        Qx, KcG, attT = cut(4, 4, P), cut(4, P), cut(4, 4, P)
        K2g, K2gn, s0gc, ecg = cut(2, P), cut(2, P), cut(2, 64), cut(2)
        oc, gsq = cut(512), cut(512)
        sg = carver(wide, WIDE)(24, TOK)
        cut = carver(work, WORK)
        merged, mtmp, yLN, rstd = cut(KC, TOK), cut(KC, TOK), cut(KC, TOK), cut(TOK)
        cut = carver(work, WORK)
        hid, sgt = [cut(2, TOK) for _ in range(2)], [cut(2, TOK) for _ in range(2)]
        cut = carver(wide, WIDE)
        gateB, diag = cut(NE, TOK), cut(2, NE, P)
        cut = carver(small, 64)
        lg, top8, idxf, gts = cut(2, 8), cut(2, 8), cut(2, 8), cut(2, 8)

        block = ctx.enter_context(nc.Block())

        def w_tile(l, name):
            w_in = ins["w_in"][l].rearrange("(c p) n -> p c n", p=P)
            if name == "decay_rate":
                return [((slice(None), 64 * d + 128 * a, 64), ins[w][l, d].rearrange("(c p) n -> p c n", p=P))
                        for a, w in enumerate(["rwkv_w_a", "rwkv_a_a"]) for d in range(2)]
            if name == "gate_gla":
                return [((slice(None), 0, P), ins["rwkv_g_a"][l].rearrange("(c p) n -> p c n", p=P))] + [
                    ((slice(None), P + 16 * d, 16), ins["gla_gate_a"][l, d].rearrange("(c p) n -> p c n", p=P))
                    for d in range(2)]
            if name in ("q0", "q1"):
                h0 = 2 * int(name[1])
                return [((slice(None), P * jj + 64 * g, 64), w_in[:, :, 256 * g + 64 * (h0 + jj):256 * g + 64 * (h0 + jj) + 64])
                        for jj in range(2) for g in range(2)]
            t = PROJ.index(name) - len(SMALL)
            return [((slice(None), 0, TW), w_in[:, :, t * TW:(t + 1) * TW])]

        def slot8(s):
            return ring[:, s, :].rearrange("p (c n) -> p c n", c=KC)

        def slot2(s):
            return ring[:, s, :].rearrange("p (c n) -> p c n", c=2)

        fills = {}
        count = [0] * RING
        for l in range(L):
            for i, n in enumerate(MIX):
                count[i % RING] += 16 * MIX_DMAS.get(n, 1)
                fills[(l, n)] = (i % RING, count[i % RING])

        def tile_number(l, name):
            return MIX_TILES * l + MIX.index(name) + 1

        EVAC = {"decay_rate": "act", "gate_gla": "act", "q0": "dve", "q1": "dve", "kv": "dve", "br": "act",
                "bk": "dve", "bv": "act", "cqk": "dve", "cv": "act", "cog": "dve"}
        EVAC.update({g: "act" for g in GATES})
        evac_at, n = {}, {"act": 0, "dve": 0}
        for name in PROJ:
            n[EVAC[name]] += 1
            evac_at[name] = (EVAC[name], n[EVAC[name]])
        EV_ACT, EV_DVE = n["act"], n["dve"]

        def evacuated(eng, l, name):
            who, k = evac_at[name]
            eng.wait_ge(sem(f"ev_{who}"), (EV_ACT if who == "act" else EV_DVE) * l + k)

        def dense_loop(eng, unit):
            for par in range(2):
                unit(0, par, par, par, True)
            with eng.Fori(1, DENSE_UNITS // 2) as i:
                for par in range(2):
                    unit(0, i * 2 + par, i * 2 + par, par)
            unit(0, DENSE_UNITS - 1, DENSE_UNITS - 1, 0)

        def moe_loop(eng, unit):
            for par in range(2):
                unit(0, par, par, par, True)
            with eng.Fori(1, EXPERT_UNITS // 2) as i:
                for par in range(2):
                    unit(0, i * 2 + par, i * 2 + par, par)
            with eng.Fori(1, NE) as e:
                with eng.Fori(0, EXPERT_UNITS // 2) as i:
                    for par in range(2):
                        unit(e, i * 2 + par, e * EXPERT_UNITS + i * 2 + par, par)

        @block.sync
        def _(sp):
            for name, dst in [("cT", cT), ("cst", cst), ("xT", xT), ("bada", bada), ("lnp", lnp), ("rv", rv),
                              ("w0row", w0row), ("glbrow", glbrow), ("sinkB", sinkB), ("router", router)]:
                sp.dma_start(dst[:], ins[name]).then_inc(sem("params_in"), 16)

            def layer_params(l):
                if l > 0:
                    sp.wait_ge(sem("gla_out"), l)
                for name, dst in [("wbB", wbB), ("abB", abB), ("gbw", gbw), ("glb", glb), ("s0r", s0r),
                                  ("s0g", s0g), ("kcT", kcT), ("vc", vc)]:
                    sp.dma_start(dst[:], ins[name][:, l]).then_inc(sem("layer_in"), 16)

            layer_params(0)

            ada = ins["w_ada"].rearrange("l (c p) n -> p l c n", p=P)
            turns = ADA_TILES // RING

            def ada_tile(l, i, s):
                sp.dma_start(slot8(s), ada[:, l, :, bass.ds(i * (RING * TW) + s * TW, TW)])\
                    .then_inc(sem(f"ada_full{s}"), 16)

            for s in range(RING):
                ada_tile(0, 0, s)
            for l in range(L):
                with sp.Fori(1 - l, turns) as i:
                    for s in range(RING):
                        sp.wait_ge(sem("ada_used"), i * RING + (l * ADA_TILES + s + 1 - RING))
                        ada_tile(l, i, s)

            def mixer_tiles(l):
                for i, name in enumerate(MIX):
                    s = i % RING
                    if i >= RING:
                        sp.wait_ge(sem("tile_used"), l * MIX_TILES + i - RING + 1)
                    elif l == 0:
                        sp.wait_ge(sem("ada_used"), L * ADA_TILES - RING + s + 1)
                    else:
                        sp.wait_ge(sem("dense_gu_used" if s % 3 < 2 else "dense_d_used"),
                                   DENSE_UNITS if s < 3 else DENSE_UNITS - 1)
                    full = sem(f"mix_full{s}")
                    if name in PROJ:
                        for (_, c0, cn), src in w_tile(l, name):
                            sp.dma_start(slot8(s)[:, :, c0:c0 + cn], src).then_inc(full, 16)
                    elif name.startswith("up_a"):
                        j0 = 2 * int(name[-1])
                        wa = ins["w_up_a"][l].rearrange("(g j d) n -> g d j n", g=2, j=4)
                        for g in range(2):
                            sp.dma_start(slot2(s)[64 * g:64 * g + 64], wa[g, :, j0:j0 + 2, :]).then_inc(full, 16)
                    else:
                        if name in ("up_b", "up_c"):
                            w = ins["w_" + name][l]
                        else:
                            w = ins["w_out"][l][int(name[-1]) * 256:int(name[-1]) * 256 + 256, :]
                        sp.dma_start(slot2(s), w.rearrange("(c p) n -> p c n", p=P)).then_inc(full, 16)

            def unit_loads(kind, u, par, gate, up, down):
                for k, src in enumerate([gate, up, down]):
                    s = 3 * par + k
                    if u is None:
                        last = max(i for i in range(MIX_TILES) if i % RING == s)
                        sp.wait_ge(sem("tile_used"), (MIX_TILES if kind == "moe" else 0) + last + 1)
                    elif k != 1:
                        sp.wait_ge(sem(f"{kind}_{'gu' if k == 0 else 'd'}_used"), u - 1)
                    sp.dma_start(slot8(s) if k < 2 else slot2(s), src).then_inc(sem(f"{kind}_full{s}"), 16)

            mixer_tiles(0)
            dg = ins["ffn_w_gate"][0].rearrange("(c p) n -> p c n", p=P)
            du = ins["ffn_w_up"][0].rearrange("(c p) n -> p c n", p=P)
            dd = ins["ffn_w_down"][0].rearrange("(u c p) n -> p u c n", p=P, c=2)

            def dense_unit(e, r, u, par, first=False):
                cols = bass.ds(u * TW, TW)
                unit_loads("dense", None if first else u, par, dg[:, :, cols], du[:, :, cols],
                           dd[:, bass.ds(u, 1)].rearrange("p u c n -> p (u c) n"))

            dense_loop(sp, dense_unit)
            layer_params(1)
            mixer_tiles(1)
            mg = ins["moe_w_gate"][0].rearrange("e (c p) n -> p e c n", p=P)
            mu = ins["moe_w_up"][0].rearrange("e (c p) n -> p e c n", p=P)
            md = ins["moe_w_down"][0].rearrange("e (u c p) n -> p (e u) c n", p=P, c=2)

            def moe_unit(e, r, u, par, first=False):
                cols = bass.ds(r * TW, TW)
                unit_loads("moe", None if first else u, par,
                           mg[:, bass.ds(e, 1), :, cols].rearrange("p e c n -> p (e c) n"),
                           mu[:, bass.ds(e, 1), :, cols].rearrange("p e c n -> p (e c) n"),
                           md[:, bass.ds(u, 1)].rearrange("p u c n -> p (u c) n"))

            moe_loop(sp, moe_unit)
            sp.wait_ge(sem("y_ready"), 1)
            sp.dma_start(outs["yT"], xT[:]).then_inc(sem("stored"), 16)
            sp.wait_ge(sem("stored"), 16)

        @block.gpsimd
        def _(pool):
            for l in range(L):
                evacuated(pool, l, "kv")
                pool.dma_start(outs["kT"][l], kT[:, 0:P]).then_inc(sem("kept"), 16)
                pool.dma_start(outs["v"][l], av[:, 0, :]).then_inc(sem("kept"), 16)
                pool.wait_ge(sem("fstate_ready"), l + 1)
                for i in range(2):
                    dst = outs["rwkv"][0, l].rearrange("d (c i) v k -> i v d c k", i=2)[i]
                    for d in range(2):
                        pool.dma_start(dst[:, d], fstate[64 * i:64 * i + 64, d, :, 64 * i:64 * i + 64])\
                            .then_inc(sem("kept"), 16)
                pool.wait_ge(sem("gstate_ready"), l + 1)
                for h in range(4):
                    pool.dma_start(outs["gla"][0, l, :, h].rearrange("d k v -> k d v"),
                                   gstate[32 * h:32 * h + 32, :, 64 * h:64 * h + 64]).then_inc(sem("kept"), 16)
                pool.wait_ge(sem("kept"), 160 * (l + 1))

        @block.tensor
        def _(pe):
            mm = nc.tensor.matmul
            ident = C("ident")

            def acc(out, pairs, **kw):
                for n, (a, b) in enumerate(pairs):
                    last = mm(out, a, b, start=(n == 0), stop=(n == len(pairs) - 1), **kw)
                return last

            pe.wait_ge(sem("silu_c"), 1)
            for l in range(L):
                with pe.Fori(0, ADA_TILES // RING) as i:
                    for s in range(RING):
                        pe.wait_ge(sem(f"ada_full{s}"), i * 16 + 16 + l * 16 * (ADA_TILES // RING))
                        for h in range(2):
                            out = bank[l][:, bass.ds(i * (4 * RING) + (4 * s + 2 * h), 2)]
                            last = acc(out, [(slot8(s)[:, c, P * h:P * h + P], cS[:, c, :]) for c in range(KC)])
                        last.then_inc(sem("ada_used"), 1)

            def project(l, names):
                if names is FIRST:
                    pe.wait_ge(sem("h_ready"), 2 * l + 1)
                for name in names:
                    i = PROJ.index(name)
                    s, full = fills[(l, name)]
                    b = bk(i % 2, 2, TOK)
                    if i >= 2:
                        evacuated(pe, l, PROJ[i - 2])
                    pe.wait_ge(sem(f"mix_full{s}"), full)
                    w = slot8(s)
                    if name == "kv":
                        acc(b[:, 0, :], [(w[:, c, 0:P], hT[:, c, :]) for c in range(KC)])
                        for st in range(2):
                            last = acc(bank[i % 2][:, 256 + P * st:384 + P * st],
                                       [(hT[:, c, P * st:P * st + P], w[:, c, P:2 * P]) for c in range(KC)])
                    elif name == "cv":
                        for st in range(2):
                            last = acc(b[:, st, :], [(hT[:, c, P * st:P * st + P], w[:, c, :]) for c in range(KC)])
                    elif name == "gate_gla":
                        acc(b[:, 0, :], [(w[:, c, 0:P], hT[:, c, :]) for c in range(KC)])
                        last = acc(b[0:32, 1, :], [(w[:, c, P:P + 32], hT[:, c, :]) for c in range(KC)])
                    else:
                        for h in range(2):
                            last = acc(b[:, h, :], [(w[:, c, P * h:P * h + P], hT[:, c, :]) for c in range(KC)])
                    last.then_inc(sem("tile_used"), 1)

            def attention(l):
                evacuated(pe, l, "kv")
                pe.wait_ge(sem("layer_in"), 128 * (l + 1))
                mm(bank[2][:, :], C("rot"), qT[:, :, P:TOK], start=True, stop=True)
                mm(bank[3][:, 0:P], C("rot"), kT[:, P:TOK], start=True, stop=True).then_inc(sem("rot_done"), 1)
                pe.wait_ge(sem("attn_in"), l + 1)
                for j in range(4):
                    mm(bank[4 + j][:, :], qL[:, j, :], kxL[:, :, :], start=True, stop=True)
                for j in range(4):
                    last = mm(bk(2 + j // 2, 2, 256)[:, j % 2, :], qT[:, j, 0:P], kxP[:, :, :], start=True, stop=True)
                last.then_inc(sem("scores_done"), 1)
                pe.wait_ge(sem("probs_ready"), l + 1)
                for n in range(24):
                    src = pL[:, n // 2, P * (n % 2):P * (n % 2) + P] if n < 16 else pP[:, n - 16, :]
                    b = 4 + n // 4 if n < 16 else 2 + (n - 16) // 4
                    last = nc.tensor.transpose(bk(b, 4, P)[:, n % 4, :], src, ident)
                last.then_inc(sem("probsT_done"), 1)
                pe.wait_ge(sem("probsT_dve"), l + 1)
                pe.wait_ge(sem("probsT_act"), l + 1)
                for j in range(4):
                    out = bk(2 + j // 2, 2, TOK)
                    for g in range(2):
                        h = 2 * j + g
                        mm(out[64 * g:64 * g + 64, j % 2, 0:P], av[:, 0, 64 * g:64 * g + 64], pT[:, 16 + h, :],
                           start=True, stop=True)
                        mm(out[64 * g:64 * g + 64, j % 2, P:TOK], av[:, 1, 64 * g:64 * g + 64], pT[:, 2 * h, :],
                           start=True, stop=False)
                        last = mm(out[64 * g:64 * g + 64, j % 2, P:TOK], vc[:, 64 * g:64 * g + 64],
                                  pT[:, 2 * h + 1, :], start=False, stop=True)
                last.then_inc(sem("attn_done"), 1)

            def rwkv_inputs(l):
                pe.wait_ge(sem("attn_out"), l + 1)
                evacuated(pe, l, "gate_gla")
                evacuated(pe, l, "bv")
                for st in range(2):
                    mm(bank[2 + st][:, :], tanhT[:, P * st:P * st + P], wbB[:, :], start=True, stop=False)
                    mm(bank[2 + st][:, :], C("ones")[0:1, :], w0row[:, l, :], start=False, stop=True)
                for d in range(2):
                    for c in range(2):
                        mm(bk(4 + d, 2, TOK)[:, c, :], abB[:, 256 * d + P * c:256 * d + P * c + P], aaT[:, :],
                           start=True, stop=True)
                for c in range(2):
                    last = mm(bk(6, 2, TOK)[:, c, :], gbw[:, P * c:P * c + P], sgaT[:, :], start=True, stop=True)
                last.then_inc(sem("rw_logits"), 1)
                pe.wait_ge(sem("kk_sq"), l + 1)
                mm(bank[7][:, :], C("blk"), rtmp, start=True, stop=True).then_inc(sem("kk_norm"), 1)
                pe.wait_ge(sem("rw_act"), l + 1)
                for st in range(2):
                    for c in range(2):
                        last = nc.tensor.transpose(bk(2, 2, 2, P)[:, st, c, :], vT[:, c, P * st:P * st + P], ident)
                last.then_inc(sem("vn_done"), 1)
                pe.wait_ge(sem("bonus_in"), l + 1)
                mm(bank[3][:, :], C("blk"), rtmp2, start=True, stop=True).then_inc(sem("bonus_sum"), 1)
                pe.wait_ge(sem("bonus_out"), l + 1)

            def rwkv_stream(l, st):
                k = 2 * l + st + 1
                for d in range(2):
                    for c in range(2):
                        last = mm(bk(2 + d, 2, 256)[:, c, :], sigz[:, st, 256 * d + P * c:256 * d + P * c + P],
                                  C(f"tri{d}"), start=True, stop=True)
                if st == 1:
                    for d in range(2):
                        for c in range(2):
                            last = mm(bank[4][:, 2 * d + c:2 * d + c + 1],
                                      sigz[:, st, 256 * d + P * c:256 * d + P * c + P], C(f"cen{d}"),
                                      start=True, stop=True)
                last.then_inc(sem("cum_done"), 1)
                pe.wait_ge(sem("decays_ready"), 2 * k)
                for d in range(2):
                    pe.wait_ge(sem("khat_ready"), 2 * (k - 1) + d + 1)
                    if d == 1:
                        pe.wait_ge(sem("mats_read"), 2 * (k - 1) + 1)
                    for c in range(2):
                        mm(bank[2 + c][:, :], Bc[d][:, c, :], KR[d][:, c, :, :, :], start=True, stop=True)
                        mm(bank[4 + c][:, :], KcR[d][:, c, :], KR[d][:, c, :, :, :], start=True, stop=True)
                    for c in range(2):
                        for i in range(2):
                            last = mm(bk(6, 4, P)[:, 2 * c + i, :], KR[d][:, c, 0, i, :], Bc[d][:, c, :],
                                      start=True, stop=True)
                    last.then_inc(sem("mats_done"), 1)
                for j in range(1, LEVELS + 1):
                    n = (k - 1) * LEVELS + j
                    for d in range(2):
                        if j == 1:
                            pe.wait_ge(sem("mats_read"), 2 * k)
                        else:
                            pe.wait_ge(sem(f"inv_T{d}"), n - 1)
                        for h in range(4):
                            last = mm(bk(2 + 3 * d, 4, P)[:, h, :], MTQ[d][:, h // 2, 0, h % 2, :], Tm[d][:, h, :],
                                      start=True, stop=True)
                        last.then_inc(sem(f"inv_MT{d}"), 1)
                    for d in range(2):
                        pe.wait_ge(sem(f"inv_P{d}"), n)
                        for h in range(4):
                            mm(bk(3 + 3 * d, 4, P)[:, h, :], TmT[d][:, h, :], P1[d][:, h, :], start=True, stop=True)
                        for h in range(4):
                            last = mm(bk(4 + 3 * d, 4, P)[:, h, :], P1[d][:, h, :],
                                      TmT[d][:, h, :], start=True, stop=True)
                        last.then_inc(sem(f"inv_TP{d}"), 1)
                for d in range(2):
                    pe.wait_ge(sem(f"inv_T{d}"), k * LEVELS)
                    for h in range(4):
                        c, i = h // 2, h % 2
                        out = bank[2 + d][:, 64 * h:64 * h + 64]
                        pairs = [(AKQ[d][:, c, 0, i, :], Vn[:, st, 64 * h:64 * h + 64])]
                        if st == 1:
                            pairs.append((KR[d][:, c, 0, i, :], s0c[:, 2 * d + c, :]))
                        last = acc(out, pairs)
                    last.then_inc(sem("x_done"), 1)
                for d in range(2):
                    pe.wait_ge(sem("xs_ready"), 2 * (k - 1) + d + 1)
                    for h in range(4):
                        last = mm(bank[4 + d][:, 64 * h:64 * h + 64], TmT[d][:, h, :], Xs[d][:, 64 * h:64 * h + 64],
                                  start=True, stop=True)
                    last.then_inc(sem("u_done"), 1)
                pe.wait_ge(sem("nu_ready"), 2 * k)
                for c in range(2):
                    for i in range(2):
                        h = 2 * c + i
                        pairs = []
                        for d in range(2):
                            pairs.append((Vn[:, st, 64 * h:64 * h + 64], AKQ[d][:, c, 1, i, :]))
                            pairs.append((nU[d][:, 64 * h:64 * h + 64], MTQ[d][:, c, 1, i, :]))
                            if st == 1:
                                pairs.append((s0c[:, 2 * d + c, :], KR[d][:, c, 1, i, :]))
                        last = acc(bk(6, 2, P)[64 * i:64 * i + 64, c, :], pairs)
                last.then_inc(sem("y_done"), 1)
                if st == 0:
                    pe.wait_ge(sem("k2_ready"), l + 1)
                    for x in range(2):
                        for e in range(4):
                            last = nc.tensor.transpose(bk(2 + x, 4, P)[:, e, :], K2T[:, x, e, :], ident)
                    last.then_inc(sem("k2T_done"), 1)
                    pe.wait_ge(sem("k2n_ready"), l + 1)
                    for d in range(2):
                        for c in range(2):
                            last = acc(bk(7, 4, P)[:, 2 * d + c, :],
                                       [(Vn[:, 0, P * c:P * c + P], K2n[0][:, 2 * d + c, :]),
                                        (nU[d][:, P * c:P * c + P], K2n[1][:, 2 * d + c, :])])
                    last.then_inc(sem("fs_done"), 1)
                    pe.wait_ge(sem("fstate_ready"), l + 1)
                pe.wait_ge(sem("yT_ready"), k)

            def rwkv_norm(l):
                mm(bank[2][:, :], C("blkm"), yT[:, :, :], start=True, stop=True).then_inc(sem("gn_mean"), 1)
                pe.wait_ge(sem("gn_sq"), l + 1)
                mm(bank[3][:, :], C("blkm"), rtmp, start=True, stop=True).then_inc(sem("gn_var"), 1)

            def gla(l):
                pe.wait_ge(sem("rwkv_out"), l + 1)
                evacuated(pe, l, "cog")
                for st in range(2):
                    mm(bk(2, 2, 256)[:, st, :], glaT[:, P * st:P * st + P], glb[:, :], start=True, stop=False)
                    last = mm(bk(2, 2, 256)[:, st, :], C("ones")[0:1, :], glbrow[:, l, :], start=False, stop=True)
                last.then_inc(sem("gl_done"), 1)
                pe.wait_ge(sem("glog_ready"), l + 1)
                lgv = glog.rearrange("p (s d c) -> p s d c", s=2, d=2)
                for st in range(2):
                    for d in range(2):
                        mm(bk(3, 4, P)[:, 2 * st + d, :], lgv[:, st, d, :], C(f"trig{d}"), start=True, stop=True)
                for d in range(2):
                    last = mm(bank[4][:, d:d + 1], lgv[:, 1, d, :], C(f"ceng{d}"), start=True, stop=True)
                last.then_inc(sem("gcum_done"), 1)
                pe.wait_ge(sem("gq_ready"), l + 1)
                for x in range(4):
                    last = mm(bank[4 + x][:, :], KcG[:, x, :], Qx[:, x, :, :], start=True, stop=True)
                last.then_inc(sem("att_done"), 1)
                pe.wait_ge(sem("att_ready"), l + 1)
                for st in range(2):
                    for h in range(4):
                        c, i = h // 2, h % 2
                        pairs = []
                        for d in range(2):
                            pairs.append((cv[:, st, 64 * h:64 * h + 64], attT[:, 2 * st + d, h, :]))
                            if st == 1:
                                pairs.append((s0gc[:, d, :], Qx[:, 2 * st + d, h, :]))
                        last = acc(bk(2, 2, TOK)[64 * i:64 * i + 64, c, P * st:P * st + P], pairs)
                last.then_inc(sem("go_done"), 1)
                for d in range(2):
                    last = nc.tensor.transpose(bk(3, 4, P)[:, d, :], K2g[:, d, :], ident)
                last.then_inc(sem("k2g_done"), 1)
                pe.wait_ge(sem("k2g_ready"), l + 1)
                for d in range(2):
                    last = mm(bk(4, 2, 256)[:, d, :], K2gn[:, d, :], cv[:, 0, :], start=True, stop=True)
                last.then_inc(sem("gs_done"), 1)
                pe.wait_ge(sem("gsq_ready"), l + 1)
                mm(bank[5][:, :], C("blkm"), gsq, start=True, stop=True).then_inc(sem("gms_done"), 1)

            def rows_outer(l, tiles, src, first_bank):
                n = 0
                for name in tiles:
                    s, full = fills[(l, name)]
                    pe.wait_ge(sem(f"mix_full{s}"), full)
                    for c in range(2):
                        for m in range(KC):
                            last = mm(bk(first_bank + m // 2, 2, TOK)[:, m % 2, :], slot2(s)[:, c, P * m:P * m + P],
                                      src[:, n, :], start=(n == 0 and m % 2 == 0),
                                      stop=(n == 2 * len(tiles) - 1), skip_group_check=True)
                        n += 1
                    last.then_inc(sem("tile_used"), 1)

            def merge(l):
                evacuated(pe, l, "gate11")
                evacuated(pe, l, "gate10")
                pe.wait_ge(sem("gla_out"), l + 1)
                rows_outer(l, ["up_a0", "up_a1"], oaT, 0)
                rows_outer(l, ["up_b"], obT, 4)
                pe.wait_ge(sem("up_read"), 3 * l + 1)
                rows_outer(l, ["up_c"], ocT, 0)
                pe.wait_ge(sem("up_read"), 3 * l + 3)
                rows_outer(l, [f"out{i}" for i in range(4)], merged, 4)

            def layer_norm(n):
                pe.wait_ge(sem("ln_y"), n + 1)
                acc(bank[0][:, 0:TOK], [(C("mean_d"), yLN[:, m, :]) for m in range(KC)]).then_inc(sem("ln_mean"), 1)
                pe.wait_ge(sem("ln_sq"), n + 1)
                acc(bank[1][:, 0:TOK], [(C("mean_d"), mtmp[:, m, :]) for m in range(KC)]).then_inc(sem("ln_var"), 1)

            def gate_up(kind, par, k):
                pe.wait_ge(sem(f"{kind}_full{3 * par}"), k * 16)
                for h in range(2):
                    acc(bk(2 * par, 2, TOK)[:, h, :], [(slot8(3 * par)[:, c, P * h:P * h + P], hT[:, c, :])
                                                       for c in range(KC)])
                pe.wait_ge(sem(f"{kind}_full{3 * par + 1}"), k * 16)
                for h in range(2):
                    last = acc(bk(2 * par + 1, 2, TOK)[:, h, :], [(slot8(3 * par + 1)[:, c, P * h:P * h + P], hT[:, c, :])
                                                                  for c in range(KC)])
                last.then_inc(sem(f"{kind}_gu_used"), 1)

            def down(kind, par, k, hid_count):
                pe.wait_ge(sem(f"{kind}_full{3 * par + 2}"), k * 16)
                pe.wait_ge(sem(f"{kind}_hid"), hid_count)
                for c in range(2):
                    for m in range(KC):
                        last = mm(bk(4 + m // 2, 2, TOK)[:, m % 2, :], slot2(3 * par + 2)[:, c, P * m:P * m + P],
                                  hid[par][:, c, :], start=False, stop=False, skip_group_check=True)
                last.then_inc(sem(f"{kind}_d_used"), 1)

            def channel_mixer(l):
                pe.wait_ge(sem("h_ready"), 2 * l + 2)
                kind, units = ("dense", DENSE_UNITS) if l == 0 else ("moe", MOE_UNITS)
                if l == 1:
                    for st in range(2):
                        last = acc(bank[st][:, 0:NE], [(hT[:, c, P * st:P * st + P], router[:, c, :])
                                                       for c in range(KC)])
                    last.then_inc(sem("logits_done"), 1)
                    pe.wait_ge(sem("diag_ready"), 1)
                    for st in range(2):
                        for q in range(2):
                            last = mm(bank[4 + 2 * st + q][:, :], C("ones"), diag[:, st, 4 * q:4 * q + 4, :],
                                      start=True, stop=True)
                    last.then_inc(sem("gates_done"), 1)
                    pe.wait_ge(sem("gateB_ready"), 1)
                for b in range(4):
                    mm(bank[4 + b][:, :], zeros[:, 0:P], zeros[:, :], start=True, stop=False,
                       skip_group_check=True)
                gate_up(kind, 0, 1)

                def turn(i):
                    for par in (1, 0):
                        if par == 0 or not isinstance(i, int):
                            pe.wait_ge(sem(f"{kind}_hid"), i * 2 + (0 if par else 1))
                        gate_up(kind, par, i + (1 if par else 2))
                        down(kind, 1 - par, i + 1, i * 2 + (1 if par else 2))

                turn(0)
                with pe.Fori(1, (units - 1) // 2) as i:
                    turn(i)
                if units % 2 == 0:
                    pe.wait_ge(sem(f"{kind}_hid"), units - 2)
                    gate_up(kind, 1, units // 2)
                    down(kind, 0, units // 2, units - 1)
                    down(kind, 1, units // 2, units)
                else:
                    down(kind, 0, (units + 1) // 2, units)
            for l in range(L):
                project(l, FIRST)
                attention(l)
                rwkv_inputs(l)
                for st in range(2):
                    rwkv_stream(l, st)
                rwkv_norm(l)
                gla(l)
                project(l, GATES)
                merge(l)
                layer_norm(2 * l)
                channel_mixer(l)
                layer_norm(2 * l + 1)

        @block.scalar
        def _(act):
            af = nc.scalar.activation
            steps = [0]

            def chained(ins):
                steps[0] += 1
                ins.then_inc(sem("act_chain"), 1)
                act.wait_ge(sem("act_chain"), steps[0])

            act.wait_ge(sem("params_in"), 10 * 16)
            af(cS[:], cT[:], ACT.Sigmoid).then_inc(sem("sig_c"), 1)
            roots = [0]

            def square_root(buf):
                roots[0] += 1
                act.wait_ge(sem("root_in"), roots[0])
                af(buf, buf, ACT.Sqrt).then_inc(sem("root_out"), 1)

            def project(l, names):
                for name in names:
                    if EVAC[name] != "act" and name != "cog":
                        continue
                    act.wait_ge(sem("tile_used"), tile_number(l, name))
                    b = bk(PROJ.index(name) % 2, 2, TOK)
                    done = sem("ev_act")
                    if name == "decay_rate":
                        af(tanhT[:], b[:, 0, :], ACT.Tanh)
                        af(aaT[:], b[:, 1, :], ACT.Copy).then_inc(done, 1)
                    elif name == "gate_gla":
                        af(sgaT[:], b[:, 0, :], ACT.Sigmoid)
                        af(glaT[:], b[0:32, 1, :], ACT.Copy).then_inc(done, 1)
                    elif name == "cog":
                        af(ogs[:], b, ACT.Sigmoid).then_inc(sem("sig_og"), 1)
                    elif name in GATES:
                        i = GATES.index(name)
                        af(sg[:, 2 * i:2 * i + 2, :], b, ACT.Sigmoid).then_inc(done, 1)
                    else:
                        dst = {"br": rT, "bv": vT, "cv": cv}[name]
                        af(dst[:], b, ACT.Copy).then_inc(done, 1)

            def attention(l):
                act.wait_ge(sem("max_ready"), l + 1)
                for h in range(8):
                    j, g = h // 2, h % 2
                    af(pP[:, h, :], bk(2 + j // 2, 4, P)[:, 2 * (j % 2) + g, :], ACT.Exp, bias=mneg[:, h:h + 1],
                       scale=0.125, accum_out=den[:, h:h + 1])
                    af(pL[:, h, :], bk(4 + j, 2, 256)[:, g, :], ACT.Exp, bias=mneg[:, 8 + h:9 + h],
                       scale=0.125, accum_out=den[:, 8 + h:9 + h])
                af(esink, esink, ACT.Exp).then_inc(sem("probs_exp"), 1)
                act.wait_ge(sem("probsT_done"), l + 1)
                for b, n in [(7, 12), (2, 16), (3, 20)]:
                    last = af(pT[:, n:n + 4, :], bk(b, 4, P), ACT.Copy)
                last.then_inc(sem("probsT_act"), 1)

            def rwkv(l):
                act.wait_ge(sem("rw_logits"), l + 1)
                for st in range(2):
                    af(sigz[:, st, :], bank[2 + st][:, :], ACT.Sigmoid)
                for d in range(2):
                    for c in range(2):
                        af(aT[:, d, c, :], bk(4 + d, 2, TOK)[:, c, :], ACT.Sigmoid,
                           bias=rv[:, l, 2 * d + c:2 * d + c + 1])
                af(gT, bk(6, 2, TOK), ACT.Copy).then_inc(sem("rw_act"), 1)
                square_root(rtmp2)
                for st in range(2):
                    k = 2 * l + st + 1
                    act.wait_ge(sem("cum_done"), k)
                    if st == 1:
                        af(ecr, bank[4][:, 0:4], ACT.Exp).then_inc(sem("center_ready"), 1)
                    for d in range(2):
                        b = bk(2 + d, 2, 2, P)
                        af(Ep[d], b, ACT.Exp)
                        af(En[d], b[:, :, 0, :], ACT.Exp, scale=-1.0).then_inc(sem("decays_ready"), 1)
                    for d in range(2):
                        act.wait_ge(sem("x_done"), 2 * (k - 1) + d + 1)
                        af(Xs[d], bank[2 + d][:, 0:256], ACT.Copy).then_inc(sem("xs_ready"), 1)
                    for d in range(2):
                        act.wait_ge(sem("u_done"), 2 * (k - 1) + d + 1)
                        af(nU[d], bank[4 + d][:, 0:256], ACT.Copy, scale=-1.0).then_inc(sem("nu_ready"), 1)
                    act.wait_ge(sem("y_done"), k)
                    af(yT[:, :, P * st:P * st + P], bk(6, 2, P), ACT.Copy).then_inc(sem("yT_ready"), 1)
                square_root(rtmp2)

            def gla(l):
                act.wait_ge(sem("gabs_ready"), l + 1)
                chained(af(glog, glog, ACT.Exp))
                af(glog, glog, ACT.Ln, bias=1.0).then_inc(sem("gln_ready"), 1)
                act.wait_ge(sem("gcum_done"), l + 1)
                af(ecg, bank[4][:, 0:2], ACT.Exp)
                af(EG, bk(3, 4, P), ACT.Exp)
                af(EGn, bk(3, 4, P), ACT.Exp, scale=-1.0).then_inc(sem("gdecay_ready"), 1)

            def unit_sigmoid(kind):
                def unit(e, r, u, par, first=False):
                    act.wait_ge(sem(f"{kind}_gu_used"), u + 1)
                    if not first:
                        act.wait_ge(sem(f"{kind}_hid"), u - 1)
                    af(sgt[par], bk(2 * par, 2, TOK), ACT.Sigmoid).then_inc(sem(f"{kind}_sig"), 1)
                return unit

            for l in range(L):
                project(l, FIRST)
                attention(l)
                rwkv(l)
                gla(l)
                square_root(gtm)
                project(l, GATES)
                square_root(rstd)
                if l == 0:
                    dense_loop(act, unit_sigmoid("dense"))
                else:
                    act.wait_ge(sem("gap_ready"), 1)
                    af(small[:, 0:2], small[:, 0:2], ACT.Exp).then_inc(sem("gap_exp"), 1)
                    moe_loop(act, unit_sigmoid("moe"))
                square_root(rstd)

        @block.vector
        def _(dve):
            v = nc.vector
            steps = [0]

            def chained(ins):
                steps[0] += 1
                ins.then_inc(sem("dve_chain"), 1)
                dve.wait_ge(sem("dve_chain"), steps[0])

            mul = lambda o, a, b: v.tensor_tensor(o, a, b, ALU.mult)
            add = lambda o, a, b: v.tensor_tensor(o, a, b, ALU.add)
            sub = lambda o, a, b: v.tensor_tensor(o, a, b, ALU.subtract)

            def scaled(o, a, s1, s2=None):
                return v.tensor_scalar(o, a, s1, s2, ALU.mult, ALU.add) if s2 is not None else \
                    v.tensor_scalar(o, a, s1, None, ALU.mult)

            def over(a, n, axis=1):
                x = a.unsqueeze(axis)
                shape = list(x.shape)
                shape[axis] = n
                return x.to_broadcast(shape)

            roots = [0]

            def inverse_root(buf, source, eps):
                roots[0] += 1
                v.tensor_scalar(buf, source, eps, None, ALU.add).then_inc(sem("root_in"), 1)
                dve.wait_ge(sem("root_out"), roots[0])
                chained(v.reciprocal(buf, buf))

            dve.wait_ge(sem("params_in"), 10 * 16)
            v.memset(zeros[:], 0.0)
            for l in range(L):
                v.tensor_scalar(omk[:, l, :], rv[:, l, 6:8], -1.0, 1.0, ALU.mult, ALU.add)
            dve.wait_ge(sem("sig_c"), 1)
            mul(cS[:], cS[:], cT[:]).then_inc(sem("silu_c"), 1)
            for l in range(L):
                dve.wait_ge(sem("ada_used"), ADA_TILES * (l + 1))
                chained(add(mod[:, l], bk(l, 48, 2), over(bada[:, l, :], 2, 2)))
                for a in (8, 32):
                    last = v.tensor_scalar(mod[:, l, a:a + 8, :], mod[:, l, a:a + 8, :], 1.0, None, ALU.add)
                chained(last)

            def modulate(l, sub_layer):
                for m in range(KC):
                    for st in range(2):
                        sh, sc = mod[:, l, 24 * sub_layer + m, st:st + 1], mod[:, l, 24 * sub_layer + 8 + m, st:st + 1]
                        last = scaled(hT[:, m, P * st:P * st + P], xT[:, m, P * st:P * st + P], sc, sh)
                last.then_inc(sem("h_ready"), 1)

            def project(l):
                for name in FIRST:
                    if EVAC[name] != "dve":
                        continue
                    dve.wait_ge(sem("tile_used"), tile_number(l, name))
                    i = PROJ.index(name) % 2
                    b = bk(i, 2, TOK)
                    if name in ("q0", "q1"):
                        j = 2 * int(name[1])
                        last = v.tensor_copy(qT[:, j:j + 2, :], b)
                    elif name == "kv":
                        if l > 0:
                            dve.wait_ge(sem("kept"), 160 * l)
                        v.tensor_copy(kT[:], b[:, 0, :])
                        last = v.tensor_copy(av[:], bk(i, 4, P)[:, 2:4, :])
                    elif name == "bk":
                        last = v.tensor_copy(kfT[:], b)
                    elif name == "cqk":
                        v.tensor_copy(cqT[:], b[:, 0, :])
                        last = v.tensor_copy(ckT[:], b[:, 1, :])
                    else:
                        dve.wait_ge(sem("sig_og"), l + 1)
                        last = mul(ogs[:], ogs[:], b)
                    last.then_inc(sem("ev_dve"), 1)
                dve.wait_ge(sem("ev_dve"), EV_DVE * (l + 1))

            def attention(l):
                dve.wait_ge(sem("rot_done"), l + 1)
                dve.wait_ge(sem("layer_in"), 128 * (l + 1))
                mul(atmp, bk(2, 4, P), over(C("sin"), 4))
                mul(qL, qT[:, :, P:TOK], over(C("cos"), 4))
                mul(krot, bank[3][:, 0:P], C("sin"))
                chained(mul(rtmp_k, kT[:, P:TOK], C("cos")))
                add(qL, qL, atmp)
                chained(add(krot, krot, rtmp_k))
                hm = C("hm64")
                for g in range(2):
                    scaled(kxL[:, g, 0:P], krot, hm[:, g:g + 1])
                    scaled(kxL[:, g, P:256], kcT[:, :], hm[:, g:g + 1])
                    last = scaled(kxP[:, g, :], kT[:, 0:P], hm[:, g:g + 1])
                last.then_inc(sem("attn_in"), 1)
                dve.wait_ge(sem("scores_done"), l + 1)
                for j in range(4):
                    v.tensor_reduce(mneg[:, 8 + 2 * j:10 + 2 * j], bk(4 + j, 2, 256), AX.X, ALU.max)
                for b in range(2):
                    last = v.tensor_reduce(mneg[:, 4 * b:4 * b + 4], bk(2 + b, 4, P), AX.X, ALU.max)
                chained(last)
                for st in range(2):
                    last = v.scalar_tensor_tensor(mneg[:, 8 * st:8 * st + 8], mneg[:, 8 * st:8 * st + 8], 0.125,
                                                  sinkB[:, l, :], ALU.mult, ALU.max)
                chained(last)
                for st in range(2):
                    last = sub(esink[:, 8 * st:8 * st + 8], sinkB[:, l, :], mneg[:, 8 * st:8 * st + 8])
                chained(last)
                scaled(mneg, mneg, -1.0).then_inc(sem("max_ready"), 1)
                dve.wait_ge(sem("probs_exp"), l + 1)
                chained(add(den, den, esink))
                chained(v.reciprocal(den, den))
                mul(pP, pP, over(den[:, 0:8], P, 2))
                mul(pL, pL, over(den[:, 8:16], 256, 2)).then_inc(sem("probs_ready"), 1)
                dve.wait_ge(sem("probsT_done"), l + 1)
                for b in range(3):
                    last = v.tensor_copy(pT[:, 4 * b:4 * b + 4, :], bk(4 + b, 4, P))
                last.then_inc(sem("probsT_dve"), 1)
                dve.wait_ge(sem("attn_done"), l + 1)
                v.tensor_copy(oaT[:, 0:2, :], bk(2, 2, TOK))
                v.tensor_copy(oaT[:, 2:4, :], bk(3, 2, TOK)).then_inc(sem("attn_out"), 1)

            def rwkv_inputs(l):
                evacuated(dve, l, "bv")
                par = lambda i: rv[:, l, i:i + 1]
                for c in range(2):
                    last = scaled(kapT[:, c, :], kfT[:, c, :], par(4 + c))
                chained(last)
                mul(rtmp, kapT, kapT).then_inc(sem("kk_sq"), 1)
                dve.wait_ge(sem("kk_norm"), l + 1)
                inverse_root(rtmp2, bk(7, 2, TOK), 1e-12)
                chained(mul(kapT, kapT, rtmp2))
                dve.wait_ge(sem("rw_act"), l + 1)
                for d in range(2):
                    mul(akT[:, d], aT[:, d], kapT)
                    for c in range(2):
                        last = scaled(ktT[:, d, c, :], aT[:, d, c, :], par(6 + c), omk[:, l, c:c + 1])
                chained(last)
                for d in range(2):
                    last = mul(ktT[:, d], ktT[:, d], kfT[:])
                chained(last)
                chained(add(rtmp2, ktT[:, 0], ktT[:, 1]))
                chained(mul(rtmp2, rtmp2, rT[:]))
                for c in range(2):
                    last = scaled(rtmp2[:, c, :], rtmp2[:, c, :], par(8 + c))
                last.then_inc(sem("bonus_in"), 1)
                dve.wait_ge(sem("vn_done"), l + 1)
                v.tensor_copy(Vn, bk(2, 2, TOK))
                dve.wait_ge(sem("bonus_sum"), l + 1)
                mul(bonT, bk(3, 2, TOK), vT[:]).then_inc(sem("bonus_out"), 1)

            def rwkv_stream(l, st):
                k = 2 * l + st + 1
                cols = slice(P * st, P * st + P)
                hm = C("hm64")
                if st == 1:
                    dve.wait_ge(sem("center_ready"), l + 1)
                    for e in range(4):
                        scaled(s0c[:, e, :], s0r[:, e, :], ecr[:, e:e + 1])
                for d in range(2):
                    dve.wait_ge(sem("decays_ready"), 2 * (k - 1) + d + 1)
                    for i in range(2):
                        v.scalar_tensor_tensor(KR[d][:, :, 0, i, :], kapT[:, :, cols], hm[:, i:i + 1],
                                               Ep[d][:, :, 1, :], ALU.mult, ALU.mult)
                        v.scalar_tensor_tensor(KR[d][:, :, 1, i, :], rT[:, :, cols], hm[:, i:i + 1],
                                               Ep[d][:, :, 0, :], ALU.mult, ALU.mult)
                    mul(Bc[d], akT[:, d, :, cols], En[d])
                    end = P - 1 if d == 0 else 0
                    v.tensor_copy(elast[:, 2 * d:2 * d + 2], Ep[d][:, :, 0, end])
                    mul(KcR[d], ktT[:, d, :, cols], En[d]).then_inc(sem("khat_ready"), 1)
                for d in range(2):
                    dve.wait_ge(sem("mats_done"), 2 * (k - 1) + d + 1)
                    mask = C(f"mask{d}").rearrange("p (x i t) -> p x i t", x=2, i=2)
                    for c in range(2):
                        mul(MTQ[d][:, c], bk(2 + c, 2, 2, P), mask)
                    mul(Tm[d], bk(6, 4, P), over(C(f"lv0{d}"), 4))
                    for c in range(2):
                        last = mul(AKQ[d][:, c], bk(4 + c, 2, 2, P), mask)
                    chained(last)
                    for c in range(2):
                        mul(TmT[d][:, 2 * c:2 * c + 2, :], MTQ[d][:, c, 0], over(C(f"lv0T{d}"), 2))
                    chained(add(Tm[d], Tm[d], over(C("ident"), 4)))
                    add(TmT[d], TmT[d], over(C("ident"), 4)).then_inc(sem("mats_read"), 1)
                for j in range(1, LEVELS + 1):
                    n = (k - 1) * LEVELS + j
                    for d in range(2):
                        dve.wait_ge(sem(f"inv_MT{d}"), n)
                        mul(P1[d], bk(2 + 3 * d, 4, P), over(C(f"lv{j}"), 4)).then_inc(sem(f"inv_P{d}"), 1)
                    for d in range(2):
                        dve.wait_ge(sem(f"inv_TP{d}"), n)
                        sub(Tm[d], Tm[d], bk(3 + 3 * d, 4, P))
                        sub(TmT[d], TmT[d], bk(4 + 3 * d, 4, P)).then_inc(sem(f"inv_T{d}"), 1)
                if st == 0:
                    dve.wait_ge(sem("x_done"), 2 * k)
                    for d in range(2):
                        for c in range(2):
                            e = 2 * d + c
                            scaled(K2T[:, 0, e, :], KcR[d][:, c, :], elast[:, e:e + 1])
                            last = scaled(K2T[:, 1, e, :], Bc[d][:, c, :], elast[:, e:e + 1])
                    last.then_inc(sem("k2_ready"), 1)
                    dve.wait_ge(sem("k2T_done"), l + 1)
                    v.tensor_copy(K2n[0], bk(2, 4, P))
                    v.tensor_copy(K2n[1], bk(3, 4, P)).then_inc(sem("k2n_ready"), 1)
                    dve.wait_ge(sem("fs_done"), l + 1)
                    v.tensor_copy(fstate[:], bk(7, 2, 2, P)).then_inc(sem("fstate_ready"), 1)

            def rwkv_norm(l):
                dve.wait_ge(sem("gn_mean"), l + 1)
                chained(sub(yT, yT, bk(2, 2, TOK)))
                mul(rtmp, yT, yT).then_inc(sem("gn_sq"), 1)
                dve.wait_ge(sem("gn_var"), l + 1)
                inverse_root(rtmp2, bk(3, 2, TOK), GN_EPS)
                chained(mul(yT, yT, rtmp2))
                for c in range(2):
                    last = scaled(yT[:, c, :], yT[:, c, :], rv[:, l, 10 + c:11 + c], rv[:, l, 12 + c:13 + c])
                chained(last)
                chained(add(yT, yT, bonT))
                mul(obT[:], yT, gT).then_inc(sem("rwkv_out"), 1)

            def gla(l):
                dve.wait_ge(sem("gl_done"), l + 1)
                v.tensor_scalar(gtm, bank[2][:, :], 0.0, None, ALU.min)
                chained(v.tensor_scalar(glog, bank[2][:, :], 0.0, None, ALU.max))
                sub(glog, gtm, glog).then_inc(sem("gabs_ready"), 1)
                dve.wait_ge(sem("gln_ready"), l + 1)
                sub(glog, gtm, glog).then_inc(sem("glog_ready"), 1)
                dve.wait_ge(sem("gdecay_ready"), l + 1)
                for st in range(2):
                    for d in range(2):
                        x = 2 * st + d
                        cols = slice(P * st, P * st + P)
                        mul(KcG[:, x, :], ckT[:, cols], EGn[:, x, :])
                        chained(v.scalar_tensor_tensor(Qh, cqT[:, cols], 32.0 ** -0.5, EG[:, x, :],
                                                       ALU.mult, ALU.mult))
                        for h in range(4):
                            last = scaled(Qx[:, x, h, :], Qh, C("hm32")[:, h:h + 1])
                        chained(last)
                for d in range(2):
                    end = P - 1 if d == 0 else 0
                    scaled(s0gc[:, d, :], s0g[:, d, :], ecg[:, d:d + 1])
                    last = scaled(K2g[:, d, :], KcG[:, d, :], EG[:, d, end:end + 1])
                last.then_inc(sem("gq_ready"), 1)
                dve.wait_ge(sem("att_done"), l + 1)
                for x in range(4):
                    last = mul(attT[:, x], bk(4 + x, 4, P), over(C(f"mask{x % 2}")[:, 256:384], 4))
                last.then_inc(sem("att_ready"), 1)
                dve.wait_ge(sem("go_done"), l + 1)
                chained(v.tensor_copy(oc, bank[2][:, :]))
                mul(gsq, oc, oc).then_inc(sem("gsq_ready"), 1)
                dve.wait_ge(sem("k2g_done"), l + 1)
                v.tensor_copy(K2gn, bk(3, 2, P)).then_inc(sem("k2g_ready"), 1)
                dve.wait_ge(sem("gs_done"), l + 1)
                v.tensor_copy(gstate[:], bk(4, 2, 256)).then_inc(sem("gstate_ready"), 1)
                dve.wait_ge(sem("gms_done"), l + 1)
                inverse_root(gtm, bank[5][:, :], LN_EPS)
                chained(mul(oc, oc, gtm))
                v.scalar_tensor_tensor(ocT[:], shaped(oc, (2, TOK)), rv[:, l, 14:15], ogs[:], ALU.mult, ALU.mult)\
                    .then_inc(sem("gla_out"), 1)

            def merge(l):
                evacuated(dve, l, "gate11")
                for br, tile in enumerate(["up_a1", "up_b", "up_c"]):
                    dve.wait_ge(sem("tile_used"), tile_number(l, tile))
                    if br > 0:
                        dve.wait_ge(sem("up_read"), 3 * l + br)
                    for b in range(4):
                        ps = bk((4 if br == 1 else 0) + b, 2, TOK)
                        gate = sg[:, 8 * br + 2 * b:8 * br + 2 * b + 2, :]
                        last = mul((merged if br == 0 else mtmp)[:, 2 * b:2 * b + 2, :], ps, gate)
                    if br > 0:
                        chained(last)
                        last = add(merged, merged, mtmp)
                    last.then_inc(sem("up_read"), 1)
                chained(v.tensor_scalar(xT[:], xT[:], ALPHA, None, ALU.mult))

            def layer_norm(n, tile_sem, tile_count, last_norm=False):
                l, half = n // 2, n % 2
                dve.wait_ge(sem(tile_sem), tile_count)
                for m in range(KC):
                    for st in range(2):
                        cols = slice(P * st, P * st + P)
                        last = v.scalar_tensor_tensor(yLN[:, m, cols], bk(4 + m // 2, 2, TOK)[:, m % 2, cols],
                                                      mod[:, l, 24 * half + 16 + m, st:st + 1], xT[:, m, cols],
                                                      ALU.mult, ALU.add)
                last.then_inc(sem("ln_y"), 1)
                dve.wait_ge(sem("ln_mean"), n + 1)
                chained(sub(yLN, yLN, over(bank[0][:, 0:TOK], KC)))
                mul(mtmp, yLN, yLN).then_inc(sem("ln_sq"), 1)
                dve.wait_ge(sem("ln_var"), n + 1)
                inverse_root(rstd, bank[1][:, 0:TOK], LN_EPS)
                chained(mul(yLN, yLN, over(rstd, KC)))
                for m in range(KC):
                    last = scaled(xT[:, m, :], yLN[:, m, :], lnp[:, l, 2 * half, m:m + 1],
                                  lnp[:, l, 2 * half + 1, m:m + 1])
                if last_norm:
                    last.then_inc(sem("y_ready"), 1)
                else:
                    chained(last)

            def unit_hidden(kind):
                def unit(e, r, u, par, first=False):
                    dve.wait_ge(sem(f"{kind}_sig"), u + 1)
                    if not first:
                        dve.wait_ge(sem(f"{kind}_d_used"), u - 1)
                    hop(kind, u, mul(sgt[par], sgt[par], bk(2 * par, 2, TOK)), 0)
                    ins = mul(hid[par], sgt[par], bk(2 * par + 1, 2, TOK))
                    if kind == "moe":
                        hop(kind, u, ins, 1)
                        gate = gateB[:, bass.ds(e, 1), :].to_broadcast([P, 2, TOK])
                        ins = mul(hid[par], hid[par], gate)
                    ins.then_inc(sem(f"{kind}_hid"), 1)
                return unit

            def hop(kind, u, ins, k):
                per = 2 if kind == "moe" else 1
                ins.then_inc(sem(f"{kind}_step"), 1)
                dve.wait_ge(sem(f"{kind}_step"), u * per + (k + 1))

            def route():
                dve.wait_ge(sem("logits_done"), 1)
                for st in range(2):
                    last = v.tensor_copy(lg[:, st, :], bank[st][:, 0:NE])
                chained(last)
                for st in range(2):
                    last = v.max(top8[:, st, :], lg[:, st, :])
                chained(last)
                for st in range(2):
                    last = v.max_index(idxu[:, st, :], top8[:, st, :], lg[:, st, :])
                chained(last)
                v.tensor_copy(idxf, idxu[:])
                sub(small[:, 0:2], top8[:, :, 1], top8[:, :, 0]).then_inc(sem("gap_ready"), 1)
                dve.wait_ge(sem("gap_exp"), 1)
                chained(v.tensor_scalar(small[:, 2:4], small[:, 0:2], 1.0, None, ALU.add))
                chained(v.reciprocal(small[:, 2:4], small[:, 2:4]))
                chained(mul(small[:, 0:2], small[:, 0:2], small[:, 2:4]))
                for st in range(2):
                    v.tensor_scalar(gts[:, st, :], C("iota8"), idxf[:, st, 0:1], small[:, 2 + st:3 + st],
                                    ALU.is_equal, ALU.mult)
                    last = v.tensor_scalar(top8[:, st, :], C("iota8"), idxf[:, st, 1:2], small[:, st:st + 1],
                                           ALU.is_equal, ALU.mult)
                chained(last)
                chained(add(gts, gts, top8))
                for st in range(2):
                    for e in range(NE):
                        last = scaled(diag[:, st, e, :], C("ident"), gts[:, st, e:e + 1])
                last.then_inc(sem("diag_ready"), 1)
                dve.wait_ge(sem("gates_done"), 1)
                for st in range(2):
                    for q in range(2):
                        last = v.tensor_copy(gateB[:, 4 * q:4 * q + 4, P * st:P * st + P],
                                             bk(4 + 2 * st + q, 4, P))
                last.then_inc(sem("gateB_ready"), 1)

            for l in range(L):
                modulate(l, 0)
                project(l)
                attention(l)
                rwkv_inputs(l)
                for st in range(2):
                    rwkv_stream(l, st)
                rwkv_norm(l)
                gla(l)
                merge(l)
                layer_norm(2 * l, "tile_used", tile_number(l, "out3"))
                modulate(l, 1)
                dve.wait_ge(sem("h_ready"), 2 * l + 2)
                v.tensor_scalar(xT[:], xT[:], ALPHA, None, ALU.mult)
                if l == 0:
                    dense_loop(dve, unit_hidden("dense"))
                    layer_norm(1, "dense_d_used", DENSE_UNITS)
                else:
                    route()
                    moe_loop(dve, unit_hidden("moe"))
                    layer_norm(3, "moe_d_used", MOE_UNITS, last_norm=True)


def lay_out(x):
    def chunks(a):
        a = np.asarray(a)
        a = a.reshape(a.shape[:-1] + (a.shape[-1] // P, P))
        return np.ascontiguousarray(np.moveaxis(a, -1, 0))

    g = {}
    xs = np.concatenate([x["x_prompt"][0], x["x_sample"][0]], 0)
    g["xT"] = np.ascontiguousarray(chunks(xs).transpose(0, 2, 1))
    cc = np.stack([x["c_ctx"], x["c"][0]], 0)
    g["cT"] = np.ascontiguousarray(chunks(cc).transpose(0, 2, 1))
    g["bada"] = chunks(x["b_ada"])
    g["lnp"] = chunks(np.stack([x["ln1_g"], x["ln1_b"], x["ln2_g"], x["ln2_b"]], 1))
    rows = [chunks(x["rwkv_a0"]).reshape(P, L, 4)]
    for n in ["rwkv_k_k", "rwkv_k_a"]:
        rows.append(chunks(x[n]))
    rows.append(chunks(x["rwkv_r_k"].reshape(L, 256)))
    for n in ["rwkv_ln_g", "rwkv_ln_b"]:
        rows.append(chunks(x[n]))
    rows.append(chunks(np.concatenate([x["gla_norm_g"], x["gla_norm_g"]], 1)))
    g["rv"] = np.ascontiguousarray(np.concatenate(rows, 2))
    g["w0row"] = np.ascontiguousarray(x["rwkv_w0"].reshape(1, L, 512))
    g["glbrow"] = np.ascontiguousarray(x["gla_gate_bias"].reshape(1, L, 256))
    sink = x["attn_sink"].reshape(L, 2, 4).transpose(0, 2, 1).reshape(1, L, 8)
    g["sinkB"] = np.ascontiguousarray(np.broadcast_to(sink, (P, L, 8)))

    def on_diagonal(a):
        _, nd, r, n = a.shape
        out = np.zeros((nd * r, L, nd * n), a.dtype)
        for d in range(nd):
            out[d * r:(d + 1) * r, :, d * n:(d + 1) * n] = a[:, d].transpose(1, 0, 2)
        return out

    g["wbB"] = on_diagonal(x["rwkv_w_b"])
    g["abB"] = on_diagonal(x["rwkv_a_b"])
    g["glb"] = on_diagonal(x["gla_gate_b"])
    g["gbw"] = np.ascontiguousarray(x["rwkv_g_b"].transpose(1, 0, 2))
    s = x["state_rwkv"][0].reshape(L, 2, 2, 2, 64, 64)
    g["s0r"] = np.ascontiguousarray(s.transpose(3, 5, 0, 1, 2, 4)).reshape(P, L, 4, 64)
    g["s0g"] = np.ascontiguousarray(x["state_gla"][0].transpose(2, 3, 0, 1, 4)).reshape(P, L, 2, 64)
    g["kcT"] = np.ascontiguousarray(x["cache_attn_k"][0].transpose(2, 3, 0, 1)).reshape(P, L, P)
    g["vc"] = np.ascontiguousarray(x["cache_attn_v"][0].transpose(1, 0, 2, 3)).reshape(P, L, P)
    g["router"] = np.ascontiguousarray(x["moe_router"][0].reshape(KC, P, NE).transpose(1, 0, 2))
    g["cst"] = build_constants()
    for n in ["w_ada", "w_in", "rwkv_w_a", "rwkv_a_a", "rwkv_g_a", "gla_gate_a", "w_up_a", "w_up_b", "w_up_c",
              "w_out", "ffn_w_gate", "ffn_w_up", "ffn_w_down", "moe_w_gate", "moe_w_up", "moe_w_down"]:
        g[n] = np.ascontiguousarray(x[n])
    return g


OUTS = {"yT": (P, KC, TOK), "kT": (L, P, P), "v": (L, P, P), "rwkv": (1, L, 2, 4, 64, 64), "gla": (1, L, 2, 4, 32, 64)}


def kernel(**inputs):
    import concourse.bacc as bacc
    from concourse.bass_utils import run_bass_kernel_spmd

    x = {n: np.asarray(a) for n, a in inputs.items()}
    arrays = lay_out(x)
    nc = bacc.Bacc("TRN2", target_bir_lowering=False, num_devices=1)
    ins = {n: nc.dram_tensor(f"in_{n}", a.shape, mybir.dt.from_np(a.dtype), kind="ExternalInput").ap()
           for n, a in arrays.items()}
    outs = {n: nc.dram_tensor(f"out_{n}", s, F32, kind="ExternalOutput").ap() for n, s in OUTS.items()}
    build_program(nc, ins, outs)
    r = run_bass_kernel_spmd(nc, [{f"in_{n}": a for n, a in arrays.items()}], core_ids=[0]).results[0]
    y = r["out_yT"].transpose(2, 1, 0).reshape(TOK, D)
    k = r["out_kT"].transpose(0, 2, 1).reshape(1, L, P, 2, 64)
    val = r["out_v"].reshape(1, L, P, 2, 64)
    return (np.ascontiguousarray(y[None, 0:P]), np.ascontiguousarray(y[None, P:]), np.ascontiguousarray(k),
            val, r["out_rwkv"], r["out_gla"])
```

```python
from contextlib import ExitStack

import numpy as np

import concourse.bass as bass
from concourse import mybir

ALU = mybir.AluOpType
ACT = mybir.ActivationFunctionType
AX = mybir.AxisListType
F32 = mybir.dt.float32
U32 = mybir.dt.uint32
I32 = mybir.dt.int32

P = 128
D = 1024
KC = D // P
TOK = 2 * P
L = 2
TW = 256
RING = 6
FF = 2816
FFE = 3584
NE = 8
DENSE_UNITS = FF // TW
EXPERT_UNITS = FFE // TW
OVER = 3
LN_EPS = 1e-5
GN_EPS = 64e-5
ALPHA = (2.0 * L) ** 0.25
LEVELS = 6

SMALL = ["decay_rate", "gate_gla"]
FIRST = SMALL + ["q0", "q1", "kv", "br", "bk", "bv", "cqk", "cv", "cog"]
GATES = [f"gate{i}" for i in range(12)]
PROJ = FIRST + GATES
ADA_TILES = 6 * D // TW
ADA_FIRST = ADA_TILES // 2
EARLY = [f"ada{n}" for n in range(ADA_FIRST, L * ADA_TILES)]
MIX = [FIRST + EARLY * (l == 0) + GATES + ["up_a0", "up_a1", "up_b", "up_c"] + [f"out{i}" for i in range(4)]
       for l in range(L)]
MIX_DMAS = {"q0": 4, "q1": 4, "decay_rate": 4, "gate_gla": 3, "up_a0": 2, "up_a1": 2}
MIX_TILES = [len(m) for m in MIX]
MIX_BASE = [0, MIX_TILES[0], sum(MIX_TILES)]

CST = {}


def build_constants():
    t = np.arange(P)
    row, col = t[:, None], t[None, :]
    parts = []

    def add(name, a):
        CST[name] = (sum(x.shape[1] for x in parts), a.shape[1])
        parts.append(a.astype(np.float32))

    add("ident", row == col)
    add("ones", np.ones((P, P)))
    add("mean_d", np.full((P, P), 1.0 / D))
    add("blk", row // 64 == col // 64)
    add("blkm", (row // 64 == col // 64) / 64.0)
    decay = -np.exp(-0.5)
    le, lt, ge, gt = row <= col, row < col, row >= col, row > col
    first, second = row < 64, row >= 64
    for d, (inc, exc, cen) in enumerate([(le, lt, first), (ge, gt, second)]):
        add(f"tri{d}", np.concatenate([inc * 1.0 - cen, exc * 1.0 - cen], 1) * decay)
        add(f"trig{d}", (inc * 1.0 - cen) / 16.0)
        add(f"cen{d}", cen * decay)
        add(f"ceng{d}", cen / 16.0)
        add(f"mask{d}", np.concatenate([exc, exc, inc, inc], 1))
        pair = (row // 2 == col // 2) & (row != col)
        add(f"lv0T{d}", -1.0 * (exc & pair))
        add(f"lv0{d}", -1.0 * (exc.T & pair))
    for j in range(1, LEVELS + 1):
        add(f"lv{j}", (row // 2 ** (j + 1) == col // 2 ** (j + 1)) & (row // 2 ** j != col // 2 ** j))
    inv = (10000.0 ** (-np.arange(0, 32, 2, dtype=np.float32) / 32)).astype(np.float32)
    pos = np.stack([t // 64, t % 64]).astype(np.float32)
    dim = t % 64
    ang = (pos[dim // 32][:, :] * inv[dim % 16][:, None]).astype(np.float32)
    add("cos", np.cos(ang))
    add("sin", np.sin(ang))
    same = row // 32 == col // 32
    add("rot", 1.0 * (same & (row + 16 == col)) - 1.0 * (same & (row == col + 16)))
    add("hm64", (t[:, None] // 64 == np.arange(2)[None]))
    add("hm32", (t[:, None] // 32 == np.arange(4)[None]))
    add("iota", np.broadcast_to(t, (P, P)))
    add("iota8", np.broadcast_to(np.arange(8), (P, 8)))
    return np.concatenate(parts, 1)


NCST = build_constants().shape[1]


def build_program(nc, ins, outs):
    ctx = ExitStack()
    with ctx:
        def sb(name, shape, dt=F32):
            return ctx.enter_context(nc.sbuf_tensor(name, shape, dt))

        used_names = {}

        def sem(name):
            if name not in used_names:
                used_names[name] = ctx.enter_context(nc.semaphore(name))
            return used_names[name]

        ring = sb("ring", [P, RING, KC * TW])
        cst = sb("cst", [P, NCST])
        xT = sb("xT", [P, KC, TOK])
        hT = sb("hT", [P, KC, TOK])
        cT = sb("cT", [P, KC, 2])
        cS = sb("cS", [P, KC, 2])
        bada = sb("bada", [P, L, 48])
        mod = sb("mod", [P, L, 48, 2])
        lnp = sb("lnp", [P, L, 4, KC])
        rv = sb("rv", [P, L, 15])
        omk = sb("omk", [P, L, 2])
        w0row = sb("w0row", [1, L, 512])
        glbrow = sb("glbrow", [1, L, 256])
        sinkB = sb("sinkB", [P, L, 8])
        wbB = sb("wbB", [P, 512])
        abB = sb("abB", [P, 512])
        gbw = sb("gbw", [P, 256])
        glb = sb("glb", [32, 256])
        s0r = sb("s0r", [P, 4, 64])
        s0g = sb("s0g", [P, 2, 64])
        kcT = sb("kcT", [P, P])
        vc = sb("vc", [P, P])
        router = sb("router", [P, KC, NE])
        tanhT = sb("tanhT", [P, TOK])
        aaT = sb("aaT", [P, TOK])
        sgaT = sb("sgaT", [P, TOK])
        glaT = sb("glaT", [32, TOK])
        qT = sb("qT", [P, 4, TOK])
        kT = sb("kT", [P, TOK])
        av = sb("av", [P, 2, P])
        rT = sb("rT", [P, 2, TOK])
        kfT = sb("kfT", [P, 2, TOK])
        vT = sb("vT", [P, 2, TOK])
        cqT = sb("cqT", [P, TOK])
        ckT = sb("ckT", [P, TOK])
        cv = sb("cv", [P, 2, 256])
        ogs = sb("ogs", [P, 2, TOK])
        oaT = sb("oaT", [P, 4, TOK])
        obT = sb("obT", [P, 2, TOK])
        ocT = sb("ocT", [P, 2, TOK])
        WORK, WIDE = 8832, 9600
        work = sb("work", [P, WORK])
        wide = sb("wide", [P, WIDE])
        rowbuf = sb("rowbuf", [2, 2, TW])
        zeros = sb("zeros", [P, 512])
        idxu = sb("idxu", [P, 2, 8], U32)
        passes_i = sb("passes_i", [P, OVER + 1], I32)
        fstate = sb("fstate", [P, 2, 2, P])
        gstate = sb("gstate", [P, 2, 256])
        bank = [ctx.enter_context(nc.psum_tensor(f"bank{i}", [P, 512], F32)) for i in range(8)]

        def ada_rows(t, n):
            return t[32 * (n % 2):32 * (n % 2) + 2, 0:TW]

        def C(name):
            a, n = CST[name]
            return cst[:, a:a + n]

        def shaped(v, shape):
            names = "abcd"[:len(shape)]
            if len(shape) < 2:
                return v
            return v.rearrange(f"p ({' '.join(names)}) -> p {' '.join(names)}",
                               **{k: n for k, n in zip(names[:-1], shape[:-1])})

        def carver(area, size, start=0):
            at = [start]

            def cut(*shape):
                a, n = at[0], int(np.prod(shape))
                assert a + n <= size, (a, n, size)
                at[0] = a + n
                return shaped(area[:, a:a + n], shape)
            return cut

        def bk(i, *shape):
            return shaped(bank[i][:, 0:int(np.prod(shape))], shape)

        cut = carver(work, WORK)
        qL, kxL, kxP = cut(4, P), cut(2, 256), cut(2, P)
        pL, pP, pT = cut(8, 256), cut(8, P), cut(24, P)
        mneg, den, esink = cut(16), cut(16), cut(16)
        atmp, krot, rtmp_k = cut(4, P), cut(P), cut(P)
        cut = carver(work, WORK)
        sigz = cut(2, 512)
        aT, kapT, akT, ktT = cut(2, 2, TOK), cut(2, TOK), cut(2, 2, TOK), cut(2, 2, TOK)
        gT, bonT, Vn, yT, rtmp, rtmp2 = (cut(2, TOK) for _ in range(6))
        Bc, KcR = [cut(2, P) for _ in range(2)], [cut(2, P) for _ in range(2)]
        cut = carver(wide, WIDE)
        KR = [cut(2, 2, 2, P) for _ in range(2)]
        MTQ = [cut(2, 2, 2, P) for _ in range(2)]
        AKQ = [cut(2, 2, 2, P) for _ in range(2)]
        shared = 1024 * 6
        Tm, TmT = [cut(4, P) for _ in range(2)], [cut(4, P) for _ in range(2)]
        Xs, nU = [cut(256) for _ in range(2)], [cut(256) for _ in range(2)]
        s0c, ecr, elast = cut(4, 64), cut(4), cut(4)
        P1 = [qT[:, 2 * d:2 * d + 2, :].rearrange("p a (b t) -> p (a b) t", b=2) for d in range(2)]
        cut = carver(wide, WIDE, shared)
        Ep, En = [cut(2, 2, P) for _ in range(2)], [cut(2, P) for _ in range(2)]
        K2T = carver(wide, WIDE, shared)(2, 4, P)
        K2n = P1
        cut = carver(work, WORK)
        glog, gtm = cut(512), cut(512)
        EG, EGn, Qh = cut(4, P), cut(4, P), cut(P)
        Qx, KcG, attT = cut(4, 4, P), cut(4, P), cut(4, 4, P)
        K2g, K2gn, s0gc, ecg = cut(2, P), cut(2, P), cut(2, 64), cut(2)
        oc, gsq = cut(512), cut(512)
        sg = carver(wide, WIDE)(24, TOK)
        cut = carver(work, WORK)
        merged, mtmp, yLN, rstd = cut(KC, TOK), cut(KC, TOK), cut(KC, TOK), cut(TOK)
        cut = carver(work, WORK)
        hid, sgt = [cut(2, TOK) for _ in range(2)], [cut(2, TOK) for _ in range(2)]
        cut = carver(work, WORK)
        xgT, ysb, selT = cut(KC, P), cut(D), cut(TOK)
        sel, selg = cut(2, P), cut(2, P)
        mhid, mhidT, msig = ([cut(TW) for _ in range(2)] for _ in range(3))
        cut = carver(wide, WIDE)
        accT, hN = cut(KC, TOK), cut(2, D)
        lg, top8, idxf, gts, pick2, member, slotno = (cut(2, 8) for _ in range(7))
        gap, crowded, rank, onehot = cut(2, 2), cut(8), cut(8), cut(8)
        rtab, ptab, gtab, evf = cut(2, 8), cut(2, NE + OVER + 1), cut(2, NE + OVER + 1), cut(OVER + 1)

        block = ctx.enter_context(nc.Block())

        def w_tile(l, name):
            w_in = ins["w_in"][l].rearrange("(c p) n -> p c n", p=P)
            if name == "decay_rate":
                return [((slice(None), 64 * d + 128 * a, 64), ins[w][l, d].rearrange("(c p) n -> p c n", p=P))
                        for a, w in enumerate(["rwkv_w_a", "rwkv_a_a"]) for d in range(2)]
            if name == "gate_gla":
                return [((slice(None), 0, P), ins["rwkv_g_a"][l].rearrange("(c p) n -> p c n", p=P))] + [
                    ((slice(None), P + 16 * d, 16), ins["gla_gate_a"][l, d].rearrange("(c p) n -> p c n", p=P))
                    for d in range(2)]
            if name in ("q0", "q1"):
                h0 = 2 * int(name[1])
                return [((slice(None), P * jj + 64 * g, 64), w_in[:, :, 256 * g + 64 * (h0 + jj):256 * g + 64 * (h0 + jj) + 64])
                        for jj in range(2) for g in range(2)]
            t = PROJ.index(name) - len(SMALL)
            return [((slice(None), 0, TW), w_in[:, :, t * TW:(t + 1) * TW])]

        def slot8(s):
            return ring[:, s, :].rearrange("p (c n) -> p c n", c=KC)

        def slot2(s):
            return ring[:, s, :].rearrange("p (c n) -> p c n", c=2)

        fills = {}
        count = [0] * RING
        for l in range(L):
            for i, n in enumerate(MIX[l]):
                count[i % RING] += 16 * MIX_DMAS.get(n, 1)
                fills[(l, n)] = (i % RING, count[i % RING])

        def tile_number(l, name):
            return MIX_BASE[l] + MIX[l].index(name) + 1

        EVAC = {"decay_rate": "act", "gate_gla": "act", "q0": "dve", "q1": "dve", "kv": "dve", "br": "act",
                "bk": "dve", "bv": "act", "cqk": "dve", "cv": "act", "cog": "dve"}
        EVAC.update({g: "act" for g in GATES})
        evac_at, n = {}, {"act": 0, "dve": 0}
        for name in PROJ:
            n[EVAC[name]] += 1
            evac_at[name] = (EVAC[name], n[EVAC[name]])
        EV_ACT, EV_DVE = n["act"], n["dve"]

        def evacuated(eng, l, name):
            who, k = evac_at[name]
            eng.wait_ge(sem(f"ev_{who}"), (EV_ACT if who == "act" else EV_DVE) * l + k)

        def dense_loop(eng, unit):
            for par in range(2):
                unit(0, par, par, par, True)
            with eng.Fori(1, DENSE_UNITS // 2) as i:
                for par in range(2):
                    unit(0, i * 2 + par, i * 2 + par, par)
            unit(0, DENSE_UNITS - 1, DENSE_UNITS - 1, 0)

        def second_passes(eng):
            eng.wait_ge(sem("passes_known"), 1)
            return eng.value_load(passes_i[0:1, 0:1], min_val=0, max_val=OVER)

        @block.sync
        def _(sp):
            for name, dst in [("cT", cT), ("cst", cst), ("xT", xT), ("bada", bada), ("lnp", lnp), ("rv", rv),
                              ("w0row", w0row), ("glbrow", glbrow), ("sinkB", sinkB), ("router", router)]:
                sp.dma_start(dst[:], ins[name]).then_inc(sem("params_in"), 16)

            def layer_params(l):
                if l > 0:
                    sp.wait_ge(sem("gla_out"), l)
                for name, dst in [("wbB", wbB), ("abB", abB), ("gbw", gbw), ("glb", glb), ("s0r", s0r),
                                  ("s0g", s0g), ("kcT", kcT), ("vc", vc)]:
                    sp.dma_start(dst[:], ins[name][:, l]).then_inc(sem("layer_in"), 16)

            layer_params(0)

            ada = ins["w_ada"].rearrange("l (c p) n -> p l c n", p=P)
            for n in range(ADA_FIRST):
                if n >= RING:
                    sp.wait_ge(sem("ada_used"), n + 1 - RING)
                sp.dma_start(slot8(n % RING), ada[:, 0, :, n * TW:(n + 1) * TW]).then_inc(sem(f"ada_full{n % RING}"), 16)

            def mixer_tiles(l):
                for i, name in enumerate(MIX[l]):
                    s = i % RING
                    if i >= RING:
                        sp.wait_ge(sem("tile_used"), MIX_BASE[l] + i - RING + 1)
                    elif l == 0:
                        sp.wait_ge(sem("ada_used"), ADA_FIRST - RING + s + 1)
                    else:
                        sp.wait_ge(sem("dense_gu_used" if s % 3 < 2 else "dense_d_used"),
                                   DENSE_UNITS if s < 3 else DENSE_UNITS - 1)
                    full = sem(f"mix_full{s}")
                    if name in EARLY:
                        n = int(name[3:])
                        sp.dma_start(slot8(s), ada[:, n // ADA_TILES, :, (n % ADA_TILES) * TW:(n % ADA_TILES + 1) * TW])\
                            .then_inc(full, 16)
                    elif name in PROJ:
                        for (_, c0, cn), src in w_tile(l, name):
                            sp.dma_start(slot8(s)[:, :, c0:c0 + cn], src).then_inc(full, 16)
                    elif name.startswith("up_a"):
                        j0 = 2 * int(name[-1])
                        wa = ins["w_up_a"][l].rearrange("(g j d) n -> g d j n", g=2, j=4)
                        for g in range(2):
                            sp.dma_start(slot2(s)[64 * g:64 * g + 64], wa[g, :, j0:j0 + 2, :]).then_inc(full, 16)
                    else:
                        if name in ("up_b", "up_c"):
                            w = ins["w_" + name][l]
                        else:
                            w = ins["w_out"][l][int(name[-1]) * 256:int(name[-1]) * 256 + 256, :]
                        sp.dma_start(slot2(s), w.rearrange("(c p) n -> p c n", p=P)).then_inc(full, 16)

            def unit_loads(kind, u, par, gate, up, down):
                for k, src in enumerate([gate, up, down]):
                    s = 3 * par + k
                    if u is None:
                        l = int(kind == "moe")
                        last = max(i for i in range(MIX_TILES[l]) if i % RING == s)
                        sp.wait_ge(sem("tile_used"), MIX_BASE[l] + last + 1)
                    elif k != 1:
                        sp.wait_ge(sem(f"{kind}_{'gu' if k == 0 else 'd'}_used"), u - 1 + 2 * (kind == "moe"))
                    sp.dma_start(slot8(s) if k < 2 else slot2(s), src).then_inc(sem(f"{kind}_full{s}"), 16)

            mixer_tiles(0)
            dg = ins["ffn_w_gate"][0].rearrange("(c p) n -> p c n", p=P)
            du = ins["ffn_w_up"][0].rearrange("(c p) n -> p c n", p=P)
            dd = ins["ffn_w_down"][0].rearrange("(u c p) n -> p u c n", p=P, c=2)

            def dense_unit(e, r, u, par, first=False):
                cols = bass.ds(u * TW, TW)
                unit_loads("dense", None if first else u, par, dg[:, :, cols], du[:, :, cols],
                           dd[:, bass.ds(u, 1)].rearrange("p u c n -> p (u c) n"))

            dense_loop(sp, dense_unit)
            layer_params(1)
            mixer_tiles(1)
            mg = ins["moe_w_gate"][0].rearrange("e (c p) n -> p e c n", p=P)
            mu = ins["moe_w_up"][0].rearrange("e (c p) n -> p e c n", p=P)
            md = ins["moe_w_down"][0].rearrange("e (u c p) n -> p (e u) c n", p=P, c=2)

            def moe_unit(e, r, u, par, first=False):
                cols = bass.ds(r * TW, TW)
                unit_loads("moe", None if first else u, par,
                           mg[:, bass.ds(e, 1), :, cols].rearrange("p e c n -> p (e c) n"),
                           mu[:, bass.ds(e, 1), :, cols].rearrange("p e c n -> p (e c) n"),
                           md[:, bass.ds(e * EXPERT_UNITS + r, 1)].rearrange("p u c n -> p (u c) n"))

            for par in range(2):
                moe_unit(0, par, par, par, True)
            with sp.Fori(1, EXPERT_UNITS // 2) as i:
                for par in range(2):
                    moe_unit(0, i * 2 + par, i * 2 + par, par)
            with sp.Fori(1, NE) as e:
                with sp.Fori(0, EXPERT_UNITS // 2) as i:
                    for par in range(2):
                        moe_unit(e, i * 2 + par, e * EXPERT_UNITS + i * 2 + par, par)
            n_over = second_passes(sp)
            with sp.If(n_over > 0):
                with sp.Fori(0, n_over) as j:
                    expert = sp.value_load(passes_i[0:1, bass.ds(j + 1, 1)], min_val=0, max_val=NE - 1)
                    with sp.Fori(0, EXPERT_UNITS // 2) as i:
                        for par in range(2):
                            moe_unit(expert, i * 2 + par, (j + NE) * EXPERT_UNITS + i * 2 + par, par)
            sp.wait_ge(sem("y_ready"), 1)
            sp.dma_start(outs["yT"], xT[:]).then_inc(sem("stored"), 16)
            sp.wait_ge(sem("stored"), 16)

        @block.gpsimd
        def _(pool):
            for l in range(L):
                evacuated(pool, l, "kv")
                pool.dma_start(outs["kT"][l], kT[:, 0:P]).then_inc(sem("kept"), 16)
                pool.dma_start(outs["v"][l], av[:, 0, :]).then_inc(sem("kept"), 16)
                pool.wait_ge(sem("fstate_ready"), l + 1)
                for i in range(2):
                    dst = outs["rwkv"][0, l].rearrange("d (c i) v k -> i v d c k", i=2)[i]
                    for d in range(2):
                        pool.dma_start(dst[:, d], fstate[64 * i:64 * i + 64, d, :, 64 * i:64 * i + 64])\
                            .then_inc(sem("kept"), 16)
                pool.wait_ge(sem("gstate_ready"), l + 1)
                for h in range(4):
                    pool.dma_start(outs["gla"][0, l, :, h].rearrange("d k v -> k d v"),
                                   gstate[32 * h:32 * h + 32, :, 64 * h:64 * h + 64]).then_inc(sem("kept"), 16)
                pool.wait_ge(sem("kept"), 160 * (l + 1))

        @block.tensor
        def _(pe):
            mm = nc.tensor.matmul
            ident = C("ident")

            def acc(out, pairs, **kw):
                for n, (a, b) in enumerate(pairs):
                    last = mm(out, a, b, start=(n == 0), stop=(n == len(pairs) - 1), **kw)
                return last

            pe.wait_ge(sem("silu_c"), 1)

            def ada_tile(n, s, full, used):
                pe.wait_ge(full[0], full[1])
                if n >= 2:
                    pe.wait_ge(sem("ada_row"), n - 1)
                acc(ada_rows(bank[0], n), [(cS[:, c, :], slot8(s)[:, c, :])
                                           for c in range(KC)]).then_inc(used, 1)

            def ada_turn(n):
                pe.wait_ge(sem("ada_row"), n + 1)
                for h in range(2):
                    c = 4 * (n if n < ADA_FIRST else n - ADA_FIRST) + 2 * h
                    last = nc.tensor.transpose(bank[1][:, c:c + 2], rowbuf[:, n % 2, P * h:P * h + P],
                                               C("ident")[0:2, 0:2])
                last.then_inc(sem("ada_turned"), 1)

            for n in range(ADA_FIRST):
                ada_tile(n, n % RING, (sem(f"ada_full{n % RING}"), 16 * (n // RING + 1)), sem("ada_used"))
                if n >= 1:
                    ada_turn(n - 1)
            ada_turn(ADA_FIRST - 1)
            early = [ADA_FIRST]

            def early_tiles(count):
                for _ in range(count):
                    n = early[0]
                    early[0] += 1
                    if n == ADA_FIRST:
                        evacuated(pe, 0, "cv")
                        evacuated(pe, 0, "cog")
                    s, full = fills[(0, f"ada{n}")]
                    ada_tile(n, s, (sem(f"mix_full{s}"), full), sem("tile_used"))
                    if n > ADA_FIRST:
                        ada_turn(n - 1)
                    if n == L * ADA_TILES - 1:
                        ada_turn(n)

            def project(l, names):
                if names is FIRST:
                    pe.wait_ge(sem("h_ready"), 2 * l + 1)
                for name in names:
                    i = PROJ.index(name)
                    s, full = fills[(l, name)]
                    b = bk(i % 2, 2, TOK)
                    if l == 0 and i < 2:
                        pe.wait_ge(sem("mod_read"), 1)
                    if l == 0 and name == "gate0":
                        pe.wait_ge(sem("mod_read"), 2)
                    if i >= 2:
                        evacuated(pe, l, PROJ[i - 2])
                    pe.wait_ge(sem(f"mix_full{s}"), full)
                    w = slot8(s)
                    if name == "kv":
                        acc(b[:, 0, :], [(w[:, c, 0:P], hT[:, c, :]) for c in range(KC)])
                        for st in range(2):
                            last = acc(bank[i % 2][:, 256 + P * st:384 + P * st],
                                       [(hT[:, c, P * st:P * st + P], w[:, c, P:2 * P]) for c in range(KC)])
                    elif name == "cv":
                        for st in range(2):
                            last = acc(b[:, st, :], [(hT[:, c, P * st:P * st + P], w[:, c, :]) for c in range(KC)])
                    elif name == "gate_gla":
                        acc(b[:, 0, :], [(w[:, c, 0:P], hT[:, c, :]) for c in range(KC)])
                        last = acc(b[0:32, 1, :], [(w[:, c, P:P + 32], hT[:, c, :]) for c in range(KC)])
                    else:
                        for h in range(2):
                            last = acc(b[:, h, :], [(w[:, c, P * h:P * h + P], hT[:, c, :]) for c in range(KC)])
                    last.then_inc(sem("tile_used"), 1)

            def attention(l):
                evacuated(pe, l, "kv")
                pe.wait_ge(sem("layer_in"), 128 * (l + 1))
                mm(bank[2][:, :], C("rot"), qT[:, :, P:TOK], start=True, stop=True)
                mm(bank[3][:, 0:P], C("rot"), kT[:, P:TOK], start=True, stop=True).then_inc(sem("rot_done"), 1)
                pe.wait_ge(sem("attn_in"), l + 1)
                for j in range(4):
                    mm(bank[4 + j][:, :], qL[:, j, :], kxL[:, :, :], start=True, stop=True)
                for j in range(4):
                    last = mm(bk(2 + j // 2, 2, 256)[:, j % 2, :], qT[:, j, 0:P], kxP[:, :, :], start=True, stop=True)
                last.then_inc(sem("scores_done"), 1)
                pe.wait_ge(sem("probs_ready"), l + 1)
                for n in range(24):
                    src = pL[:, n // 2, P * (n % 2):P * (n % 2) + P] if n < 16 else pP[:, n - 16, :]
                    b = 4 + n // 4 if n < 16 else 2 + (n - 16) // 4
                    last = nc.tensor.transpose(bk(b, 4, P)[:, n % 4, :], src, ident)
                last.then_inc(sem("probsT_done"), 1)
                pe.wait_ge(sem("probsT_dve"), l + 1)
                pe.wait_ge(sem("probsT_act"), l + 1)
                for j in range(4):
                    out = bk(2 + j // 2, 2, TOK)
                    for g in range(2):
                        h = 2 * j + g
                        mm(out[64 * g:64 * g + 64, j % 2, 0:P], av[:, 0, 64 * g:64 * g + 64], pT[:, 16 + h, :],
                           start=True, stop=True)
                        mm(out[64 * g:64 * g + 64, j % 2, P:TOK], av[:, 1, 64 * g:64 * g + 64], pT[:, 2 * h, :],
                           start=True, stop=False)
                        last = mm(out[64 * g:64 * g + 64, j % 2, P:TOK], vc[:, 64 * g:64 * g + 64],
                                  pT[:, 2 * h + 1, :], start=False, stop=True)
                last.then_inc(sem("attn_done"), 1)

            def rwkv_inputs(l):
                pe.wait_ge(sem("attn_out"), l + 1)
                evacuated(pe, l, "gate_gla")
                evacuated(pe, l, "bv")
                for st in range(2):
                    mm(bank[2 + st][:, :], tanhT[:, P * st:P * st + P], wbB[:, :], start=True, stop=False)
                    mm(bank[2 + st][:, :], C("ones")[0:1, :], w0row[:, l, :], start=False, stop=True)
                for d in range(2):
                    for c in range(2):
                        mm(bk(4 + d, 2, TOK)[:, c, :], abB[:, 256 * d + P * c:256 * d + P * c + P], aaT[:, :],
                           start=True, stop=True)
                for c in range(2):
                    last = mm(bk(6, 2, TOK)[:, c, :], gbw[:, P * c:P * c + P], sgaT[:, :], start=True, stop=True)
                last.then_inc(sem("rw_logits"), 1)
                pe.wait_ge(sem("kk_sq"), l + 1)
                mm(bank[7][:, :], C("blk"), rtmp, start=True, stop=True).then_inc(sem("kk_norm"), 1)
                pe.wait_ge(sem("rw_act"), l + 1)
                for st in range(2):
                    for c in range(2):
                        last = nc.tensor.transpose(bk(2, 2, 2, P)[:, st, c, :], vT[:, c, P * st:P * st + P], ident)
                last.then_inc(sem("vn_done"), 1)
                pe.wait_ge(sem("bonus_in"), l + 1)
                mm(bank[3][:, :], C("blk"), rtmp2, start=True, stop=True).then_inc(sem("bonus_sum"), 1)
                pe.wait_ge(sem("bonus_out"), l + 1)

            def rwkv_stream(l, st):
                k = 2 * l + st + 1
                for d in range(2):
                    for c in range(2):
                        last = mm(bk(2 + d, 2, 256)[:, c, :], sigz[:, st, 256 * d + P * c:256 * d + P * c + P],
                                  C(f"tri{d}"), start=True, stop=True)
                if st == 1:
                    for d in range(2):
                        for c in range(2):
                            last = mm(bank[4][:, 2 * d + c:2 * d + c + 1],
                                      sigz[:, st, 256 * d + P * c:256 * d + P * c + P], C(f"cen{d}"),
                                      start=True, stop=True)
                last.then_inc(sem("cum_done"), 1)
                pe.wait_ge(sem("decays_ready"), 2 * k)
                for d in range(2):
                    pe.wait_ge(sem("khat_ready"), 2 * (k - 1) + d + 1)
                    if d == 1:
                        pe.wait_ge(sem("mats_read"), 2 * (k - 1) + 1)
                    for c in range(2):
                        mm(bank[2 + c][:, :], Bc[d][:, c, :], KR[d][:, c, :, :, :], start=True, stop=True)
                        mm(bank[4 + c][:, :], KcR[d][:, c, :], KR[d][:, c, :, :, :], start=True, stop=True)
                    for c in range(2):
                        for i in range(2):
                            last = mm(bk(6, 4, P)[:, 2 * c + i, :], KR[d][:, c, 0, i, :], Bc[d][:, c, :],
                                      start=True, stop=True)
                    last.then_inc(sem("mats_done"), 1)
                for j in range(1, LEVELS + 1):
                    n = (k - 1) * LEVELS + j
                    for d in range(2):
                        if j == 1:
                            pe.wait_ge(sem("mats_read"), 2 * k)
                        else:
                            pe.wait_ge(sem(f"inv_T{d}"), n - 1)
                        for h in range(4):
                            last = mm(bk(2 + 3 * d, 4, P)[:, h, :], MTQ[d][:, h // 2, 0, h % 2, :], Tm[d][:, h, :],
                                      start=True, stop=True)
                        last.then_inc(sem(f"inv_MT{d}"), 1)
                    if l == 0:
                        early_tiles(1)
                    for d in range(2):
                        pe.wait_ge(sem(f"inv_P{d}"), n)
                        for h in range(4 if j < LEVELS else 0):
                            mm(bk(3 + 3 * d, 4, P)[:, h, :], TmT[d][:, h, :], P1[d][:, h, :], start=True, stop=True)
                        for h in range(4):
                            last = mm(bk(4 + 3 * d, 4, P)[:, h, :], P1[d][:, h, :],
                                      TmT[d][:, h, :], start=True, stop=True)
                        last.then_inc(sem(f"inv_TP{d}"), 1)
                    if l == 0:
                        early_tiles(2)
                for d in range(2):
                    pe.wait_ge(sem(f"inv_T{d}"), k * LEVELS)
                    for h in range(4):
                        c, i = h // 2, h % 2
                        out = bank[2 + d][:, 64 * h:64 * h + 64]
                        pairs = [(AKQ[d][:, c, 0, i, :], Vn[:, st, 64 * h:64 * h + 64])]
                        if st == 1:
                            pairs.append((KR[d][:, c, 0, i, :], s0c[:, 2 * d + c, :]))
                        last = acc(out, pairs)
                    last.then_inc(sem("x_done"), 1)
                for d in range(2):
                    pe.wait_ge(sem("xs_ready"), 2 * (k - 1) + d + 1)
                    for h in range(4):
                        last = mm(bank[4 + d][:, 64 * h:64 * h + 64], TmT[d][:, h, :], Xs[d][:, 64 * h:64 * h + 64],
                                  start=True, stop=True)
                    last.then_inc(sem("u_done"), 1)
                pe.wait_ge(sem("nu_ready"), 2 * k)
                for c in range(2):
                    for i in range(2):
                        h = 2 * c + i
                        pairs = []
                        for d in range(2):
                            pairs.append((Vn[:, st, 64 * h:64 * h + 64], AKQ[d][:, c, 1, i, :]))
                            pairs.append((nU[d][:, 64 * h:64 * h + 64], MTQ[d][:, c, 1, i, :]))
                            if st == 1:
                                pairs.append((s0c[:, 2 * d + c, :], KR[d][:, c, 1, i, :]))
                        last = acc(bk(6, 2, P)[64 * i:64 * i + 64, c, :], pairs)
                last.then_inc(sem("y_done"), 1)
                if st == 0:
                    pe.wait_ge(sem("k2_ready"), l + 1)
                    for x in range(2):
                        for e in range(4):
                            last = nc.tensor.transpose(bk(2 + x, 4, P)[:, e, :], K2T[:, x, e, :], ident)
                    last.then_inc(sem("k2T_done"), 1)
                    pe.wait_ge(sem("k2n_ready"), l + 1)
                    for d in range(2):
                        for c in range(2):
                            last = acc(bk(7, 4, P)[:, 2 * d + c, :],
                                       [(Vn[:, 0, P * c:P * c + P], K2n[0][:, 2 * d + c, :]),
                                        (nU[d][:, P * c:P * c + P], K2n[1][:, 2 * d + c, :])])
                    last.then_inc(sem("fs_done"), 1)
                    pe.wait_ge(sem("fstate_ready"), l + 1)
                pe.wait_ge(sem("yT_ready"), k)

            def rwkv_norm(l):
                mm(bank[2][:, :], C("blkm"), yT[:, :, :], start=True, stop=True).then_inc(sem("gn_mean"), 1)
                pe.wait_ge(sem("gn_sq"), l + 1)
                mm(bank[3][:, :], C("blkm"), rtmp, start=True, stop=True).then_inc(sem("gn_var"), 1)

            def gla(l):
                pe.wait_ge(sem("rwkv_out"), l + 1)
                evacuated(pe, l, "cog")
                for st in range(2):
                    mm(bk(2, 2, 256)[:, st, :], glaT[:, P * st:P * st + P], glb[:, :], start=True, stop=False)
                    last = mm(bk(2, 2, 256)[:, st, :], C("ones")[0:1, :], glbrow[:, l, :], start=False, stop=True)
                last.then_inc(sem("gl_done"), 1)
                pe.wait_ge(sem("glog_ready"), l + 1)
                lgv = glog.rearrange("p (s d c) -> p s d c", s=2, d=2)
                for st in range(2):
                    for d in range(2):
                        mm(bk(3, 4, P)[:, 2 * st + d, :], lgv[:, st, d, :], C(f"trig{d}"), start=True, stop=True)
                for d in range(2):
                    last = mm(bank[4][:, d:d + 1], lgv[:, 1, d, :], C(f"ceng{d}"), start=True, stop=True)
                last.then_inc(sem("gcum_done"), 1)
                pe.wait_ge(sem("gq_ready"), l + 1)
                for x in range(4):
                    last = mm(bank[4 + x][:, :], KcG[:, x, :], Qx[:, x, :, :], start=True, stop=True)
                last.then_inc(sem("att_done"), 1)
                pe.wait_ge(sem("att_ready"), l + 1)
                for st in range(2):
                    for h in range(4):
                        c, i = h // 2, h % 2
                        pairs = []
                        for d in range(2):
                            pairs.append((cv[:, st, 64 * h:64 * h + 64], attT[:, 2 * st + d, h, :]))
                            if st == 1:
                                pairs.append((s0gc[:, d, :], Qx[:, 2 * st + d, h, :]))
                        last = acc(bk(2, 2, TOK)[64 * i:64 * i + 64, c, P * st:P * st + P], pairs)
                last.then_inc(sem("go_done"), 1)
                for d in range(2):
                    last = nc.tensor.transpose(bk(3, 4, P)[:, d, :], K2g[:, d, :], ident)
                last.then_inc(sem("k2g_done"), 1)
                pe.wait_ge(sem("k2g_ready"), l + 1)
                for d in range(2):
                    last = mm(bk(4, 2, 256)[:, d, :], K2gn[:, d, :], cv[:, 0, :], start=True, stop=True)
                last.then_inc(sem("gs_done"), 1)
                pe.wait_ge(sem("gsq_ready"), l + 1)
                mm(bank[5][:, :], C("blkm"), gsq, start=True, stop=True).then_inc(sem("gms_done"), 1)

            def rows_outer(l, tiles, src, first_bank):
                n = 0
                for name in tiles:
                    s, full = fills[(l, name)]
                    pe.wait_ge(sem(f"mix_full{s}"), full)
                    for c in range(2):
                        for m in range(KC):
                            last = mm(bk(first_bank + m // 2, 2, TOK)[:, m % 2, :], slot2(s)[:, c, P * m:P * m + P],
                                      src[:, n, :], start=(n == 0 and m % 2 == 0),
                                      stop=(n == 2 * len(tiles) - 1), skip_group_check=True)
                        n += 1
                    last.then_inc(sem("tile_used"), 1)

            def merge(l):
                evacuated(pe, l, "gate11")
                evacuated(pe, l, "gate10")
                pe.wait_ge(sem("gla_out"), l + 1)
                rows_outer(l, ["up_a0", "up_a1"], oaT, 0)
                rows_outer(l, ["up_b"], obT, 4)
                pe.wait_ge(sem("up_read"), 3 * l + 1)
                rows_outer(l, ["up_c"], ocT, 0)
                pe.wait_ge(sem("up_read"), 3 * l + 3)
                rows_outer(l, [f"out{i}" for i in range(4)], merged, 4)

            def layer_norm(n):
                pe.wait_ge(sem("ln_y"), n + 1)
                acc(bank[0][:, 0:TOK], [(C("mean_d"), yLN[:, m, :]) for m in range(KC)]).then_inc(sem("ln_mean"), 1)
                pe.wait_ge(sem("ln_sq"), n + 1)
                acc(bank[1][:, 0:TOK], [(C("mean_d"), mtmp[:, m, :]) for m in range(KC)]).then_inc(sem("ln_var"), 1)

            def gate_up(kind, par, k):
                pe.wait_ge(sem(f"{kind}_full{3 * par}"), k * 16)
                for h in range(2):
                    acc(bk(2 * par, 2, TOK)[:, h, :], [(slot8(3 * par)[:, c, P * h:P * h + P], hT[:, c, :])
                                                       for c in range(KC)])
                pe.wait_ge(sem(f"{kind}_full{3 * par + 1}"), k * 16)
                for h in range(2):
                    last = acc(bk(2 * par + 1, 2, TOK)[:, h, :], [(slot8(3 * par + 1)[:, c, P * h:P * h + P], hT[:, c, :])
                                                                  for c in range(KC)])
                last.then_inc(sem(f"{kind}_gu_used"), 1)

            def down(kind, par, k, hid_count):
                pe.wait_ge(sem(f"{kind}_full{3 * par + 2}"), k * 16)
                pe.wait_ge(sem(f"{kind}_hid"), hid_count)
                for c in range(2):
                    for m in range(KC):
                        last = mm(bk(4 + m // 2, 2, TOK)[:, m % 2, :], slot2(3 * par + 2)[:, c, P * m:P * m + P],
                                  hid[par][:, c, :], start=False, stop=False, skip_group_check=True)
                last.then_inc(sem(f"{kind}_d_used"), 1)

            def dense_mixer():
                kind, units = "dense", DENSE_UNITS
                pe.wait_ge(sem("h_ready"), 2)
                for b in range(4):
                    mm(bank[4 + b][:, :], zeros[:, 0:P], zeros[:, :], start=True, stop=False,
                       skip_group_check=True)
                gate_up(kind, 0, 1)

                def turn(i):
                    for par in (1, 0):
                        if par == 0 or not isinstance(i, int):
                            pe.wait_ge(sem(f"{kind}_hid"), i * 2 + (0 if par else 1))
                        gate_up(kind, par, i + (1 if par else 2))
                        down(kind, 1 - par, i + 1, i * 2 + (1 if par else 2))

                turn(0)
                with pe.Fori(1, units // 2) as i:
                    turn(i)
                down(kind, 0, (units + 1) // 2, units)

            def expert_mixer():
                pe.wait_ge(sem("h_ready"), 4)
                for st in range(2):
                    last = acc(bank[st][:, 0:NE], [(hT[:, c, P * st:P * st + P], router[:, c, :]) for c in range(KC)])
                last.then_inc(sem("logits_done"), 1)
                for st in range(2):
                    for m in range(KC):
                        last = nc.tensor.transpose(bk(4 + 2 * st + m // 4, 4, P)[:, m % 4, :],
                                                   hT[:, m, P * st:P * st + P], ident)
                last.then_inc(sem("hN_done"), 1)
                pe.wait_ge(sem("member_ready"), 1)
                before = C("mask0")[:, 0:P]
                mm(bank[2][:, 0:NE], before, member[:, 0, :], start=True, stop=True)
                acc(bank[2][:, NE:2 * NE], [(before, member[:, 1, :]), (C("ones"), member[:, 0, :])])
                acc(bank[2][:, 2 * NE:3 * NE], [(C("ones"), member[:, 0, :]), (C("ones"), member[:, 1, :])])\
                    .then_inc(sem("slots_done"), 1)
                pe.wait_ge(sem("hN_ready"), 1)
                pe.sem_inc(sem("moe_gu_used"), 2)
                pe.sem_inc(sem("moe_d_used"), 2)

                def gather(p):
                    pe.wait_ge(sem("moe_sel"), p + 1)
                    for m in range(KC):
                        last = acc(bk(6 + m // 4, 4, P)[:, m % 4, :],
                                   [(hN[:, st, P * m:P * m + P], sel[:, st, :]) for st in range(2)])
                    last.then_inc(sem("moe_xg_done"), 1)

                def turn_selection():
                    for st in range(2):
                        last = nc.tensor.transpose(bank[1][:, P * st:P * st + P], selg[:, st, :], ident)
                    last.then_inc(sem("moe_selT_done"), 1)

                def rows(k, par, p, u):
                    pe.wait_ge(sem(f"moe_full{3 * par + k}"), u[1] * 16)
                    if k == 0:
                        pe.wait_ge(sem("moe_hid"), u[0] + 1)
                    last = acc(bank[par][:, TW * k:TW * k + TW], [(xgT[:, c, :], slot8(3 * par + k)[:, c, :])
                                                                  for c in range(KC)])
                    if k == 1:
                        last.then_inc(sem("moe_gu_used"), 1)

                def turn_hidden(par, u):
                    pe.wait_ge(sem("moe_hid"), u[0] + 3)
                    pe.wait_ge(sem("moe_hidT"), u[0] + 1)
                    for c in range(2):
                        last = nc.tensor.transpose(bank[2 + par][:, P * c:P * c + P], mhid[par][:, P * c:P * c + P], ident)
                    last.then_inc(sem("moe_turned"), 1)

                def down_rows(par, u, first=False, final=False):
                    pe.wait_ge(sem(f"moe_full{3 * par + 2}"), u[1] * 16)
                    pe.wait_ge(sem("moe_hidT"), u[0] + 3)
                    for c in range(2):
                        for h in range(2):
                            last = mm(bank[4 + h][:, :], mhidT[par][:, P * c:P * c + P],
                                      slot2(3 * par + 2)[:, c, 512 * h:512 * h + 512], start=(first and c == 0),
                                      stop=(final and c == 1), skip_group_check=True)
                    last.then_inc(sem("moe_d_used"), 1)

                def step(par, p, here, ahead, first=False):
                    rows(0, 1 - par, p, ahead)
                    turn_hidden(par, here)
                    rows(1, 1 - par, p, ahead)
                    down_rows(par, here, first)

                gather(0)
                turn_selection()
                n_pass = second_passes(pe) + NE
                H = EXPERT_UNITS // 2
                with pe.Fori(0, n_pass) as p:
                    def unit(k, i=0):
                        return p * EXPERT_UNITS + (i * 2 + k), p * H + (i + (k // 2 + 1))
                    pe.wait_ge(sem("moe_xg"), p + 1)
                    rows(0, 0, p, unit(0))
                    rows(1, 0, p, unit(0))
                    pe.wait_ge(sem("moe_selT"), p + 1)
                    pe.wait_ge(sem("moe_acc"), p * 4 + 1)
                    pe.wait_ge(sem("moe_y"), p + 1)
                    step(0, p, unit(0), unit(1), first=True)
                    with pe.Fori(0, H - 1) as i:
                        step(1, p, unit(1, i), unit(2, i))
                        step(0, p, unit(2, i), unit(3, i))
                    gather(p + 1)
                    turn_hidden(1, unit(EXPERT_UNITS - 1))
                    down_rows(1, unit(EXPERT_UNITS - 1), final=True)
                    pe.wait_ge(sem("moe_xg"), p + 2)
                    pe.wait_ge(sem("moe_y"), p + 2)
                    for b in range(4):
                        for h in range(2):
                            m = 2 * b + h
                            last = mm(bk([2, 3, 6, 7][b], 2, TOK)[:, h, :], ysb[:, P * m:P * m + P], selT,
                                      start=True, stop=True)
                        last.then_inc(sem("moe_back"), 1)
                    turn_selection()

            for l in range(L):
                project(l, FIRST)
                attention(l)
                rwkv_inputs(l)
                for st in range(2):
                    rwkv_stream(l, st)
                rwkv_norm(l)
                gla(l)
                project(l, GATES)
                merge(l)
                layer_norm(2 * l)
                dense_mixer() if l == 0 else expert_mixer()
                layer_norm(2 * l + 1)

        @block.scalar
        def _(act):
            af = nc.scalar.activation
            steps = [0]

            def chained(ins):
                steps[0] += 1
                ins.then_inc(sem("act_chain"), 1)
                act.wait_ge(sem("act_chain"), steps[0])

            act.wait_ge(sem("params_in"), 10 * 16)
            af(cS[:], cT[:], ACT.Sigmoid).then_inc(sem("sig_c"), 1)
            def ada_row(n):
                act.wait_ge(sem("ada_used") if n < ADA_FIRST else sem("tile_used"),
                            n + 1 if n < ADA_FIRST else tile_number(0, f"ada{n}"))
                af(rowbuf[:, n % 2, :], ada_rows(bank[0], n), ACT.Copy)\
                    .then_inc(sem("ada_row"), 1)

            for n in range(ADA_FIRST):
                ada_row(n)
            early = [ADA_FIRST]
            roots = [0]

            def square_root(buf):
                roots[0] += 1
                act.wait_ge(sem("root_in"), roots[0])
                af(buf, buf, ACT.Sqrt).then_inc(sem("root_out"), 1)

            def project(l, names):
                for name in names:
                    if EVAC[name] != "act" and name != "cog":
                        continue
                    act.wait_ge(sem("tile_used"), tile_number(l, name))
                    b = bk(PROJ.index(name) % 2, 2, TOK)
                    done = sem("ev_act")
                    if name == "decay_rate":
                        af(tanhT[:], b[:, 0, :], ACT.Tanh)
                        af(aaT[:], b[:, 1, :], ACT.Copy).then_inc(done, 1)
                    elif name == "gate_gla":
                        af(sgaT[:], b[:, 0, :], ACT.Sigmoid)
                        af(glaT[:], b[0:32, 1, :], ACT.Copy).then_inc(done, 1)
                    elif name == "cog":
                        af(ogs[:], b, ACT.Sigmoid).then_inc(sem("sig_og"), 1)
                    elif name in GATES:
                        i = GATES.index(name)
                        af(sg[:, 2 * i:2 * i + 2, :], b, ACT.Sigmoid).then_inc(done, 1)
                    else:
                        dst = {"br": rT, "bv": vT, "cv": cv}[name]
                        af(dst[:], b, ACT.Copy).then_inc(done, 1)

            def attention(l):
                act.wait_ge(sem("max_ready"), l + 1)
                for h in range(8):
                    j, g = h // 2, h % 2
                    af(pP[:, h, :], bk(2 + j // 2, 4, P)[:, 2 * (j % 2) + g, :], ACT.Exp, bias=mneg[:, h:h + 1],
                       scale=0.125, accum_out=den[:, h:h + 1])
                    af(pL[:, h, :], bk(4 + j, 2, 256)[:, g, :], ACT.Exp, bias=mneg[:, 8 + h:9 + h],
                       scale=0.125, accum_out=den[:, 8 + h:9 + h])
                af(esink, esink, ACT.Exp).then_inc(sem("probs_exp"), 1)
                act.wait_ge(sem("probsT_done"), l + 1)
                for b, n in [(7, 12), (2, 16), (3, 20)]:
                    last = af(pT[:, n:n + 4, :], bk(b, 4, P), ACT.Copy)
                last.then_inc(sem("probsT_act"), 1)

            def rwkv(l):
                act.wait_ge(sem("rw_logits"), l + 1)
                for st in range(2):
                    af(sigz[:, st, :], bank[2 + st][:, :], ACT.Sigmoid)
                for d in range(2):
                    for c in range(2):
                        af(aT[:, d, c, :], bk(4 + d, 2, TOK)[:, c, :], ACT.Sigmoid,
                           bias=rv[:, l, 2 * d + c:2 * d + c + 1])
                af(gT, bk(6, 2, TOK), ACT.Copy).then_inc(sem("rw_act"), 1)
                square_root(rtmp2)
                for st in range(2):
                    k = 2 * l + st + 1
                    act.wait_ge(sem("cum_done"), k)
                    if st == 1:
                        af(ecr, bank[4][:, 0:4], ACT.Exp).then_inc(sem("center_ready"), 1)
                    for d in range(2):
                        b = bk(2 + d, 2, 2, P)
                        af(Ep[d], b, ACT.Exp)
                        af(En[d], b[:, :, 0, :], ACT.Exp, scale=-1.0).then_inc(sem("decays_ready"), 1)
                    if l == 0:
                        for n in range(early[0], early[0] + 3 * LEVELS):
                            ada_row(n)
                        early[0] += 3 * LEVELS
                    for d in range(2):
                        act.wait_ge(sem("x_done"), 2 * (k - 1) + d + 1)
                        af(Xs[d], bank[2 + d][:, 0:256], ACT.Copy).then_inc(sem("xs_ready"), 1)
                    for d in range(2):
                        act.wait_ge(sem("u_done"), 2 * (k - 1) + d + 1)
                        af(nU[d], bank[4 + d][:, 0:256], ACT.Copy, scale=-1.0).then_inc(sem("nu_ready"), 1)
                    act.wait_ge(sem("y_done"), k)
                    af(yT[:, :, P * st:P * st + P], bk(6, 2, P), ACT.Copy).then_inc(sem("yT_ready"), 1)
                square_root(rtmp2)

            def gla(l):
                act.wait_ge(sem("gabs_ready"), l + 1)
                chained(af(glog, glog, ACT.Exp))
                af(glog, glog, ACT.Ln, bias=1.0).then_inc(sem("gln_ready"), 1)
                act.wait_ge(sem("gcum_done"), l + 1)
                af(ecg, bank[4][:, 0:2], ACT.Exp)
                af(EG, bk(3, 4, P), ACT.Exp)
                af(EGn, bk(3, 4, P), ACT.Exp, scale=-1.0).then_inc(sem("gdecay_ready"), 1)

            def unit_sigmoid(kind):
                def unit(e, r, u, par, first=False):
                    act.wait_ge(sem(f"{kind}_gu_used"), u + 1)
                    if not first:
                        act.wait_ge(sem(f"{kind}_hid"), u - 1)
                    af(sgt[par], bk(2 * par, 2, TOK), ACT.Sigmoid).then_inc(sem(f"{kind}_sig"), 1)
                return unit

            def experts():
                act.wait_ge(sem("gap_ready"), 1)
                af(gap[:, 0, :], gap[:, 0, :], ACT.Exp).then_inc(sem("gap_exp"), 1)
                act.wait_ge(sem("hN_done"), 1)
                for b in range(4):
                    last = af(hN[:, b // 2, 512 * (b % 2):512 * (b % 2) + 512], bank[4 + b][:, :], ACT.Copy)
                last.then_inc(sem("hN_ready"), 1)
                act.sem_inc(sem("moe_hidT"), 2)

                def take_gathered(p):
                    act.wait_ge(sem("moe_xg_done"), p + 1)
                    for b in range(2):
                        last = af(xgT[:, 4 * b:4 * b + 4, :], bk(6 + b, 4, P), ACT.Copy)
                    last.then_inc(sem("moe_xg"), 1)

                def take_selection(p):
                    act.wait_ge(sem("moe_selT_done"), p + 1)
                    af(selT, bank[1][:, 0:TOK], ACT.Copy).then_inc(sem("moe_selT"), 1)

                def sigmoid(par, u):
                    act.wait_ge(sem("moe_gu_used"), u + 3)
                    act.wait_ge(sem("moe_hid"), u + 1)
                    af(msig[par], bank[par][:, 0:TW], ACT.Sigmoid).then_inc(sem("moe_sig"), 1)

                def take_hidden(par, u):
                    act.wait_ge(sem("moe_turned"), u + 1)
                    act.wait_ge(sem("moe_d_used"), u + 1)
                    af(mhidT[par], bank[2 + par][:, 0:TW], ACT.Copy).then_inc(sem("moe_hidT"), 1)

                take_gathered(0)
                take_selection(0)
                n_pass = second_passes(act) + NE
                with act.Fori(0, n_pass) as p:
                    u = p * EXPERT_UNITS
                    sigmoid(0, u)
                    take_hidden(0, u)
                    sigmoid(1, u + 1)
                    with act.Fori(0, EXPERT_UNITS // 2 - 1) as i:
                        for k in (1, 2):
                            take_hidden(k % 2, u + i * 2 + k)
                            sigmoid(1 - k % 2, u + i * 2 + (k + 1))
                    take_gathered(p + 1)
                    take_hidden(1, u + (EXPERT_UNITS - 1))
                    take_selection(p + 1)

            for l in range(L):
                project(l, FIRST)
                attention(l)
                rwkv(l)
                gla(l)
                square_root(gtm)
                project(l, GATES)
                square_root(rstd)
                if l == 0:
                    dense_loop(act, unit_sigmoid("dense"))
                else:
                    experts()
                square_root(rstd)

        @block.vector
        def _(dve):
            v = nc.vector
            steps = [0]

            def chained(ins):
                steps[0] += 1
                ins.then_inc(sem("dve_chain"), 1)
                dve.wait_ge(sem("dve_chain"), steps[0])

            mul = lambda o, a, b: v.tensor_tensor(o, a, b, ALU.mult)
            add = lambda o, a, b: v.tensor_tensor(o, a, b, ALU.add)
            sub = lambda o, a, b: v.tensor_tensor(o, a, b, ALU.subtract)

            def scaled(o, a, s1, s2=None):
                return v.tensor_scalar(o, a, s1, s2, ALU.mult, ALU.add) if s2 is not None else \
                    v.tensor_scalar(o, a, s1, None, ALU.mult)

            def over(a, n, axis=1):
                x = a.unsqueeze(axis)
                shape = list(x.shape)
                shape[axis] = n
                return x.to_broadcast(shape)

            roots = [0]

            def inverse_root(buf, source, eps):
                roots[0] += 1
                v.tensor_scalar(buf, source, eps, None, ALU.add).then_inc(sem("root_in"), 1)
                dve.wait_ge(sem("root_out"), roots[0])
                chained(v.reciprocal(buf, buf))

            dve.wait_ge(sem("params_in"), 10 * 16)
            v.memset(zeros[:], 0.0)
            for l in range(L):
                v.tensor_scalar(omk[:, l, :], rv[:, l, 6:8], -1.0, 1.0, ALU.mult, ALU.add)
            dve.wait_ge(sem("sig_c"), 1)
            mul(cS[:], cS[:], cT[:]).then_inc(sem("silu_c"), 1)

            def take_modulations(l, c0, c1, at):
                chained(add(mod[:, l, c0:c1, :], shaped(bank[1][:, at:at + 2 * (c1 - c0)], (c1 - c0, 2)),
                            over(bada[:, l, c0:c1], 2, 2)))
                for a in (8, 32):
                    if c0 <= a < c1:
                        chained(v.tensor_scalar(mod[:, l, a:a + 8, :], mod[:, l, a:a + 8, :], 1.0, None, ALU.add))

            dve.wait_ge(sem("ada_turned"), ADA_FIRST)
            take_modulations(0, 0, 24, 0)
            v.memset(zeros[:, 0:1], 0.0).then_inc(sem("mod_read"), 1)

            def modulate(l, sub_layer):
                for m in range(KC):
                    for st in range(2):
                        sh, sc = mod[:, l, 24 * sub_layer + m, st:st + 1], mod[:, l, 24 * sub_layer + 8 + m, st:st + 1]
                        last = scaled(hT[:, m, P * st:P * st + P], xT[:, m, P * st:P * st + P], sc, sh)
                last.then_inc(sem("h_ready"), 1)

            def project(l):
                for name in FIRST:
                    if EVAC[name] != "dve":
                        continue
                    dve.wait_ge(sem("tile_used"), tile_number(l, name))
                    i = PROJ.index(name) % 2
                    b = bk(i, 2, TOK)
                    if name in ("q0", "q1"):
                        j = 2 * int(name[1])
                        last = v.tensor_copy(qT[:, j:j + 2, :], b)
                    elif name == "kv":
                        if l > 0:
                            dve.wait_ge(sem("kept"), 160 * l)
                        v.tensor_copy(kT[:], b[:, 0, :])
                        last = v.tensor_copy(av[:], bk(i, 4, P)[:, 2:4, :])
                    elif name == "bk":
                        last = v.tensor_copy(kfT[:], b)
                    elif name == "cqk":
                        v.tensor_copy(cqT[:], b[:, 0, :])
                        last = v.tensor_copy(ckT[:], b[:, 1, :])
                    else:
                        dve.wait_ge(sem("sig_og"), l + 1)
                        last = mul(ogs[:], ogs[:], b)
                    last.then_inc(sem("ev_dve"), 1)
                dve.wait_ge(sem("ev_dve"), EV_DVE * (l + 1))

            def attention(l):
                dve.wait_ge(sem("rot_done"), l + 1)
                dve.wait_ge(sem("layer_in"), 128 * (l + 1))
                mul(atmp, bk(2, 4, P), over(C("sin"), 4))
                mul(qL, qT[:, :, P:TOK], over(C("cos"), 4))
                mul(krot, bank[3][:, 0:P], C("sin"))
                chained(mul(rtmp_k, kT[:, P:TOK], C("cos")))
                add(qL, qL, atmp)
                chained(add(krot, krot, rtmp_k))
                hm = C("hm64")
                for g in range(2):
                    scaled(kxL[:, g, 0:P], krot, hm[:, g:g + 1])
                    scaled(kxL[:, g, P:256], kcT[:, :], hm[:, g:g + 1])
                    last = scaled(kxP[:, g, :], kT[:, 0:P], hm[:, g:g + 1])
                last.then_inc(sem("attn_in"), 1)
                dve.wait_ge(sem("scores_done"), l + 1)
                for j in range(4):
                    v.tensor_reduce(mneg[:, 8 + 2 * j:10 + 2 * j], bk(4 + j, 2, 256), AX.X, ALU.max)
                for b in range(2):
                    last = v.tensor_reduce(mneg[:, 4 * b:4 * b + 4], bk(2 + b, 4, P), AX.X, ALU.max)
                chained(last)
                for st in range(2):
                    last = v.scalar_tensor_tensor(mneg[:, 8 * st:8 * st + 8], mneg[:, 8 * st:8 * st + 8], 0.125,
                                                  sinkB[:, l, :], ALU.mult, ALU.max)
                chained(last)
                for st in range(2):
                    last = sub(esink[:, 8 * st:8 * st + 8], sinkB[:, l, :], mneg[:, 8 * st:8 * st + 8])
                chained(last)
                scaled(mneg, mneg, -1.0).then_inc(sem("max_ready"), 1)
                dve.wait_ge(sem("probs_exp"), l + 1)
                chained(add(den, den, esink))
                chained(v.reciprocal(den, den))
                mul(pP, pP, over(den[:, 0:8], P, 2))
                mul(pL, pL, over(den[:, 8:16], 256, 2)).then_inc(sem("probs_ready"), 1)
                dve.wait_ge(sem("probsT_done"), l + 1)
                for b in range(3):
                    last = v.tensor_copy(pT[:, 4 * b:4 * b + 4, :], bk(4 + b, 4, P))
                last.then_inc(sem("probsT_dve"), 1)
                dve.wait_ge(sem("attn_done"), l + 1)
                v.tensor_copy(oaT[:, 0:2, :], bk(2, 2, TOK))
                v.tensor_copy(oaT[:, 2:4, :], bk(3, 2, TOK)).then_inc(sem("attn_out"), 1)

            def rwkv_inputs(l):
                evacuated(dve, l, "bv")
                par = lambda i: rv[:, l, i:i + 1]
                for c in range(2):
                    last = scaled(kapT[:, c, :], kfT[:, c, :], par(4 + c))
                chained(last)
                mul(rtmp, kapT, kapT).then_inc(sem("kk_sq"), 1)
                dve.wait_ge(sem("kk_norm"), l + 1)
                inverse_root(rtmp2, bk(7, 2, TOK), 1e-12)
                chained(mul(kapT, kapT, rtmp2))
                dve.wait_ge(sem("rw_act"), l + 1)
                for d in range(2):
                    mul(akT[:, d], aT[:, d], kapT)
                    for c in range(2):
                        last = scaled(ktT[:, d, c, :], aT[:, d, c, :], par(6 + c), omk[:, l, c:c + 1])
                chained(last)
                for d in range(2):
                    last = mul(ktT[:, d], ktT[:, d], kfT[:])
                chained(last)
                chained(add(rtmp2, ktT[:, 0], ktT[:, 1]))
                chained(mul(rtmp2, rtmp2, rT[:]))
                for c in range(2):
                    last = scaled(rtmp2[:, c, :], rtmp2[:, c, :], par(8 + c))
                last.then_inc(sem("bonus_in"), 1)
                dve.wait_ge(sem("vn_done"), l + 1)
                v.tensor_copy(Vn, bk(2, 2, TOK))
                dve.wait_ge(sem("bonus_sum"), l + 1)
                mul(bonT, bk(3, 2, TOK), vT[:]).then_inc(sem("bonus_out"), 1)

            def rwkv_stream(l, st):
                k = 2 * l + st + 1
                cols = slice(P * st, P * st + P)
                hm = C("hm64")
                if st == 1:
                    dve.wait_ge(sem("center_ready"), l + 1)
                    for e in range(4):
                        scaled(s0c[:, e, :], s0r[:, e, :], ecr[:, e:e + 1])
                for d in range(2):
                    dve.wait_ge(sem("decays_ready"), 2 * (k - 1) + d + 1)
                    for i in range(2):
                        v.scalar_tensor_tensor(KR[d][:, :, 0, i, :], kapT[:, :, cols], hm[:, i:i + 1],
                                               Ep[d][:, :, 1, :], ALU.mult, ALU.mult)
                        v.scalar_tensor_tensor(KR[d][:, :, 1, i, :], rT[:, :, cols], hm[:, i:i + 1],
                                               Ep[d][:, :, 0, :], ALU.mult, ALU.mult)
                    mul(Bc[d], akT[:, d, :, cols], En[d])
                    end = P - 1 if d == 0 else 0
                    v.tensor_copy(elast[:, 2 * d:2 * d + 2], Ep[d][:, :, 0, end])
                    mul(KcR[d], ktT[:, d, :, cols], En[d]).then_inc(sem("khat_ready"), 1)
                for d in range(2):
                    dve.wait_ge(sem("mats_done"), 2 * (k - 1) + d + 1)
                    mask = C(f"mask{d}").rearrange("p (x i t) -> p x i t", x=2, i=2)
                    for c in range(2):
                        mul(MTQ[d][:, c], bk(2 + c, 2, 2, P), mask)
                    mul(Tm[d], bk(6, 4, P), over(C(f"lv0{d}"), 4))
                    for c in range(2):
                        last = mul(AKQ[d][:, c], bk(4 + c, 2, 2, P), mask)
                    chained(last)
                    for c in range(2):
                        mul(TmT[d][:, 2 * c:2 * c + 2, :], MTQ[d][:, c, 0], over(C(f"lv0T{d}"), 2))
                    chained(add(Tm[d], Tm[d], over(C("ident"), 4)))
                    add(TmT[d], TmT[d], over(C("ident"), 4)).then_inc(sem("mats_read"), 1)
                for j in range(1, LEVELS + 1):
                    n = (k - 1) * LEVELS + j
                    for d in range(2):
                        dve.wait_ge(sem(f"inv_MT{d}"), n)
                        mul(P1[d], bk(2 + 3 * d, 4, P), over(C(f"lv{j}"), 4)).then_inc(sem(f"inv_P{d}"), 1)
                    for d in range(2):
                        dve.wait_ge(sem(f"inv_TP{d}"), n)
                        if j < LEVELS:
                            sub(Tm[d], Tm[d], bk(3 + 3 * d, 4, P))
                        sub(TmT[d], TmT[d], bk(4 + 3 * d, 4, P)).then_inc(sem(f"inv_T{d}"), 1)
                if st == 0:
                    dve.wait_ge(sem("x_done"), 2 * k)
                    for d in range(2):
                        for c in range(2):
                            e = 2 * d + c
                            scaled(K2T[:, 0, e, :], KcR[d][:, c, :], elast[:, e:e + 1])
                            last = scaled(K2T[:, 1, e, :], Bc[d][:, c, :], elast[:, e:e + 1])
                    last.then_inc(sem("k2_ready"), 1)
                    dve.wait_ge(sem("k2T_done"), l + 1)
                    v.tensor_copy(K2n[0], bk(2, 4, P))
                    v.tensor_copy(K2n[1], bk(3, 4, P)).then_inc(sem("k2n_ready"), 1)
                    dve.wait_ge(sem("fs_done"), l + 1)
                    v.tensor_copy(fstate[:], bk(7, 2, 2, P)).then_inc(sem("fstate_ready"), 1)

            def rwkv_norm(l):
                dve.wait_ge(sem("gn_mean"), l + 1)
                chained(sub(yT, yT, bk(2, 2, TOK)))
                mul(rtmp, yT, yT).then_inc(sem("gn_sq"), 1)
                dve.wait_ge(sem("gn_var"), l + 1)
                inverse_root(rtmp2, bk(3, 2, TOK), GN_EPS)
                chained(mul(yT, yT, rtmp2))
                for c in range(2):
                    last = scaled(yT[:, c, :], yT[:, c, :], rv[:, l, 10 + c:11 + c], rv[:, l, 12 + c:13 + c])
                chained(last)
                chained(add(yT, yT, bonT))
                mul(obT[:], yT, gT).then_inc(sem("rwkv_out"), 1)

            def gla(l):
                dve.wait_ge(sem("gl_done"), l + 1)
                v.tensor_scalar(gtm, bank[2][:, :], 0.0, None, ALU.min)
                chained(v.tensor_scalar(glog, bank[2][:, :], 0.0, None, ALU.max))
                sub(glog, gtm, glog).then_inc(sem("gabs_ready"), 1)
                dve.wait_ge(sem("gln_ready"), l + 1)
                sub(glog, gtm, glog).then_inc(sem("glog_ready"), 1)
                dve.wait_ge(sem("gdecay_ready"), l + 1)
                for st in range(2):
                    for d in range(2):
                        x = 2 * st + d
                        cols = slice(P * st, P * st + P)
                        mul(KcG[:, x, :], ckT[:, cols], EGn[:, x, :])
                        chained(v.scalar_tensor_tensor(Qh, cqT[:, cols], 32.0 ** -0.5, EG[:, x, :],
                                                       ALU.mult, ALU.mult))
                        for h in range(4):
                            last = scaled(Qx[:, x, h, :], Qh, C("hm32")[:, h:h + 1])
                        chained(last)
                for d in range(2):
                    end = P - 1 if d == 0 else 0
                    scaled(s0gc[:, d, :], s0g[:, d, :], ecg[:, d:d + 1])
                    last = scaled(K2g[:, d, :], KcG[:, d, :], EG[:, d, end:end + 1])
                last.then_inc(sem("gq_ready"), 1)
                dve.wait_ge(sem("att_done"), l + 1)
                for x in range(4):
                    last = mul(attT[:, x], bk(4 + x, 4, P), over(C(f"mask{x % 2}")[:, 256:384], 4))
                last.then_inc(sem("att_ready"), 1)
                dve.wait_ge(sem("go_done"), l + 1)
                chained(v.tensor_copy(oc, bank[2][:, :]))
                mul(gsq, oc, oc).then_inc(sem("gsq_ready"), 1)
                dve.wait_ge(sem("k2g_done"), l + 1)
                v.tensor_copy(K2gn, bk(3, 2, P)).then_inc(sem("k2g_ready"), 1)
                dve.wait_ge(sem("gs_done"), l + 1)
                v.tensor_copy(gstate[:], bk(4, 2, 256)).then_inc(sem("gstate_ready"), 1)
                dve.wait_ge(sem("gms_done"), l + 1)
                inverse_root(gtm, bank[5][:, :], LN_EPS)
                chained(mul(oc, oc, gtm))
                v.scalar_tensor_tensor(ocT[:], shaped(oc, (2, TOK)), rv[:, l, 14:15], ogs[:], ALU.mult, ALU.mult)\
                    .then_inc(sem("gla_out"), 1)

            def merge(l):
                evacuated(dve, l, "gate11")
                for br, tile in enumerate(["up_a1", "up_b", "up_c"]):
                    dve.wait_ge(sem("tile_used"), tile_number(l, tile))
                    if br > 0:
                        dve.wait_ge(sem("up_read"), 3 * l + br)
                    for b in range(4):
                        ps = bk((4 if br == 1 else 0) + b, 2, TOK)
                        gate = sg[:, 8 * br + 2 * b:8 * br + 2 * b + 2, :]
                        last = mul((merged if br == 0 else mtmp)[:, 2 * b:2 * b + 2, :], ps, gate)
                    if br > 0:
                        chained(last)
                        last = add(merged, merged, mtmp)
                    last.then_inc(sem("up_read"), 1)
                chained(v.tensor_scalar(xT[:], xT[:], ALPHA, None, ALU.mult))

            def layer_norm(n, last_norm=False):
                l, half = n // 2, n % 2

                def f(m, cols):
                    return accT[:, m, cols] if last_norm else bk(4 + m // 2, 2, TOK)[:, m % 2, cols]

                for m in range(KC):
                    for st in range(2):
                        cols = slice(P * st, P * st + P)
                        last = v.scalar_tensor_tensor(yLN[:, m, cols], f(m, cols),
                                                      mod[:, l, 24 * half + 16 + m, st:st + 1], xT[:, m, cols],
                                                      ALU.mult, ALU.add)
                last.then_inc(sem("ln_y"), 1)
                dve.wait_ge(sem("ln_mean"), n + 1)
                chained(sub(yLN, yLN, over(bank[0][:, 0:TOK], KC)))
                mul(mtmp, yLN, yLN).then_inc(sem("ln_sq"), 1)
                dve.wait_ge(sem("ln_var"), n + 1)
                inverse_root(rstd, bank[1][:, 0:TOK], LN_EPS)
                chained(mul(yLN, yLN, over(rstd, KC)))
                for m in range(KC):
                    last = scaled(xT[:, m, :], yLN[:, m, :], lnp[:, l, 2 * half, m:m + 1],
                                  lnp[:, l, 2 * half + 1, m:m + 1])
                if last_norm:
                    last.then_inc(sem("y_ready"), 1)
                else:
                    chained(last)

            def unit_hidden(kind):
                def unit(e, r, u, par, first=False):
                    dve.wait_ge(sem(f"{kind}_sig"), u + 1)
                    if not first:
                        dve.wait_ge(sem(f"{kind}_d_used"), u - 1)
                    mul(sgt[par], sgt[par], bk(2 * par, 2, TOK)).then_inc(sem("dense_step"), 1)
                    dve.wait_ge(sem("dense_step"), u + 1)
                    mul(hid[par], sgt[par], bk(2 * par + 1, 2, TOK)).then_inc(sem(f"{kind}_hid"), 1)
                return unit

            def route():
                dve.wait_ge(sem("logits_done"), 1)
                for st in range(2):
                    last = v.tensor_copy(lg[:, st, :], bank[st][:, 0:NE])
                chained(last)
                for st in range(2):
                    last = v.max(top8[:, st, :], lg[:, st, :])
                chained(last)
                for st in range(2):
                    last = v.max_index(idxu[:, st, :], top8[:, st, :], lg[:, st, :])
                sub(gap[:, 0, :], top8[:, :, 1], top8[:, :, 0]).then_inc(sem("gap_ready"), 1)
                dve.wait_ge(sem("gap_ready"), 1)
                chained(v.tensor_copy(idxf, idxu[:]))
                for st in range(2):
                    v.tensor_scalar(lg[:, st, :], C("iota8"), idxf[:, st, 0:1], None, ALU.is_equal)
                    last = v.tensor_scalar(pick2[:, st, :], C("iota8"), idxf[:, st, 1:2], None, ALU.is_equal)
                chained(last)
                add(member, lg, pick2).then_inc(sem("member_ready"), 1)
                dve.wait_ge(sem("gap_exp"), 1)
                chained(v.tensor_scalar(gap[:, 1, :], gap[:, 0, :], 1.0, None, ALU.add))
                chained(v.reciprocal(gap[:, 1, :], gap[:, 1, :]))
                chained(mul(gap[:, 0, :], gap[:, 0, :], gap[:, 1, :]))
                chained(mul(gts, lg, over_last(gap[:, 1, :])))
                chained(mul(pick2, pick2, over_last(gap[:, 0, :])))
                chained(add(gts, gts, pick2))
                v.memset(ptab, -1.0)
                chained(v.memset(gtab, 0.0))
                dve.wait_ge(sem("slots_done"), 1)
                slots = bk(2, 3, NE)
                v.scalar_tensor_tensor(slotno, slots[:, 0:2, :], 1.0, member, ALU.add, ALU.mult)
                chained(v.tensor_scalar(crowded, slots[:, 2, :], float(P), None, ALU.is_gt))
                v.tensor_scalar(ptab[:, :, 0:NE], slotno, -1.0, None, ALU.add)
                chained(v.tensor_copy(gtab[:, :, 0:NE], gts))
                chained(v.memset(rank, 0.0))
                for e in range(1, NE):
                    chained(add(rank[:, e:e + 1], rank[:, e - 1:e], crowded[:, e - 1:e]))
                chained(v.tensor_reduce(evf[:, 0:1], crowded, AX.X, ALU.add))
                chained(v.scalar_tensor_tensor(slotno, member, -float(P), slotno, ALU.mult, ALU.add))
                for j in range(OVER):
                    chained(v.scalar_tensor_tensor(onehot, rank, float(j), crowded, ALU.is_equal, ALU.mult))
                    for table, source in ((ptab, slotno), (gtab, gts)):
                        chained(mul(rtab, source, onehot.unsqueeze(1).to_broadcast([P, 2, NE])))
                        chained(v.tensor_reduce(table[:, :, NE + j], rtab, AX.X, ALU.add))
                    chained(v.tensor_scalar(ptab[:, :, NE + j], ptab[:, :, NE + j], -1.0, None, ALU.add))
                    chained(mul(rtab[:, 0, :], C("iota8"), onehot))
                    chained(v.tensor_reduce(evf[:, j + 1:j + 2], rtab[:, 0, :], AX.X, ALU.add))
                v.tensor_copy(passes_i[:], evf).then_inc(sem("passes_known"), 1)

            def over_last(a):
                return a.unsqueeze(2).to_broadcast([P, 2, NE])

            def experts():
                v.memset(accT, 0.0).then_inc(sem("moe_acc"), 1)
                dve.sem_inc(sem("moe_hid"), 2)
                dve.sem_inc(sem("moe_y"), 1)

                def select(p):
                    place = ptab[:, :, bass.ds(p, 1)].to_broadcast([P, 2, P])
                    gate = gtab[:, :, bass.ds(p, 1)].to_broadcast([P, 2, P])
                    v.tensor_tensor(sel, over_streams(C("iota")), place, ALU.is_equal).then_inc(sem("moe_match"), 1)
                    dve.wait_ge(sem("moe_match"), p + 1)
                    mul(selg, sel, gate).then_inc(sem("moe_sel"), 1)

                def over_streams(a):
                    return a.unsqueeze(1).to_broadcast([P, 2, P])

                def hidden(par, u):
                    dve.wait_ge(sem("moe_sig"), u + 1)
                    dve.wait_ge(sem("moe_hidT"), u + 1)
                    mul(msig[par], msig[par], bank[par][:, 0:TW]).then_inc(sem("moe_silu"), 1)
                    dve.wait_ge(sem("moe_silu"), u + 1)
                    mul(mhid[par], msig[par], bank[par][:, TW:2 * TW]).then_inc(sem("moe_hid"), 1)

                select(0)
                n_pass = second_passes(dve) + NE
                with dve.Fori(0, n_pass) as p:
                    dve.wait_ge(sem("moe_selT_done"), p + 1)
                    select(p + 1)
                    with dve.Fori(0, EXPERT_UNITS // 2) as i:
                        for par in range(2):
                            hidden(par, p * EXPERT_UNITS + i * 2 + par)
                    dve.wait_ge(sem("moe_d_used"), (p + 1) * EXPERT_UNITS + 2)
                    v.tensor_copy(ysb[:, 0:512], bank[4][:, :])
                    v.tensor_copy(ysb[:, 512:1024], bank[5][:, :]).then_inc(sem("moe_y"), 1)
                    dve.wait_ge(sem("moe_acc"), p * 4 + 1)
                    for b in range(4):
                        dve.wait_ge(sem("moe_back"), p * 4 + (b + 1))
                        add(accT[:, 2 * b:2 * b + 2, :], accT[:, 2 * b:2 * b + 2, :], bk([2, 3, 6, 7][b], 2, TOK))\
                            .then_inc(sem("moe_acc"), 1)
                dve.wait_ge(sem("moe_acc"), n_pass * 4 + 1)
                dve.wait_ge(sem("moe_selT"), n_pass + 1)

            for l in range(L):
                modulate(l, 0)
                project(l)
                attention(l)
                rwkv_inputs(l)
                for st in range(2):
                    rwkv_stream(l, st)
                if l == 0:
                    dve.wait_ge(sem("ada_turned"), L * ADA_TILES)
                    take_modulations(0, 24, 48, 0)
                    take_modulations(1, 0, 48, 48)
                    v.memset(zeros[:, 0:1], 0.0).then_inc(sem("mod_read"), 1)
                rwkv_norm(l)
                gla(l)
                merge(l)
                dve.wait_ge(sem("tile_used"), tile_number(l, "out3"))
                layer_norm(2 * l)
                modulate(l, 1)
                dve.wait_ge(sem("h_ready"), 2 * l + 2)
                v.tensor_scalar(xT[:], xT[:], ALPHA, None, ALU.mult)
                if l == 0:
                    dense_loop(dve, unit_hidden("dense"))
                    dve.wait_ge(sem("dense_d_used"), DENSE_UNITS)
                    layer_norm(1)
                else:
                    route()
                    experts()
                    layer_norm(3, last_norm=True)


def lay_out(x):
    def chunks(a):
        a = np.asarray(a)
        a = a.reshape(a.shape[:-1] + (a.shape[-1] // P, P))
        return np.ascontiguousarray(np.moveaxis(a, -1, 0))

    g = {}
    xs = np.concatenate([x["x_prompt"][0], x["x_sample"][0]], 0)
    g["xT"] = np.ascontiguousarray(chunks(xs).transpose(0, 2, 1))
    cc = np.stack([x["c_ctx"], x["c"][0]], 0)
    g["cT"] = np.ascontiguousarray(chunks(cc).transpose(0, 2, 1))
    g["bada"] = chunks(x["b_ada"])
    g["lnp"] = chunks(np.stack([x["ln1_g"], x["ln1_b"], x["ln2_g"], x["ln2_b"]], 1))
    rows = [chunks(x["rwkv_a0"]).reshape(P, L, 4)]
    for n in ["rwkv_k_k", "rwkv_k_a"]:
        rows.append(chunks(x[n]))
    rows.append(chunks(x["rwkv_r_k"].reshape(L, 256)))
    for n in ["rwkv_ln_g", "rwkv_ln_b"]:
        rows.append(chunks(x[n]))
    rows.append(chunks(np.concatenate([x["gla_norm_g"], x["gla_norm_g"]], 1)))
    g["rv"] = np.ascontiguousarray(np.concatenate(rows, 2))
    g["w0row"] = np.ascontiguousarray(x["rwkv_w0"].reshape(1, L, 512))
    g["glbrow"] = np.ascontiguousarray(x["gla_gate_bias"].reshape(1, L, 256))
    sink = x["attn_sink"].reshape(L, 2, 4).transpose(0, 2, 1).reshape(1, L, 8)
    g["sinkB"] = np.ascontiguousarray(np.broadcast_to(sink, (P, L, 8)))

    def on_diagonal(a):
        _, nd, r, n = a.shape
        out = np.zeros((nd * r, L, nd * n), a.dtype)
        for d in range(nd):
            out[d * r:(d + 1) * r, :, d * n:(d + 1) * n] = a[:, d].transpose(1, 0, 2)
        return out

    g["wbB"] = on_diagonal(x["rwkv_w_b"])
    g["abB"] = on_diagonal(x["rwkv_a_b"])
    g["glb"] = on_diagonal(x["gla_gate_b"])
    g["gbw"] = np.ascontiguousarray(x["rwkv_g_b"].transpose(1, 0, 2))
    s = x["state_rwkv"][0].reshape(L, 2, 2, 2, 64, 64)
    g["s0r"] = np.ascontiguousarray(s.transpose(3, 5, 0, 1, 2, 4)).reshape(P, L, 4, 64)
    g["s0g"] = np.ascontiguousarray(x["state_gla"][0].transpose(2, 3, 0, 1, 4)).reshape(P, L, 2, 64)
    g["kcT"] = np.ascontiguousarray(x["cache_attn_k"][0].transpose(2, 3, 0, 1)).reshape(P, L, P)
    g["vc"] = np.ascontiguousarray(x["cache_attn_v"][0].transpose(1, 0, 2, 3)).reshape(P, L, P)
    g["router"] = np.ascontiguousarray(x["moe_router"][0].reshape(KC, P, NE).transpose(1, 0, 2))
    g["cst"] = build_constants()
    for n in ["w_ada", "w_in", "rwkv_w_a", "rwkv_a_a", "rwkv_g_a", "gla_gate_a", "w_up_a", "w_up_b", "w_up_c",
              "w_out", "ffn_w_gate", "ffn_w_up", "ffn_w_down", "moe_w_gate", "moe_w_up", "moe_w_down"]:
        g[n] = np.ascontiguousarray(x[n])
    return g


OUTS = {"yT": (P, KC, TOK), "kT": (L, P, P), "v": (L, P, P), "rwkv": (1, L, 2, 4, 64, 64), "gla": (1, L, 2, 4, 32, 64)}


def kernel(**inputs):
    import concourse.bacc as bacc
    from concourse.bass_utils import run_bass_kernel_spmd

    x = {n: np.asarray(a) for n, a in inputs.items()}
    arrays = lay_out(x)
    nc = bacc.Bacc("TRN2", target_bir_lowering=False, num_devices=1)
    ins = {n: nc.dram_tensor(f"in_{n}", a.shape, mybir.dt.from_np(a.dtype), kind="ExternalInput").ap()
           for n, a in arrays.items()}
    outs = {n: nc.dram_tensor(f"out_{n}", s, F32, kind="ExternalOutput").ap() for n, s in OUTS.items()}
    build_program(nc, ins, outs)
    r = run_bass_kernel_spmd(nc, [{f"in_{n}": a for n, a in arrays.items()}], core_ids=[0]).results[0]
    y = r["out_yT"].transpose(2, 1, 0).reshape(TOK, D)
    k = r["out_kT"].transpose(0, 2, 1).reshape(1, L, P, 2, 64)
    val = r["out_v"].reshape(1, L, P, 2, 64)
    return (np.ascontiguousarray(y[None, 0:P]), np.ascontiguousarray(y[None, P:]), np.ascontiguousarray(k),
            val, r["out_rwkv"], r["out_gla"])
```

```python
from contextlib import ExitStack

import numpy as np

import concourse.bass as bass
from concourse import mybir

ALU = mybir.AluOpType
ACT = mybir.ActivationFunctionType
AX = mybir.AxisListType
F32 = mybir.dt.float32
U32 = mybir.dt.uint32
I32 = mybir.dt.int32

P = 128
D = 1024
KC = D // P
TOK = 2 * P
L = 2
TW = 256
RING = 6
FF = 2816
FFE = 3584
NE = 8
DENSE_UNITS = FF // TW
EXPERT_UNITS = FFE // TW
OVER = 3
LN_EPS = 1e-5
GN_EPS = 64e-5
ALPHA = (2.0 * L) ** 0.25
LEVELS = 6

FIRST = ["q0", "q1", "kv", "decay_rate", "gate_gla", "br", "bk", "bv", "cqk", "cv", "cog"]
GATES = [f"gate{i}" for i in range(12)]
W_IN = ["q0", "q1", "kv", "br", "bk", "bv", "cqk", "cv", "cog"] + GATES
PROJ = FIRST + GATES
ADA_TILES = 6 * D // TW
ADA_FIRST = ADA_TILES // 2
EARLY = [f"ada{n}" for n in range(ADA_FIRST, L * ADA_TILES)]
MIX = [FIRST + EARLY * (l == 0) + GATES + ["up_a0", "up_a1", "up_b", "up_c"] + [f"out{i}" for i in range(4)]
       for l in range(L)]
MIX_DMAS = {"q0": 4, "q1": 4, "decay_rate": 4, "gate_gla": 3, "up_a0": 2, "up_a1": 2}
MIX_TILES = [len(m) for m in MIX]
MIX_BASE = [0, MIX_TILES[0], sum(MIX_TILES)]

CST = {}


def build_constants():
    t = np.arange(P)
    row, col = t[:, None], t[None, :]
    parts = []

    def add(name, a):
        CST[name] = (sum(x.shape[1] for x in parts), a.shape[1])
        parts.append(a.astype(np.float32))

    add("ident", row == col)
    add("ones", np.ones((P, P)))
    add("mean_d", np.full((P, P), 1.0 / D))
    add("blk", row // 64 == col // 64)
    add("blkm", (row // 64 == col // 64) / 64.0)
    decay = -np.exp(-0.5)
    le, lt, ge, gt = row <= col, row < col, row >= col, row > col
    first, second = row < 64, row >= 64
    for d, (inc, exc, cen) in enumerate([(le, lt, first), (ge, gt, second)]):
        add(f"tri{d}", np.concatenate([inc * 1.0 - cen, exc * 1.0 - cen], 1) * decay)
        add(f"trig{d}", (inc * 1.0 - cen) / 16.0)
        add(f"cen{d}", cen * decay)
        add(f"ceng{d}", cen / 16.0)
        add(f"mask{d}", np.concatenate([exc, exc, inc, inc], 1))
        pair = (row // 2 == col // 2) & (row != col)
        add(f"lv0T{d}", -1.0 * (exc & pair))
        add(f"lv0{d}", -1.0 * (exc.T & pair))
    for j in range(1, LEVELS + 1):
        add(f"lv{j}", (row // 2 ** (j + 1) == col // 2 ** (j + 1)) & (row // 2 ** j != col // 2 ** j))
    inv = (10000.0 ** (-np.arange(0, 32, 2, dtype=np.float32) / 32)).astype(np.float32)
    pos = np.stack([t // 64, t % 64]).astype(np.float32)
    dim = t % 64
    ang = (pos[dim // 32][:, :] * inv[dim % 16][:, None]).astype(np.float32)
    add("cos", np.cos(ang))
    add("sin", np.sin(ang))
    same = row // 32 == col // 32
    add("rot", 1.0 * (same & (row + 16 == col)) - 1.0 * (same & (row == col + 16)))
    add("hm64", (t[:, None] // 64 == np.arange(2)[None]))
    add("hm32", (t[:, None] // 32 == np.arange(4)[None]))
    add("iota", np.broadcast_to(t, (P, P)))
    add("ln_eps", np.full((P, 1), LN_EPS))
    add("iota8", np.broadcast_to(np.arange(8), (P, 8)))
    return np.concatenate(parts, 1)


NCST = build_constants().shape[1]


def build_program(nc, ins, outs):
    ctx = ExitStack()
    with ctx:
        def sb(name, shape, dt=F32):
            return ctx.enter_context(nc.sbuf_tensor(name, shape, dt))

        used_names = {}

        def sem(name):
            if name not in used_names:
                used_names[name] = ctx.enter_context(nc.semaphore(name))
            return used_names[name]

        ring = sb("ring", [P, RING, KC * TW])
        cst = sb("cst", [P, NCST])
        xT = sb("xT", [P, KC, TOK])
        hT = sb("hT", [P, KC, TOK])
        cT = sb("cT", [P, KC, 2])
        cS = sb("cS", [P, KC, 2])
        bada = sb("bada", [P, L, 48])
        mod = sb("mod", [P, L, 48, 2])
        lnp = sb("lnp", [P, L, 4, KC])
        lna = sb("lna", [P, L, 4, KC])
        hgb = sb("hgb", [P, 3, 2, KC, 2])
        rv = sb("rv", [P, L, 15])
        omk = sb("omk", [P, L, 2])
        w0row = sb("w0row", [1, L, 512])
        glbrow = sb("glbrow", [1, L, 256])
        sinkB = sb("sinkB", [P, L, 8])
        wbB = sb("wbB", [P, 512])
        abB = sb("abB", [P, 512])
        gbw = sb("gbw", [P, 256])
        glb = sb("glb", [32, 256])
        s0r = sb("s0r", [P, 4, 64])
        s0g = sb("s0g", [P, 2, 64])
        kcT = sb("kcT", [P, P])
        vc = sb("vc", [P, P])
        router = sb("router", [P, KC, NE])
        decay_rate = sb("decay_rate", [P, 2, TOK])
        tanhT, aaT = decay_rate[:, 0, :], decay_rate[:, 1, :]
        sgaT = sb("sgaT", [P, TOK])
        glaT = sb("glaT", [32, TOK])
        qT = sb("qT", [P, 4, TOK])
        kT = sb("kT", [P, TOK])
        av = sb("av", [P, 2, P])
        rT = sb("rT", [P, 2, TOK])
        kfT = sb("kfT", [P, 2, TOK])
        vT = sb("vT", [P, 2, TOK])
        cqT = sb("cqT", [P, TOK])
        ckT = sb("ckT", [P, TOK])
        cv = sb("cv", [P, 2, 256])
        ogs = sb("ogs", [P, 2, TOK])
        oaT = sb("oaT", [P, 4, TOK])
        obT = sb("obT", [P, 2, TOK])
        ocT = sb("ocT", [P, 2, TOK])
        WORK, WIDE = 8832, 9600
        work = sb("work", [P, WORK])
        wide = sb("wide", [P, WIDE])
        rowbuf = sb("rowbuf", [2, 2, TW])
        zeros = sb("zeros", [P, 512])
        table_in = sb("table_in", [P, 1])
        idxu = sb("idxu", [P, 2, 8], U32)
        passes_i = sb("passes_i", [P, OVER + 1], I32)
        fstate = sb("fstate", [P, 2, 2, P])
        gstate = sb("gstate", [P, 2, 256])
        bank = [ctx.enter_context(nc.psum_tensor(f"bank{i}", [P, 512], F32)) for i in range(8)]

        def ada_rows(t, n):
            return t[32 * (n % 2):32 * (n % 2) + 2, 0:TW]

        def C(name):
            a, n = CST[name]
            return cst[:, a:a + n]

        def shaped(v, shape):
            names = "abcd"[:len(shape)]
            if len(shape) < 2:
                return v
            return v.rearrange(f"p ({' '.join(names)}) -> p {' '.join(names)}",
                               **{k: n for k, n in zip(names[:-1], shape[:-1])})

        def carver(area, size, start=0):
            at = [start]

            def cut(*shape):
                a, n = at[0], int(np.prod(shape))
                assert a + n <= size, (a, n, size)
                at[0] = a + n
                return shaped(area[:, a:a + n], shape)
            return cut

        def bk(i, *shape):
            return shaped(bank[i][:, 0:int(np.prod(shape))], shape)

        cut = carver(wide, WIDE)
        qL, kxL, kxP = cut(4, P), cut(2, 256), cut(2, P)
        pL, pP, pT = cut(8, 256), cut(8, P), cut(24, P)
        mneg, den, esink = cut(16), cut(16), cut(16)
        atmp, krot, rtmp_k = cut(4, P), cut(P), cut(P)
        cut = carver(work, WORK)
        sigz = cut(2, 512)
        aT, kapT, akT, ktT = cut(2, 2, TOK), cut(2, TOK), cut(2, 2, TOK), cut(2, 2, TOK)
        gT, bonT, Vn, yT, rtmp, rtmp2 = (cut(2, TOK) for _ in range(6))
        Bc, KcR = [cut(2, P) for _ in range(2)], [cut(2, P) for _ in range(2)]
        cut = carver(wide, WIDE)
        KR = [cut(2, 2, 2, P) for _ in range(2)]
        MTQ = [cut(2, 2, 2, P) for _ in range(2)]
        AKQ = [cut(2, 2, 2, P) for _ in range(2)]
        shared = 1024 * 6
        Tm, TmT = [cut(4, P) for _ in range(2)], [cut(4, P) for _ in range(2)]
        Xs, nU = [cut(256) for _ in range(2)], [cut(256) for _ in range(2)]
        s0c, ecr, elast = cut(4, 64), cut(4), cut(4)
        P1 = [qT[:, 2 * d:2 * d + 2, :].rearrange("p a (b t) -> p (a b) t", b=2) for d in range(2)]
        cut = carver(wide, WIDE, shared)
        Ep, En = [cut(2, 2, P) for _ in range(2)], [cut(2, P) for _ in range(2)]
        K2T = carver(wide, WIDE, shared)(2, 4, P)
        K2n = P1
        cut = carver(work, WORK)
        glog, gtm, ecg = cut(512), cut(512), cut(2)
        EG, EGn, Qh = cut(4, P), cut(4, P), cut(P)
        Qx, KcG, attT = cut(4, 4, P), cut(4, P), cut(4, 4, P)
        K2g, K2gn, s0gc = cut(2, P), cut(2, P), cut(2, 64)
        oc, gsq = cut(512), cut(512)
        sg = carver(wide, WIDE)(2 * len(GATES) - 8, TOK)
        early_gates = [kfT[:, :, :], decay_rate[:, :, :], shaped(wbB[:, :], (2, TOK)), shaped(abB[:, :], (2, TOK))]

        def gate_tile(l, i):
            if l == 1 and i == 4:
                return shaped(zeros[:, :], (2, TOK))
            return early_gates[i] if i < 4 else sg[:, 2 * i - 8:2 * i - 6, :]

        cut = carver(work, WORK)
        merged, mtmp, yLN, rstd = cut(KC, TOK), cut(KC, TOK), cut(KC, TOK), cut(TOK)
        cut = carver(work, WORK)
        hid, sgt = [cut(2, TOK) for _ in range(2)], [cut(2, TOK) for _ in range(2)]
        cut = carver(work, WORK)
        xgT, ysb, selT = cut(KC, P), cut(D), cut(TOK)
        sel, selg = cut(2, P), cut(2, P)
        mhid, mhidT, msig = ([cut(TW) for _ in range(2)] for _ in range(3))
        cut = carver(wide, WIDE)
        accT, hN = cut(KC, TOK), cut(2, D)
        lg, top8, idxf, gts, pick2, member, slotno = (cut(2, 8) for _ in range(7))
        gap, crowded, rank, onehot = cut(2, 2), cut(8), cut(8), cut(8)
        rtab, ptab, gtab, evf = cut(2, 8), cut(2, NE + OVER + 1), cut(2, NE + OVER + 1), cut(OVER + 1)

        block = ctx.enter_context(nc.Block())

        def w_tile(l, name):
            w_in = ins["w_in"][l].rearrange("(c p) n -> p c n", p=P)
            if name == "decay_rate":
                return [((slice(None), 64 * d + 128 * a, 64), ins[w][l, d].rearrange("(c p) n -> p c n", p=P))
                        for a, w in enumerate(["rwkv_w_a", "rwkv_a_a"]) for d in range(2)]
            if name == "gate_gla":
                return [((slice(None), 0, P), ins["rwkv_g_a"][l].rearrange("(c p) n -> p c n", p=P))] + [
                    ((slice(None), P + 16 * d, 16), ins["gla_gate_a"][l, d].rearrange("(c p) n -> p c n", p=P))
                    for d in range(2)]
            if name in ("q0", "q1"):
                h0 = 2 * int(name[1])
                return [((slice(None), P * jj + 64 * g, 64), w_in[:, :, 256 * g + 64 * (h0 + jj):256 * g + 64 * (h0 + jj) + 64])
                        for jj in range(2) for g in range(2)]
            t = W_IN.index(name)
            return [((slice(None), 0, TW), w_in[:, :, t * TW:(t + 1) * TW])]

        def slot8(s):
            return ring[:, s, :].rearrange("p (c n) -> p c n", c=KC)

        def slot2(s):
            return ring[:, s, :].rearrange("p (c n) -> p c n", c=2)

        fills = {}
        count = [0] * RING
        for l in range(L):
            for i, n in enumerate(MIX[l]):
                count[i % RING] += 16 * MIX_DMAS.get(n, 1)
                fills[(l, n)] = (i % RING, count[i % RING])

        def tile_number(l, name):
            return MIX_BASE[l] + MIX[l].index(name) + 1

        EVAC = {"decay_rate": "act", "gate_gla": "act", "q0": "dve", "q1": "dve", "kv": "dve", "br": "dve",
                "bk": "dve", "bv": "act", "cqk": "dve", "cv": "act", "cog": "dve"}
        EVAC.update({g: "act" for g in GATES})
        evac_at, n = {}, {"act": 0, "dve": 0}
        for name in PROJ:
            n[EVAC[name]] += 1
            evac_at[name] = (EVAC[name], n[EVAC[name]])
        EV_ACT, EV_DVE = n["act"], n["dve"]

        def evacuated(eng, l, name):
            who, k = evac_at[name]
            eng.wait_ge(sem(f"ev_{who}"), (EV_ACT if who == "act" else EV_DVE) * l + k)

        def dense_loop(eng, unit):
            for par in range(2):
                unit(0, par, par, par, True)
            with eng.Fori(1, DENSE_UNITS // 2) as i:
                for par in range(2):
                    unit(0, i * 2 + par, i * 2 + par, par)
            unit(0, DENSE_UNITS - 1, DENSE_UNITS - 1, 0)

        def second_passes(eng):
            eng.wait_ge(sem("passes_known"), 1)
            return eng.value_load(passes_i[0:1, 0:1], min_val=0, max_val=OVER)

        @block.sync
        def _(sp):
            sp.dma_start(cT[:], ins["cT"]).then_inc(sem("c_in"), 16)
            ada = ins["w_ada"].rearrange("l (c p) n -> p l c n", p=P)

            def ada_first(n):
                if n >= RING:
                    sp.wait_ge(sem("ada_used"), n + 1 - RING)
                sp.dma_start(slot8(n % RING), ada[:, 0, :, n * TW:(n + 1) * TW]).then_inc(sem(f"ada_full{n % RING}"), 16)

            ada_first(0)
            ada_first(1)
            for name, dst in [("cst", cst), ("xT", xT), ("bada", bada), ("lnp", lnp), ("rv", rv)]:
                if name == "xT":
                    for n in range(2, RING):
                        ada_first(n)
                sp.dma_start(dst[:], ins[name]).then_inc(sem("cst_in" if name == "cst" else "params_in"), 16)

            def layer_params(l):
                if l > 0:
                    sp.wait_ge(sem("gla_out"), l)
                    sp.wait_ge(sem("up_read"), 2 * (l - 1) + 1)
                if l == 0:
                    for name, dst in [("w0row", w0row), ("glbrow", glbrow), ("sinkB", sinkB), ("router", router)]:
                        sp.dma_start(dst[:], ins[name]).then_inc(sem("layer_in"), 16)
                for name, dst in [("wbB", wbB), ("abB", abB), ("gbw", gbw), ("glb", glb), ("s0r", s0r),
                                  ("s0g", s0g), ("kcT", kcT), ("vc", vc)]:
                    sp.dma_start(dst[:], ins[name][:, l]).then_inc(sem("layer_in"), 16)

            for n in range(RING, ADA_FIRST):
                ada_first(n)

            def mixer_tiles(l):
                for i, name in enumerate(MIX[l]):
                    s = i % RING
                    if l == 0 and i == 3:
                        layer_params(0)
                    if i >= RING:
                        sp.wait_ge(sem("tile_used"), MIX_BASE[l] + i - RING + 1)
                    elif l == 0:
                        sp.wait_ge(sem("ada_used"), ADA_FIRST - RING + s + 1)
                    else:
                        sp.wait_ge(sem("dense_gu_used" if s % 3 < 2 else "dense_d_used"),
                                   DENSE_UNITS if s < 3 else DENSE_UNITS - 1)
                    full = sem(f"mix_full{s}")
                    if name in EARLY:
                        n = int(name[3:])
                        sp.dma_start(slot8(s), ada[:, n // ADA_TILES, :, (n % ADA_TILES) * TW:(n % ADA_TILES + 1) * TW])\
                            .then_inc(full, 16)
                    elif name in PROJ:
                        for (_, c0, cn), src in w_tile(l, name):
                            sp.dma_start(slot8(s)[:, :, c0:c0 + cn], src).then_inc(full, 16)
                    elif name.startswith("up_a"):
                        j0 = 2 * int(name[-1])
                        wa = ins["w_up_a"][l].rearrange("(g j d) n -> g d j n", g=2, j=4)
                        for g in range(2):
                            sp.dma_start(slot2(s)[64 * g:64 * g + 64], wa[g, :, j0:j0 + 2, :]).then_inc(full, 16)
                    else:
                        if name in ("up_b", "up_c"):
                            w = ins["w_" + name][l]
                        else:
                            w = ins["w_out"][l][int(name[-1]) * 256:int(name[-1]) * 256 + 256, :]
                        sp.dma_start(slot2(s), w.rearrange("(c p) n -> p c n", p=P)).then_inc(full, 16)

            def unit_loads(kind, u, par, gate, up, down):
                for k, src in enumerate([gate, up, down]):
                    s = 3 * par + k
                    if u is None:
                        l = int(kind == "moe")
                        last = max(i for i in range(MIX_TILES[l]) if i % RING == s)
                        sp.wait_ge(sem("tile_used"), MIX_BASE[l] + last + 1)
                    elif k != 1:
                        sp.wait_ge(sem(f"{kind}_{'gu' if k == 0 else 'd'}_used"), u - 1 + 2 * (kind == "moe"))
                    sp.dma_start(slot8(s) if k < 2 else slot2(s), src).then_inc(sem(f"{kind}_full{s}"), 16)

            mixer_tiles(0)
            dg = ins["ffn_w_gate"][0].rearrange("(c p) n -> p c n", p=P)
            du = ins["ffn_w_up"][0].rearrange("(c p) n -> p c n", p=P)
            dd = ins["ffn_w_down"][0].rearrange("(u c p) n -> p u c n", p=P, c=2)

            def dense_unit(e, r, u, par, first=False):
                cols = bass.ds(u * TW, TW)
                unit_loads("dense", None if first else u, par, dg[:, :, cols], du[:, :, cols],
                           dd[:, bass.ds(u, 1)].rearrange("p u c n -> p (u c) n"))

            dense_loop(sp, dense_unit)
            layer_params(1)
            mixer_tiles(1)
            mg = ins["moe_w_gate"][0].rearrange("e (c p) n -> p e c n", p=P)
            mu = ins["moe_w_up"][0].rearrange("e (c p) n -> p e c n", p=P)
            md = ins["moe_w_down"][0].rearrange("e (u c p) n -> p (e u) c n", p=P, c=2)

            def moe_unit(e, r, u, par, first=False):
                cols = bass.ds(r * TW, TW)
                unit_loads("moe", None if first else u, par,
                           mg[:, bass.ds(e, 1), :, cols].rearrange("p e c n -> p (e c) n"),
                           mu[:, bass.ds(e, 1), :, cols].rearrange("p e c n -> p (e c) n"),
                           md[:, bass.ds(e * EXPERT_UNITS + r, 1)].rearrange("p u c n -> p (u c) n"))

            for par in range(2):
                moe_unit(0, par, par, par, True)
            with sp.Fori(1, EXPERT_UNITS // 2) as i:
                for par in range(2):
                    moe_unit(0, i * 2 + par, i * 2 + par, par)
            with sp.Fori(1, NE) as e:
                with sp.Fori(0, EXPERT_UNITS // 2) as i:
                    for par in range(2):
                        moe_unit(e, i * 2 + par, e * EXPERT_UNITS + i * 2 + par, par)
            n_over = second_passes(sp)
            with sp.If(n_over > 0):
                with sp.Fori(0, n_over) as j:
                    expert = sp.value_load(passes_i[0:1, bass.ds(j + 1, 1)], min_val=0, max_val=NE - 1)
                    with sp.Fori(0, EXPERT_UNITS // 2) as i:
                        for par in range(2):
                            moe_unit(expert, i * 2 + par, (j + NE) * EXPERT_UNITS + i * 2 + par, par)
            for c in range(4):
                sp.wait_ge(sem("y_ready"), c + 1)
                sp.dma_start(outs["yT"][:, 2 * c:2 * c + 2], xT[:, 2 * c:2 * c + 2, :]).then_inc(sem("stored"), 16)
            sp.wait_ge(sem("stored"), 64)

        @block.gpsimd
        def _(pool):
            for l in range(L):
                evacuated(pool, l, "kv")
                pool.dma_start(outs["kT"][l], kT[:, 0:P]).then_inc(sem("kept"), 16)
                pool.dma_start(outs["v"][l], av[:, 0, :]).then_inc(sem("kept"), 16)
                pool.wait_ge(sem("fstate_ready"), l + 1)
                for i in range(2):
                    dst = outs["rwkv"][0, l].rearrange("d (c i) v k -> i v d c k", i=2)[i]
                    for d in range(2):
                        pool.dma_start(dst[:, d], fstate[64 * i:64 * i + 64, d, :, 64 * i:64 * i + 64])\
                            .then_inc(sem("kept"), 16)
                pool.wait_ge(sem("gstate_ready"), l + 1)
                for h in range(4):
                    pool.dma_start(outs["gla"][0, l, :, h].rearrange("d k v -> k d v"),
                                   gstate[32 * h:32 * h + 32, :, 64 * h:64 * h + 64]).then_inc(sem("kept"), 16)
                pool.wait_ge(sem("kept"), 160 * (l + 1))

        @block.tensor
        def _(pe):
            mm = nc.tensor.matmul
            ident = C("ident")

            def acc(out, pairs, h_from=None, **kw):
                for n, (a, b) in enumerate(pairs):
                    if h_from is not None and n % 2 == 0:
                        pe.wait_ge(sem("h_ready"), h_from + n // 2 + 1)
                    last = mm(out, a, b, start=(n == 0), stop=(n == len(pairs) - 1), **kw)
                return last

            pe.wait_ge(sem("silu_c"), 1)

            def ada_tile(n, s, full, used):
                pe.wait_ge(full[0], full[1])
                if n >= 2:
                    pe.wait_ge(sem("ada_row"), n - 1)
                acc(ada_rows(bank[0], n), [(cS[:, c, :], slot8(s)[:, c, :])
                                           for c in range(KC)]).then_inc(used, 1)

            def ada_turn(n):
                pe.wait_ge(sem("ada_row"), n + 1)
                if n == 0:
                    pe.wait_ge(sem("cst_in"), 16)
                for h in range(2):
                    c = 4 * (n if n < ADA_FIRST else n - ADA_FIRST) + 2 * h
                    last = nc.tensor.transpose(bank[1][:, c:c + 2], rowbuf[:, n % 2, P * h:P * h + P],
                                               C("ident")[0:2, 0:2])
                last.then_inc(sem("ada_turned"), 1)

            for n in range(ADA_FIRST):
                ada_tile(n, n % RING, (sem(f"ada_full{n % RING}"), 16 * (n // RING + 1)), sem("ada_used"))
                if n >= 1:
                    ada_turn(n - 1)
            ada_turn(ADA_FIRST - 1)
            early = [ADA_FIRST]

            def early_tiles(count):
                for _ in range(count):
                    n = early[0]
                    early[0] += 1
                    if n == ADA_FIRST:
                        evacuated(pe, 0, "cv")
                        evacuated(pe, 0, "cog")
                    s, full = fills[(0, f"ada{n}")]
                    ada_tile(n, s, (sem(f"mix_full{s}"), full), sem("tile_used"))
                    if n > ADA_FIRST:
                        ada_turn(n - 1)
                    if n == L * ADA_TILES - 1:
                        ada_turn(n)

            def project(l, names):
                for name in names:
                    i = PROJ.index(name)
                    s, full = fills[(l, name)]
                    b = bk(i % 2, 2, TOK)
                    if l == 0 and i < 2:
                        pe.wait_ge(sem("mod_read"), 1)
                    if l == 0 and name == "gate0":
                        pe.wait_ge(sem("mod_read"), 2)
                    if i >= 2:
                        evacuated(pe, l, PROJ[i - 2])
                    pe.wait_ge(sem(f"mix_full{s}"), full)
                    w = slot8(s)
                    if name == "kv":
                        acc(b[:, 0, :], [(w[:, c, 0:P], hT[:, c, :]) for c in range(KC)])
                        for st in range(2):
                            last = acc(bank[i % 2][:, 256 + P * st:384 + P * st],
                                       [(hT[:, c, P * st:P * st + P], w[:, c, P:2 * P]) for c in range(KC)])
                    elif name == "cv":
                        for st in range(2):
                            last = acc(b[:, st, :], [(hT[:, c, P * st:P * st + P], w[:, c, :]) for c in range(KC)])
                    elif name == "gate_gla":
                        acc(b[:, 0, :], [(w[:, c, 0:P], hT[:, c, :]) for c in range(KC)])
                        last = acc(b[0:32, 1, :], [(w[:, c, P:P + 32], hT[:, c, :]) for c in range(KC)])
                    else:
                        for h in range(2):
                            last = acc(b[:, h, :], [(w[:, c, P * h:P * h + P], hT[:, c, :]) for c in range(KC)],
                                       h_from=8 * l if i == 0 and h == 0 else None)
                    last.then_inc(sem("tile_used"), 1)

            def attention_and_inputs(l):
                evacuated(pe, l, "kv")
                pe.wait_ge(sem("layer_in"), 64 + 128 * (l + 1))
                mm(bank[2][:, :], C("rot"), qT[:, :, P:TOK], start=True, stop=True)
                mm(bank[3][:, 0:P], C("rot"), kT[:, P:TOK], start=True, stop=True).then_inc(sem("rot_done"), 1)
                project(l, ["decay_rate"])
                pe.wait_ge(sem("attn_in"), l + 1)
                for j in range(4):
                    mm(bank[4 + j][:, :], qL[:, j, :], kxL[:, :, :], start=True, stop=True)
                for j in range(4):
                    last = mm(bk(2 + j // 2, 2, 256)[:, j % 2, :], qT[:, j, 0:P], kxP[:, :, :], start=True, stop=True)
                last.then_inc(sem("scores_done"), 1)
                project(l, ["gate_gla", "br", "bk", "bv"])
                pe.wait_ge(sem("probs_ready"), l + 1)
                for n in range(24):
                    src = pL[:, n // 2, P * (n % 2):P * (n % 2) + P] if n < 16 else pP[:, n - 16, :]
                    b = 4 + n // 4 if n < 16 else 2 + (n - 16) // 4
                    last = nc.tensor.transpose(bk(b, 4, P)[:, n % 4, :], src, ident)
                last.then_inc(sem("probsT_done"), 1)
                project(l, ["cqk"])
                pe.wait_ge(sem("probsT_dve"), l + 1)
                pe.wait_ge(sem("probsT_act"), l + 1)
                for j in range(4):
                    out = bk(2 + j // 2, 2, TOK)
                    for g in range(2):
                        h = 2 * j + g
                        mm(out[64 * g:64 * g + 64, j % 2, 0:P], av[:, 0, 64 * g:64 * g + 64], pT[:, 16 + h, :],
                           start=True, stop=True)
                        mm(out[64 * g:64 * g + 64, j % 2, P:TOK], av[:, 1, 64 * g:64 * g + 64], pT[:, 2 * h, :],
                           start=True, stop=False)
                        last = mm(out[64 * g:64 * g + 64, j % 2, P:TOK], vc[:, 64 * g:64 * g + 64],
                                  pT[:, 2 * h + 1, :], start=False, stop=True)
                last.then_inc(sem("attn_done"), 1)
                pe.wait_ge(sem("kk_sq"), l + 1)
                mm(bank[7][:, :], C("blk"), rtmp, start=True, stop=True).then_inc(sem("kk_norm"), 1)
                evacuated(pe, l, "gate_gla")
                for d in range(2):
                    for c in range(2):
                        mm(bk(4 + d, 2, TOK)[:, c, :], abB[:, 256 * d + P * c:256 * d + P * c + P], aaT,
                           start=True, stop=True)
                for c in range(2):
                    mm(bk(6, 2, TOK)[:, c, :], gbw[:, P * c:P * c + P], sgaT[:, :], start=True, stop=True)
                pe.wait_ge(sem("attn_out"), l + 1)
                for st in range(2):
                    mm(bank[2 + st][:, :], decay_rate[:, 0, P * st:P * st + P], wbB[:, :], start=True, stop=False)
                    last = mm(bank[2 + st][:, :], C("ones")[0:1, :], w0row[:, l, :], start=False, stop=True)
                last.then_inc(sem("rw_logits"), 1)
                project(l, ["cv"])
                evacuated(pe, l, "bv")
                pe.wait_ge(sem("rw_act"), l + 1)
                for st in range(2):
                    for c in range(2):
                        last = nc.tensor.transpose(bk(2, 2, 2, P)[:, st, c, :], vT[:, c, P * st:P * st + P], ident)
                last.then_inc(sem("vn_done"), 1)
                project(l, ["cog"])
                pe.wait_ge(sem("bonus_in"), l + 1)
                mm(bank[3][:, :], C("blk"), rtmp2, start=True, stop=True).then_inc(sem("bonus_sum"), 1)
                pe.wait_ge(sem("bonus_out"), l + 1)

            def rwkv_stream(l, st):
                k = 2 * l + st + 1
                for d in range(2):
                    for c in range(2):
                        last = mm(bk(2 + d, 2, 256)[:, c, :], sigz[:, st, 256 * d + P * c:256 * d + P * c + P],
                                  C(f"tri{d}"), start=True, stop=True)
                if st == 1:
                    for d in range(2):
                        for c in range(2):
                            last = mm(bank[4][:, 2 * d + c:2 * d + c + 1],
                                      sigz[:, st, 256 * d + P * c:256 * d + P * c + P], C(f"cen{d}"),
                                      start=True, stop=True)
                last.then_inc(sem("cum_done"), 1)
                if st == 0 and l == 0:
                    early_tiles(2)
                elif st == 0:
                    project(l, ["gate0"])
                pe.wait_ge(sem("decays_ready"), 2 * k)
                for d in range(2):
                    pe.wait_ge(sem("khat_ready"), 2 * (k - 1) + d + 1)
                    if d == 1:
                        pe.wait_ge(sem("mats_read"), 2 * (k - 1) + 1)
                    for c in range(2):
                        mm(bank[2 + c][:, :], Bc[d][:, c, :], KR[d][:, c, :, :, :], start=True, stop=True)
                        mm(bank[4 + c][:, :], KcR[d][:, c, :], KR[d][:, c, :, :, :], start=True, stop=True)
                    for c in range(2):
                        for i in range(2):
                            last = mm(bk(6, 4, P)[:, 2 * c + i, :], KR[d][:, c, 0, i, :], Bc[d][:, c, :],
                                      start=True, stop=True)
                    last.then_inc(sem("mats_done"), 1)
                    if l == 0:
                        early_tiles(2)
                    else:
                        project(l, [f"gate{2 * st + d + 1}"])
                for j in range(1, LEVELS + 1):
                    n = (k - 1) * LEVELS + j
                    for d in range(2):
                        if j == 1:
                            pe.wait_ge(sem("mats_read"), 2 * k)
                        else:
                            pe.wait_ge(sem(f"inv_T{d}"), n - 1)
                        for h in range(4):
                            last = mm(bk(2 + 3 * d, 4, P)[:, h, :], MTQ[d][:, h // 2, 0, h % 2, :], Tm[d][:, h, :],
                                      start=True, stop=True)
                        last.then_inc(sem(f"inv_MT{d}"), 1)
                    if l == 0:
                        early_tiles(1)
                    for d in range(2):
                        pe.wait_ge(sem(f"inv_P{d}"), n)
                        for h in range(4 if j < LEVELS else 0):
                            mm(bk(3 + 3 * d, 4, P)[:, h, :], TmT[d][:, h, :], P1[d][:, h, :], start=True, stop=True)
                        for h in range(4):
                            last = mm(bk(4 + 3 * d, 4, P)[:, h, :], P1[d][:, h, :],
                                      TmT[d][:, h, :], start=True, stop=True)
                        last.then_inc(sem(f"inv_TP{d}"), 1)
                    if l == 0:
                        early_tiles(1)
                for d in range(2):
                    pe.wait_ge(sem(f"inv_T{d}"), k * LEVELS)
                    for h in range(4):
                        c, i = h // 2, h % 2
                        out = bank[2 + d][:, 64 * h:64 * h + 64]
                        pairs = [(AKQ[d][:, c, 0, i, :], Vn[:, st, 64 * h:64 * h + 64])]
                        if st == 1:
                            pairs.append((KR[d][:, c, 0, i, :], s0c[:, 2 * d + c, :]))
                        last = acc(out, pairs)
                    last.then_inc(sem("x_done"), 1)
                for d in range(2):
                    pe.wait_ge(sem("xs_ready"), 2 * (k - 1) + d + 1)
                    for h in range(4):
                        last = mm(bank[4 + d][:, 64 * h:64 * h + 64], TmT[d][:, h, :], Xs[d][:, 64 * h:64 * h + 64],
                                  start=True, stop=True)
                    last.then_inc(sem("u_done"), 1)
                pe.wait_ge(sem("nu_ready"), 2 * k)
                for c in range(2):
                    for i in range(2):
                        h = 2 * c + i
                        pairs = []
                        for d in range(2):
                            pairs.append((Vn[:, st, 64 * h:64 * h + 64], AKQ[d][:, c, 1, i, :]))
                            pairs.append((nU[d][:, 64 * h:64 * h + 64], MTQ[d][:, c, 1, i, :]))
                            if st == 1:
                                pairs.append((s0c[:, 2 * d + c, :], KR[d][:, c, 1, i, :]))
                        last = acc(bk(6, 2, P)[64 * i:64 * i + 64, c, :], pairs)
                last.then_inc(sem("y_done"), 1)
                if st == 0:
                    pe.wait_ge(sem("k2_ready"), l + 1)
                    for x in range(2):
                        for e in range(4):
                            last = nc.tensor.transpose(bk(2 + x, 4, P)[:, e, :], K2T[:, x, e, :], ident)
                    last.then_inc(sem("k2T_done"), 1)
                    if l == 0:
                        early_tiles(2)
                    pe.wait_ge(sem("k2n_ready"), l + 1)
                    for d in range(2):
                        for c in range(2):
                            last = acc(bk(7, 4, P)[:, 2 * d + c, :],
                                       [(Vn[:, 0, P * c:P * c + P], K2n[0][:, 2 * d + c, :]),
                                        (nU[d][:, P * c:P * c + P], K2n[1][:, 2 * d + c, :])])
                    last.then_inc(sem("fs_done"), 1)
                    pe.wait_ge(sem("fstate_ready"), l + 1)
                pe.wait_ge(sem("yT_ready"), k)

            def norm_and_gla(l):
                gates = iter(GATES if l == 0 else GATES[5:])

                def next_gates(count):
                    project(l, [next(gates) for _ in range(count)])

                evacuated(pe, l, "gate_gla")
                mm(bank[2][:, :], C("blkm"), yT[:, :, :], start=True, stop=True).then_inc(sem("gn_mean"), 1)
                for st in range(2):
                    mm(bk(5, 2, 256)[:, st, :], glaT[:, P * st:P * st + P], glb[:, :], start=True, stop=False)
                    last = mm(bk(5, 2, 256)[:, st, :], C("ones")[0:1, :], glbrow[:, l, :], start=False, stop=True)
                last.then_inc(sem("gl_done"), 1)
                next_gates(1)
                pe.wait_ge(sem("gn_sq"), l + 1)
                mm(bank[3][:, :], C("blkm"), rtmp, start=True, stop=True).then_inc(sem("gn_var"), 1)
                next_gates(1)
                pe.wait_ge(sem("glog_ready"), l + 1)
                lgv = glog.rearrange("p (s d c) -> p s d c", s=2, d=2)
                for st in range(2):
                    for d in range(2):
                        mm(bk(3, 4, P)[:, 2 * st + d, :], lgv[:, st, d, :], C(f"trig{d}"), start=True, stop=True)
                for d in range(2):
                    last = mm(bank[4][:, d:d + 1], lgv[:, 1, d, :], C(f"ceng{d}"), start=True, stop=True)
                last.then_inc(sem("gcum_done"), 1)
                next_gates(2)
                pe.wait_ge(sem("gq_ready"), l + 1)
                for x in range(4):
                    last = mm(bank[4 + x][:, :], KcG[:, x, :], Qx[:, x, :, :], start=True, stop=True)
                last.then_inc(sem("att_done"), 1)
                next_gates(1)
                pe.wait_ge(sem("att_ready"), l + 1)
                for st in range(2):
                    for h in range(4):
                        c, i = h // 2, h % 2
                        pairs = []
                        for d in range(2):
                            pairs.append((cv[:, st, 64 * h:64 * h + 64], attT[:, 2 * st + d, h, :]))
                            if st == 1:
                                pairs.append((s0gc[:, d, :], Qx[:, 2 * st + d, h, :]))
                        last = acc(bk(2, 2, TOK)[64 * i:64 * i + 64, c, P * st:P * st + P], pairs)
                last.then_inc(sem("go_done"), 1)
                for d in range(2):
                    last = nc.tensor.transpose(bk(3, 4, P)[:, d, :], K2g[:, d, :], ident)
                last.then_inc(sem("k2g_done"), 1)
                next_gates(1)
                pe.wait_ge(sem("k2g_ready"), l + 1)
                for d in range(2):
                    last = mm(bk(4, 2, 256)[:, d, :], K2gn[:, d, :], cv[:, 0, :], start=True, stop=True)
                last.then_inc(sem("gs_done"), 1)
                pe.wait_ge(sem("gsq_ready"), l + 1)
                mm(bank[5][:, :], C("blkm"), gsq, start=True, stop=True).then_inc(sem("gms_done"), 1)
                next_gates(6 if l == 0 else 1)

            def rows_outer(l, tiles, src, first_bank, ready=None):
                n = 0
                for name in tiles:
                    s, full = fills[(l, name)]
                    pe.wait_ge(sem(f"mix_full{s}"), full)
                    if ready is not None:
                        pe.wait_ge(sem("merged_ready"), ready + n // 2 + 1)
                    for c in range(2):
                        for m in range(KC):
                            last = mm(bk(first_bank + m // 2, 2, TOK)[:, m % 2, :], slot2(s)[:, c, P * m:P * m + P],
                                      src[:, n, :], start=(n == 0 and m % 2 == 0),
                                      stop=(n == 2 * len(tiles) - 1), skip_group_check=True)
                        n += 1
                    last.then_inc(sem("tile_used"), 1)

            def merge(l):
                evacuated(pe, l, "gate11")
                evacuated(pe, l, "gate10")
                pe.wait_ge(sem("gla_out"), l + 1)
                rows_outer(l, ["up_a0", "up_a1"], oaT, 0)
                rows_outer(l, ["up_b"], obT, 4)
                pe.wait_ge(sem("up_read"), 2 * l + 1)
                rows_outer(l, ["up_c"], ocT, 0)
                pe.wait_ge(sem("up_read"), 2 * l + 2)
                rows_outer(l, [f"out{i}" for i in range(4)], merged, 4, ready=4 * l)

            def layer_norm(n):
                for b, src, ready, done in ((0, yLN, "ln_y", "ln_mean"), (1, mtmp, "ln_sq", "ln_var")):
                    for m in range(KC):
                        if m % 2 == 0:
                            pe.wait_ge(sem(ready), 4 * n + m // 2 + 1)
                        last = mm(bank[b][:, 0:TOK], C("mean_d"), src[:, m, :], start=(m == 0), stop=(m == KC - 1))
                    last.then_inc(sem(done), 1)

            def gate_up(par, k, h_from=None):
                pe.wait_ge(sem(f"dense_full{3 * par}"), k * 16)
                for h in range(2):
                    acc(bk(2 * par, 2, TOK)[:, h, :], [(slot8(3 * par)[:, c, P * h:P * h + P], hT[:, c, :])
                                                       for c in range(KC)], h_from=h_from if h == 0 else None)
                pe.wait_ge(sem(f"dense_full{3 * par + 1}"), k * 16)
                for h in range(2):
                    last = acc(bk(2 * par + 1, 2, TOK)[:, h, :], [(slot8(3 * par + 1)[:, c, P * h:P * h + P], hT[:, c, :])
                                                                  for c in range(KC)])
                last.then_inc(sem("dense_gu_used"), 1)

            def down(par, k, hid_count):
                pe.wait_ge(sem(f"dense_full{3 * par + 2}"), k * 16)
                pe.wait_ge(sem("dense_hid"), hid_count)
                for c in range(2):
                    for m in range(KC):
                        last = mm(bk(4 + m // 2, 2, TOK)[:, m % 2, :], slot2(3 * par + 2)[:, c, P * m:P * m + P],
                                  hid[par][:, c, :], start=False, stop=False, skip_group_check=True)
                last.then_inc(sem("dense_d_used"), 1)

            def dense_mixer():
                pe.wait_ge(sem("ln_y"), 4)
                for b in range(4):
                    mm(bank[4 + b][:, :], zeros[:, 0:P], zeros[:, :], start=True, stop=False,
                       skip_group_check=True)
                pe.wait_ge(sem("h_ready"), 5)
                gate_up(0, 1, h_from=4)

                def turn(i):
                    for par in (1, 0):
                        if par == 0 or not isinstance(i, int):
                            pe.wait_ge(sem("dense_hid"), i * 2 + (0 if par else 1))
                        gate_up(par, i + (1 if par else 2))
                        down(1 - par, i + 1, i * 2 + (1 if par else 2))

                turn(0)
                with pe.Fori(1, DENSE_UNITS // 2) as i:
                    turn(i)
                down(0, (DENSE_UNITS + 1) // 2, DENSE_UNITS)

            def expert_mixer():
                for st in range(2):
                    last = acc(bank[st][:, 0:NE], [(hT[:, c, P * st:P * st + P], router[:, c, :]) for c in range(KC)],
                               h_from=12 if st == 0 else None)
                last.then_inc(sem("logits_done"), 1)
                for st in range(2):
                    for m in range(KC):
                        last = nc.tensor.transpose(bk(4 + 2 * st + m // 4, 4, P)[:, m % 4, :],
                                                   hT[:, m, P * st:P * st + P], ident)
                last.then_inc(sem("hN_done"), 1)
                pe.wait_ge(sem("member_ready"), 1)
                before = C("mask0")[:, 0:P]
                mm(bank[2][:, 0:NE], before, member[:, 0, :], start=True, stop=True)
                acc(bank[2][:, NE:2 * NE], [(before, member[:, 1, :]), (C("ones"), member[:, 0, :])])
                acc(bank[2][:, 2 * NE:3 * NE], [(C("ones"), member[:, 0, :]), (C("ones"), member[:, 1, :])])\
                    .then_inc(sem("slots_done"), 1)
                pe.wait_ge(sem("hN_ready"), 1)
                pe.sem_inc(sem("moe_gu_used"), 2)
                pe.sem_inc(sem("moe_d_used"), 2)

                def gather(p, half):
                    if half == 0:
                        pe.wait_ge(sem("moe_sel"), p + 1)
                    for m in range(4 * half, 4 * half + 4):
                        last = acc(bk(6 + m // 4, 4, P)[:, m % 4, :],
                                   [(hN[:, st, P * m:P * m + P], sel[:, st, :]) for st in range(2)])
                    last.then_inc(sem("moe_xg_done"), 1)

                def turn_selection():
                    for st in range(2):
                        last = nc.tensor.transpose(bank[1][:, P * st:P * st + P], selg[:, st, :], ident)
                    last.then_inc(sem("moe_selT_done"), 1)

                def rows(k, par, p, u):
                    pe.wait_ge(sem(f"moe_full{3 * par + k}"), u[1] * 16)
                    if k == 0:
                        pe.wait_ge(sem("moe_hid"), u[0] + 1)
                    last = acc(bank[par][:, TW * k:TW * k + TW], [(xgT[:, c, :], slot8(3 * par + k)[:, c, :])
                                                                  for c in range(KC)])
                    if k == 1:
                        last.then_inc(sem("moe_gu_used"), 1)

                def turn_hidden(par, u):
                    pe.wait_ge(sem("moe_hid"), u[0] + 3)
                    pe.wait_ge(sem("moe_hidT"), u[0] + 1)
                    for c in range(2):
                        last = nc.tensor.transpose(bank[2 + par][:, P * c:P * c + P], mhid[par][:, P * c:P * c + P], ident)
                    last.then_inc(sem("moe_turned"), 1)

                def down_rows(par, u, first=False, final=False):
                    pe.wait_ge(sem(f"moe_full{3 * par + 2}"), u[1] * 16)
                    pe.wait_ge(sem("moe_hidT"), u[0] + 3)
                    for c in range(2):
                        for h in range(2):
                            last = mm(bank[4 + h][:, :], mhidT[par][:, P * c:P * c + P],
                                      slot2(3 * par + 2)[:, c, 512 * h:512 * h + 512], start=(first and c == 0),
                                      stop=(final and c == 1), skip_group_check=True)
                    last.then_inc(sem("moe_d_used"), 1)

                def step(par, p, here, ahead, first=False):
                    rows(0, 1 - par, p, ahead)
                    turn_hidden(par, here)
                    rows(1, 1 - par, p, ahead)
                    down_rows(par, here, first)

                gather(0, 0)
                gather(0, 1)
                turn_selection()
                n_pass = second_passes(pe) + NE
                H = EXPERT_UNITS // 2
                with pe.Fori(0, n_pass) as p:
                    def unit(k, i=0):
                        return p * EXPERT_UNITS + (i * 2 + k), p * H + (i + (k // 2 + 1))
                    pe.wait_ge(sem("moe_xg"), p + 1)
                    rows(0, 0, p, unit(0))
                    rows(1, 0, p, unit(0))
                    pe.wait_ge(sem("moe_selT"), p + 1)
                    pe.wait_ge(sem("moe_acc"), p * 4 + 1)
                    pe.wait_ge(sem("moe_y"), p + 1)
                    step(0, p, unit(0), unit(1), first=True)
                    with pe.Fori(0, H - 1) as i:
                        step(1, p, unit(1, i), unit(2, i))
                        step(0, p, unit(2, i), unit(3, i))
                    turn_hidden(1, unit(EXPERT_UNITS - 1))
                    gather(p + 1, 0)
                    down_rows(1, unit(EXPERT_UNITS - 1), final=True)
                    gather(p + 1, 1)
                    pe.wait_ge(sem("moe_y"), p + 2)
                    for b in range(4):
                        if b == 2:
                            pe.wait_ge(sem("moe_xg"), p + 2)
                        for h in range(2):
                            m = 2 * b + h
                            last = mm(bk([2, 3, 6, 7][b], 2, TOK)[:, h, :], ysb[:, P * m:P * m + P], selT,
                                      start=True, stop=True)
                        last.then_inc(sem("moe_back"), 1)
                    turn_selection()

            for l in range(L):
                project(l, ["q0", "q1", "kv"])
                attention_and_inputs(l)
                for st in range(2):
                    rwkv_stream(l, st)
                norm_and_gla(l)
                merge(l)
                layer_norm(2 * l)
                dense_mixer() if l == 0 else expert_mixer()
                layer_norm(2 * l + 1)

        @block.scalar
        def _(act):
            af = nc.scalar.activation
            steps = [0]

            def chained(ins):
                steps[0] += 1
                ins.then_inc(sem("act_chain"), 1)
                act.wait_ge(sem("act_chain"), steps[0])

            act.wait_ge(sem("c_in"), 16)
            af(cS[:], cT[:], ACT.Sigmoid).then_inc(sem("sig_c"), 1)
            def ada_row(n):
                act.wait_ge(sem("ada_used") if n < ADA_FIRST else sem("tile_used"),
                            n + 1 if n < ADA_FIRST else tile_number(0, f"ada{n}"))
                af(rowbuf[:, n % 2, :], ada_rows(bank[0], n), ACT.Copy)\
                    .then_inc(sem("ada_row"), 1)

            for n in range(ADA_FIRST):
                ada_row(n)
            early = [ADA_FIRST]
            roots, sums = [0], [0]

            def square_root(buf):
                roots[0] += 1
                sums[0] += 1
                act.wait_ge(sem("root_in"), sums[0])
                af(buf, buf, ACT.Sqrt).then_inc(sem("root_out"), 1)

            def layer_norm(n):
                for c in range(4):
                    act.wait_ge(sem("ln_centered"), 4 * n + c + 1)
                    af(mtmp[:, 2 * c:2 * c + 2, :], yLN[:, 2 * c:2 * c + 2, :], ACT.Square).then_inc(sem("ln_sq"), 1)
                af(table_in[:], C("ln_eps"), ACT.Sqrt)
                act.wait_ge(sem("ln_var"), n + 1)
                roots[0] += 1
                af(rstd, bank[1][:, 0:TOK], ACT.Sqrt, bias=C("ln_eps")).then_inc(sem("root_out"), 1)
                l, half = n // 2, n % 2
                gb = lnp if n == 3 else lna
                for m in range(KC):
                    if m % 2 == 0:
                        act.wait_ge(sem("ln_normed"), 4 * n + m // 2 + 1)
                    last = af(xT[:, m, :], yLN[:, m, :], ACT.Identity, bias=gb[:, l, 2 * half + 1, m:m + 1],
                              scale=gb[:, l, 2 * half, m:m + 1])
                    if n == 3 and m % 2 == 1:
                        last.then_inc(sem("y_ready"), 1)
                if n < 3:
                    last.then_inc(sem("x_ready"), 1)

            def project(l, names):
                for name in names:
                    if EVAC[name] != "act" and name != "cog":
                        continue
                    act.wait_ge(sem("tile_used"), tile_number(l, name))
                    b = bk(PROJ.index(name) % 2, 2, TOK)
                    done = sem("ev_act")
                    if name == "decay_rate":
                        af(tanhT, b[:, 0, :], ACT.Tanh)
                        af(aaT, b[:, 1, :], ACT.Copy).then_inc(done, 1)
                    elif name == "gate_gla":
                        af(sgaT[:], b[:, 0, :], ACT.Sigmoid)
                        af(glaT[:], b[0:32, 1, :], ACT.Copy).then_inc(done, 1)
                    elif name == "cog":
                        af(ogs[:], b, ACT.Sigmoid).then_inc(sem("sig_og"), 1)
                    elif name in GATES:
                        i = GATES.index(name)
                        af(gate_tile(l, i), b, ACT.Sigmoid).then_inc(done, 1)
                    else:
                        dst = {"bv": vT, "cv": cv}[name]
                        af(dst[:], b, ACT.Copy).then_inc(done, 1)

            def attention(l):
                project(l, ["decay_rate", "gate_gla"])
                act.wait_ge(sem("max_ready"), l + 1)
                for h in range(8):
                    j, g = h // 2, h % 2
                    af(pP[:, h, :], bk(2 + j // 2, 4, P)[:, 2 * (j % 2) + g, :], ACT.Exp, bias=mneg[:, h:h + 1],
                       scale=0.125, accum_out=den[:, h:h + 1])
                    af(pL[:, h, :], bk(4 + j, 2, 256)[:, g, :], ACT.Exp, bias=mneg[:, 8 + h:9 + h],
                       scale=0.125, accum_out=den[:, 8 + h:9 + h])
                af(esink, esink, ACT.Exp).then_inc(sem("probs_exp"), 1)
                project(l, ["bv"])
                act.wait_ge(sem("probsT_done"), l + 1)
                for b, n in [(7, 12), (2, 16), (3, 20)]:
                    last = af(pT[:, n:n + 4, :], bk(b, 4, P), ACT.Copy)
                last.then_inc(sem("probsT_act"), 1)

            def early_rows(count):
                for n in range(early[0], early[0] + count):
                    ada_row(n)
                early[0] += count

            def rwkv(l):
                square_root(rtmp2)
                act.wait_ge(sem("rw_logits"), l + 1)
                for st in range(2):
                    af(sigz[:, st, :], bank[2 + st][:, :], ACT.Sigmoid)
                for d in range(2):
                    for c in range(2):
                        af(aT[:, d, c, :], bk(4 + d, 2, TOK)[:, c, :], ACT.Sigmoid,
                           bias=rv[:, l, 2 * d + c:2 * d + c + 1])
                af(gT, bk(6, 2, TOK), ACT.Copy).then_inc(sem("rw_act"), 1)
                project(l, ["cv", "cog"])
                for st in range(2):
                    k = 2 * l + st + 1
                    act.wait_ge(sem("cum_done"), k)
                    if st == 1:
                        af(ecr, bank[4][:, 0:4], ACT.Exp).then_inc(sem("center_ready"), 1)
                    for d in range(2):
                        b = bk(2 + d, 2, 2, P)
                        af(Ep[d], b, ACT.Exp)
                        af(En[d], b[:, :, 0, :], ACT.Exp, scale=-1.0).then_inc(sem("decays_ready"), 1)
                    if l == 0:
                        early_rows(18 if st == 0 else 16)
                    else:
                        project(l, GATES[3 * st:3 + 2 * st])
                    for d in range(2):
                        act.wait_ge(sem("x_done"), 2 * (k - 1) + d + 1)
                        af(Xs[d], bank[2 + d][:, 0:256], ACT.Copy).then_inc(sem("xs_ready"), 1)
                    for d in range(2):
                        act.wait_ge(sem("u_done"), 2 * (k - 1) + d + 1)
                        af(nU[d], bank[4 + d][:, 0:256], ACT.Copy, scale=-1.0).then_inc(sem("nu_ready"), 1)
                    act.wait_ge(sem("y_done"), k)
                    af(yT[:, :, P * st:P * st + P], bk(6, 2, P), ACT.Copy).then_inc(sem("yT_ready"), 1)
                    if l == 0 and st == 0:
                        early_rows(2)

            def norm_and_gla(l):
                act.wait_ge(sem("gabs_ready"), l + 1)
                chained(af(glog, glog, ACT.Exp))
                af(glog, glog, ACT.Ln, bias=1.0).then_inc(sem("gln_ready"), 1)
                gates = GATES if l == 0 else GATES[5:]
                project(l, gates[0:1])
                square_root(rtmp2)
                project(l, gates[1:2])
                act.wait_ge(sem("gcum_done"), l + 1)
                af(ecg, bank[4][:, 0:2], ACT.Exp)
                af(EG, bk(3, 4, P), ACT.Exp)
                af(EGn, bk(3, 4, P), ACT.Exp, scale=-1.0).then_inc(sem("gdecay_ready"), 1)
                project(l, gates[2:6])
                square_root(gtm)
                project(l, gates[6:])

            def dense_sigmoid(e, r, u, par, first=False):
                act.wait_ge(sem("dense_gu_used"), u + 1)
                if not first:
                    act.wait_ge(sem("dense_hid"), u - 1)
                af(sgt[par], bk(2 * par, 2, TOK), ACT.Sigmoid).then_inc(sem("dense_sig"), 1)

            def experts():
                act.wait_ge(sem("gap_ready"), 1)
                af(gap[:, 0, :], gap[:, 0, :], ACT.Exp).then_inc(sem("gap_exp"), 1)
                act.wait_ge(sem("hN_done"), 1)
                for b in range(4):
                    last = af(hN[:, b // 2, 512 * (b % 2):512 * (b % 2) + 512], bank[4 + b][:, :], ACT.Copy)
                last.then_inc(sem("hN_ready"), 1)
                act.sem_inc(sem("moe_hidT"), 2)

                def take_gathered(p):
                    for b in range(2):
                        act.wait_ge(sem("moe_xg_done"), p * 2 + (b + 1))
                        last = af(xgT[:, 4 * b:4 * b + 4, :], bk(6 + b, 4, P), ACT.Copy)
                    last.then_inc(sem("moe_xg"), 1)

                def take_selection(p):
                    act.wait_ge(sem("moe_selT_done"), p + 1)
                    af(selT, bank[1][:, 0:TOK], ACT.Copy).then_inc(sem("moe_selT"), 1)

                def sigmoid(par, u):
                    act.wait_ge(sem("moe_gu_used"), u + 3)
                    act.wait_ge(sem("moe_hid"), u + 1)
                    af(msig[par], bank[par][:, 0:TW], ACT.Sigmoid).then_inc(sem("moe_sig"), 1)

                def take_hidden(par, u):
                    act.wait_ge(sem("moe_turned"), u + 1)
                    act.wait_ge(sem("moe_d_used"), u + 1)
                    af(mhidT[par], bank[2 + par][:, 0:TW], ACT.Copy).then_inc(sem("moe_hidT"), 1)

                take_gathered(0)
                take_selection(0)
                n_pass = second_passes(act) + NE
                with act.Fori(0, n_pass) as p:
                    u = p * EXPERT_UNITS
                    sigmoid(0, u)
                    take_hidden(0, u)
                    sigmoid(1, u + 1)
                    with act.Fori(0, EXPERT_UNITS // 2 - 1) as i:
                        for k in (1, 2):
                            take_hidden(k % 2, u + i * 2 + k)
                            sigmoid(1 - k % 2, u + i * 2 + (k + 1))
                    take_hidden(1, u + (EXPERT_UNITS - 1))
                    take_gathered(p + 1)
                    take_selection(p + 1)

            for l in range(L):
                attention(l)
                rwkv(l)
                norm_and_gla(l)
                layer_norm(2 * l)
                if l == 0:
                    dense_loop(act, dense_sigmoid)
                else:
                    experts()
                layer_norm(2 * l + 1)

        @block.vector
        def _(dve):
            v = nc.vector
            steps = [0]

            def chained(ins):
                steps[0] += 1
                ins.then_inc(sem("dve_chain"), 1)
                dve.wait_ge(sem("dve_chain"), steps[0])

            mul = lambda o, a, b: v.tensor_tensor(o, a, b, ALU.mult)
            add = lambda o, a, b: v.tensor_tensor(o, a, b, ALU.add)
            sub = lambda o, a, b: v.tensor_tensor(o, a, b, ALU.subtract)

            def scaled(o, a, s1, s2=None):
                return v.tensor_scalar(o, a, s1, s2, ALU.mult, ALU.add) if s2 is not None else \
                    v.tensor_scalar(o, a, s1, None, ALU.mult)

            def over(a, n, axis=1):
                x = a.unsqueeze(axis)
                shape = list(x.shape)
                shape[axis] = n
                return x.to_broadcast(shape)

            roots = [0]

            def finish_root(buf):
                roots[0] += 1
                dve.wait_ge(sem("root_out"), roots[0])
                chained(v.reciprocal(buf, buf))

            def inverse_root(buf, source, eps):
                v.tensor_scalar(buf, source, eps, None, ALU.add).then_inc(sem("root_in"), 1)
                finish_root(buf)

            dve.wait_ge(sem("sig_c"), 1)
            mul(cS[:], cS[:], cT[:]).then_inc(sem("silu_c"), 1)
            v.memset(zeros[:], 0.0)
            dve.wait_ge(sem("params_in"), 4 * 16)
            dve.wait_ge(sem("cst_in"), 16)
            for l in range(L):
                v.tensor_scalar(omk[:, l, :], rv[:, l, 6:8], -1.0, 1.0, ALU.mult, ALU.add)

            def take_modulations(l, c0, c1, at):
                chained(add(mod[:, l, c0:c1, :], shaped(bank[1][:, at:at + 2 * (c1 - c0)], (c1 - c0, 2)),
                            over(bada[:, l, c0:c1], 2, 2)))
                for a in (8, 32):
                    if c0 <= a < c1:
                        chained(v.tensor_scalar(mod[:, l, a:a + 8, :], mod[:, l, a:a + 8, :], 1.0, None, ALU.add))

            dve.wait_ge(sem("ada_turned"), ADA_FIRST)
            take_modulations(0, 0, 24, 0)
            v.memset(zeros[:, 0:1], 0.0).then_inc(sem("mod_read"), 1)

            def modulate_input():
                for m in range(KC):
                    for st in range(2):
                        sh, sc = mod[:, 0, m, st:st + 1], mod[:, 0, 8 + m, st:st + 1]
                        last = scaled(hT[:, m, P * st:P * st + P], xT[:, m, P * st:P * st + P], sc, sh)
                    if m % 2 == 1:
                        last.then_inc(sem("h_ready"), 1)
                dve.wait_ge(sem("h_ready"), 4)
                v.tensor_scalar(xT[:], xT[:], ALPHA, None, ALU.mult)

            def fuse_modulations():
                v.tensor_scalar(lna[:], lnp[:], ALPHA, None, ALU.mult)
                for n in range(3):
                    l, half = n // 2, n % 2
                    la, sub_layer = (n + 1) // 2, (n + 1) % 2
                    shift, scale = (mod[:, la, 24 * sub_layer + a:24 * sub_layer + a + 8, :] for a in (0, 8))
                    mul(hgb[:, n, 0], scale, over(lnp[:, l, 2 * half, :], 2, 2))
                    chained(mul(hgb[:, n, 1], scale, over(lnp[:, l, 2 * half + 1, :], 2, 2)))
                    last = add(hgb[:, n, 1], hgb[:, n, 1], shift)
                chained(last)

            def project(l, names):
                for name in names:
                    dve.wait_ge(sem("tile_used"), tile_number(l, name))
                    i = PROJ.index(name) % 2
                    b = bk(i, 2, TOK)
                    if name in ("q0", "q1"):
                        j = 2 * int(name[1])
                        last = v.tensor_copy(qT[:, j:j + 2, :], b)
                    elif name == "kv":
                        if l > 0:
                            dve.wait_ge(sem("kept"), 160 * l)
                        v.tensor_copy(kT[:], b[:, 0, :])
                        last = v.tensor_copy(av[:], bk(i, 4, P)[:, 2:4, :])
                    elif name in ("br", "bk"):
                        last = v.tensor_copy((rT if name == "br" else kfT)[:], b)
                    elif name == "cqk":
                        v.tensor_copy(cqT[:], b[:, 0, :])
                        last = v.tensor_copy(ckT[:], b[:, 1, :])
                    else:
                        dve.wait_ge(sem("sig_og"), l + 1)
                        last = mul(ogs[:], ogs[:], b)
                    last.then_inc(sem("ev_dve"), 1)
                evacuated(dve, l, names[-1])

            def attention(l):
                dve.wait_ge(sem("rot_done"), l + 1)
                dve.wait_ge(sem("layer_in"), 64 + 128 * (l + 1))
                mul(atmp, bk(2, 4, P), over(C("sin"), 4))
                mul(qL, qT[:, :, P:TOK], over(C("cos"), 4))
                mul(krot, bank[3][:, 0:P], C("sin"))
                chained(mul(rtmp_k, kT[:, P:TOK], C("cos")))
                add(qL, qL, atmp)
                chained(add(krot, krot, rtmp_k))
                hm = C("hm64")
                for g in range(2):
                    scaled(kxL[:, g, 0:P], krot, hm[:, g:g + 1])
                    scaled(kxL[:, g, P:256], kcT[:, :], hm[:, g:g + 1])
                    last = scaled(kxP[:, g, :], kT[:, 0:P], hm[:, g:g + 1])
                last.then_inc(sem("attn_in"), 1)
                dve.wait_ge(sem("scores_done"), l + 1)
                for j in range(4):
                    v.tensor_reduce(mneg[:, 8 + 2 * j:10 + 2 * j], bk(4 + j, 2, 256), AX.X, ALU.max)
                for b in range(2):
                    last = v.tensor_reduce(mneg[:, 4 * b:4 * b + 4], bk(2 + b, 4, P), AX.X, ALU.max)
                chained(last)
                for st in range(2):
                    last = v.scalar_tensor_tensor(mneg[:, 8 * st:8 * st + 8], mneg[:, 8 * st:8 * st + 8], 0.125,
                                                  sinkB[:, l, :], ALU.mult, ALU.max)
                chained(last)
                for st in range(2):
                    last = sub(esink[:, 8 * st:8 * st + 8], sinkB[:, l, :], mneg[:, 8 * st:8 * st + 8])
                chained(last)
                scaled(mneg, mneg, -1.0).then_inc(sem("max_ready"), 1)
                project(l, ["br", "bk"])
                for c in range(2):
                    last = scaled(kapT[:, c, :], kfT[:, c, :], rv[:, l, 4 + c:5 + c])
                chained(last)
                mul(rtmp, kapT, kapT).then_inc(sem("kk_sq"), 1)
                dve.wait_ge(sem("probs_exp"), l + 1)
                chained(add(den, den, esink))
                chained(v.reciprocal(den, den))
                mul(pP, pP, over(den[:, 0:8], P, 2))
                mul(pL, pL, over(den[:, 8:16], 256, 2)).then_inc(sem("probs_ready"), 1)
                dve.wait_ge(sem("probsT_done"), l + 1)
                for b in range(3):
                    last = v.tensor_copy(pT[:, 4 * b:4 * b + 4, :], bk(4 + b, 4, P))
                last.then_inc(sem("probsT_dve"), 1)
                dve.wait_ge(sem("attn_done"), l + 1)
                v.tensor_copy(oaT[:, 0:2, :], bk(2, 2, TOK))
                v.tensor_copy(oaT[:, 2:4, :], bk(3, 2, TOK)).then_inc(sem("attn_out"), 1)

            def rwkv_inputs(l):
                par = lambda i: rv[:, l, i:i + 1]
                dve.wait_ge(sem("kk_norm"), l + 1)
                inverse_root(rtmp2, bk(7, 2, TOK), 1e-12)
                mul(kapT, kapT, rtmp2)
                project(l, ["cqk"])
                dve.wait_ge(sem("rw_act"), l + 1)
                for d in range(2):
                    mul(akT[:, d], aT[:, d], kapT)
                    for c in range(2):
                        last = scaled(ktT[:, d, c, :], aT[:, d, c, :], par(6 + c), omk[:, l, c:c + 1])
                chained(last)
                for d in range(2):
                    last = mul(ktT[:, d], ktT[:, d], kfT[:])
                chained(last)
                chained(add(rtmp2, ktT[:, 0], ktT[:, 1]))
                chained(mul(rtmp2, rtmp2, rT[:]))
                for c in range(2):
                    last = scaled(rtmp2[:, c, :], rtmp2[:, c, :], par(8 + c))
                last.then_inc(sem("bonus_in"), 1)
                evacuated(dve, l, "bv")
                dve.wait_ge(sem("vn_done"), l + 1)
                v.tensor_copy(Vn, bk(2, 2, TOK))
                dve.wait_ge(sem("bonus_sum"), l + 1)
                mul(bonT, bk(3, 2, TOK), vT[:]).then_inc(sem("bonus_out"), 1)
                project(l, ["cog"])

            def rwkv_stream(l, st):
                k = 2 * l + st + 1
                cols = slice(P * st, P * st + P)
                hm = C("hm64")
                if st == 1:
                    dve.wait_ge(sem("center_ready"), l + 1)
                    for e in range(4):
                        scaled(s0c[:, e, :], s0r[:, e, :], ecr[:, e:e + 1])
                for d in range(2):
                    dve.wait_ge(sem("decays_ready"), 2 * (k - 1) + d + 1)
                    for i in range(2):
                        v.scalar_tensor_tensor(KR[d][:, :, 0, i, :], kapT[:, :, cols], hm[:, i:i + 1],
                                               Ep[d][:, :, 1, :], ALU.mult, ALU.mult)
                        v.scalar_tensor_tensor(KR[d][:, :, 1, i, :], rT[:, :, cols], hm[:, i:i + 1],
                                               Ep[d][:, :, 0, :], ALU.mult, ALU.mult)
                    mul(Bc[d], akT[:, d, :, cols], En[d])
                    end = P - 1 if d == 0 else 0
                    v.tensor_copy(elast[:, 2 * d:2 * d + 2], Ep[d][:, :, 0, end])
                    mul(KcR[d], ktT[:, d, :, cols], En[d]).then_inc(sem("khat_ready"), 1)
                for d in range(2):
                    dve.wait_ge(sem("mats_done"), 2 * (k - 1) + d + 1)
                    mask = C(f"mask{d}").rearrange("p (x i t) -> p x i t", x=2, i=2)
                    for c in range(2):
                        mul(MTQ[d][:, c], bk(2 + c, 2, 2, P), mask)
                    mul(Tm[d], bk(6, 4, P), over(C(f"lv0{d}"), 4))
                    for c in range(2):
                        last = mul(AKQ[d][:, c], bk(4 + c, 2, 2, P), mask)
                    chained(last)
                    for c in range(2):
                        mul(TmT[d][:, 2 * c:2 * c + 2, :], MTQ[d][:, c, 0], over(C(f"lv0T{d}"), 2))
                    chained(add(Tm[d], Tm[d], over(C("ident"), 4)))
                    add(TmT[d], TmT[d], over(C("ident"), 4)).then_inc(sem("mats_read"), 1)
                for j in range(1, LEVELS + 1):
                    n = (k - 1) * LEVELS + j
                    for d in range(2):
                        dve.wait_ge(sem(f"inv_MT{d}"), n)
                        mul(P1[d], bk(2 + 3 * d, 4, P), over(C(f"lv{j}"), 4)).then_inc(sem(f"inv_P{d}"), 1)
                    for d in range(2):
                        dve.wait_ge(sem(f"inv_TP{d}"), n)
                        if j < LEVELS:
                            sub(Tm[d], Tm[d], bk(3 + 3 * d, 4, P))
                        sub(TmT[d], TmT[d], bk(4 + 3 * d, 4, P)).then_inc(sem(f"inv_T{d}"), 1)
                if st == 0:
                    dve.wait_ge(sem("x_done"), 2 * k)
                    for d in range(2):
                        for c in range(2):
                            e = 2 * d + c
                            scaled(K2T[:, 0, e, :], KcR[d][:, c, :], elast[:, e:e + 1])
                            last = scaled(K2T[:, 1, e, :], Bc[d][:, c, :], elast[:, e:e + 1])
                    last.then_inc(sem("k2_ready"), 1)
                    dve.wait_ge(sem("k2T_done"), l + 1)
                    v.tensor_copy(K2n[0], bk(2, 4, P))
                    v.tensor_copy(K2n[1], bk(3, 4, P)).then_inc(sem("k2n_ready"), 1)
                    dve.wait_ge(sem("fs_done"), l + 1)
                    v.tensor_copy(fstate[:], bk(7, 2, 2, P)).then_inc(sem("fstate_ready"), 1)

            def norm_and_gla(l):
                dve.wait_ge(sem("gn_mean"), l + 1)
                chained(sub(yT, yT, bk(2, 2, TOK)))
                mul(rtmp, yT, yT).then_inc(sem("gn_sq"), 1)
                dve.wait_ge(sem("gl_done"), l + 1)
                v.tensor_scalar(gtm, bank[5][:, :], 0.0, None, ALU.min)
                chained(v.tensor_scalar(glog, bank[5][:, :], 0.0, None, ALU.max))
                sub(glog, gtm, glog).then_inc(sem("gabs_ready"), 1)
                dve.wait_ge(sem("gn_var"), l + 1)
                v.tensor_scalar(rtmp2, bk(3, 2, TOK), GN_EPS, None, ALU.add).then_inc(sem("root_in"), 1)
                dve.wait_ge(sem("gln_ready"), l + 1)
                sub(glog, gtm, glog).then_inc(sem("glog_ready"), 1)
                finish_root(rtmp2)
                chained(mul(yT, yT, rtmp2))
                for c in range(2):
                    last = scaled(yT[:, c, :], yT[:, c, :], rv[:, l, 10 + c:11 + c], rv[:, l, 12 + c:13 + c])
                chained(last)
                chained(add(yT, yT, bonT))
                mul(obT[:], yT, gT).then_inc(sem("rwkv_out"), 1)
                dve.wait_ge(sem("rwkv_out"), l + 1)
                dve.wait_ge(sem("gdecay_ready"), l + 1)
                for st in range(2):
                    for d in range(2):
                        x = 2 * st + d
                        cols = slice(P * st, P * st + P)
                        mul(KcG[:, x, :], ckT[:, cols], EGn[:, x, :])
                        chained(v.scalar_tensor_tensor(Qh, cqT[:, cols], 32.0 ** -0.5, EG[:, x, :],
                                                       ALU.mult, ALU.mult))
                        for h in range(4):
                            last = scaled(Qx[:, x, h, :], Qh, C("hm32")[:, h:h + 1])
                        chained(last)
                for d in range(2):
                    end = P - 1 if d == 0 else 0
                    scaled(s0gc[:, d, :], s0g[:, d, :], ecg[:, d:d + 1])
                    last = scaled(K2g[:, d, :], KcG[:, d, :], EG[:, d, end:end + 1])
                last.then_inc(sem("gq_ready"), 1)
                dve.wait_ge(sem("att_done"), l + 1)
                for x in range(4):
                    last = mul(attT[:, x], bk(4 + x, 4, P), over(C(f"mask{x % 2}")[:, 256:384], 4))
                last.then_inc(sem("att_ready"), 1)
                dve.wait_ge(sem("go_done"), l + 1)
                chained(v.tensor_copy(oc, bank[2][:, :]))
                mul(gsq, oc, oc).then_inc(sem("gsq_ready"), 1)
                dve.wait_ge(sem("k2g_done"), l + 1)
                v.tensor_copy(K2gn, bk(3, 2, P)).then_inc(sem("k2g_ready"), 1)
                dve.wait_ge(sem("gs_done"), l + 1)
                v.tensor_copy(gstate[:], bk(4, 2, 256)).then_inc(sem("gstate_ready"), 1)
                dve.wait_ge(sem("gms_done"), l + 1)
                inverse_root(gtm, bank[5][:, :], LN_EPS)
                chained(mul(oc, oc, gtm))
                v.scalar_tensor_tensor(ocT[:], shaped(oc, (2, TOK)), rv[:, l, 14:15], ogs[:], ALU.mult, ALU.mult)\
                    .then_inc(sem("gla_out"), 1)

            def merge(l):
                evacuated(dve, l, "gate11")
                for br, tile in enumerate(["up_a1", "up_b", "up_c"]):
                    dve.wait_ge(sem("tile_used"), tile_number(l, tile))
                    if br > 0:
                        dve.wait_ge(sem("up_read"), 2 * l + br)
                    for b in range(4):
                        ps = bk((4 if br == 1 else 0) + b, 2, TOK)
                        last = mul((merged if br == 0 else mtmp)[:, 2 * b:2 * b + 2, :], ps, gate_tile(l, 4 * br + b))
                        if br == 2:
                            chained(last)
                            two = merged[:, 2 * b:2 * b + 2, :]
                            last = add(two, two, mtmp[:, 2 * b:2 * b + 2, :])
                            last.then_inc(sem("merged_ready"), 1)
                    if br == 1:
                        chained(last)
                        last = add(merged, merged, mtmp)
                    if br < 2:
                        last.then_inc(sem("up_read"), 1)

            def layer_norm(n, last_norm=False):
                l, half = n // 2, n % 2

                def f(m, cols):
                    return accT[:, m, cols] if last_norm else bk(4 + m // 2, 2, TOK)[:, m % 2, cols]

                if n > 0:
                    dve.wait_ge(sem("x_ready"), n)
                for m in range(KC):
                    for st in range(2):
                        cols = slice(P * st, P * st + P)
                        last = v.scalar_tensor_tensor(yLN[:, m, cols], f(m, cols),
                                                      mod[:, l, 24 * half + 16 + m, st:st + 1], xT[:, m, cols],
                                                      ALU.mult, ALU.add)
                    if m % 2 == 1:
                        last.then_inc(sem("ln_y"), 1)
                dve.wait_ge(sem("ln_mean"), n + 1)
                for c in range(4):
                    two = yLN[:, 2 * c:2 * c + 2, :]
                    sub(two, two, over(bank[0][:, 0:TOK], 2)).then_inc(sem("ln_centered"), 1)
                finish_root(rstd)
                for c in range(4):
                    two = yLN[:, 2 * c:2 * c + 2, :]
                    mul(two, two, over(rstd, 2)).then_inc(sem("ln_normed"), 1)
                    if last_norm:
                        continue
                    dve.wait_ge(sem("ln_normed"), 4 * n + c + 1)
                    for m in (2 * c, 2 * c + 1):
                        for st in range(2):
                            cols = slice(P * st, P * st + P)
                            last = scaled(hT[:, m, cols], yLN[:, m, cols], hgb[:, n, 0, m, st:st + 1],
                                          hgb[:, n, 1, m, st:st + 1])
                    last.then_inc(sem("h_ready"), 1)

            def dense_hidden(e, r, u, par, first=False):
                dve.wait_ge(sem("dense_sig"), u + 1)
                if not first:
                    dve.wait_ge(sem("dense_d_used"), u - 1)
                mul(sgt[par], sgt[par], bk(2 * par, 2, TOK)).then_inc(sem("dense_step"), 1)
                dve.wait_ge(sem("dense_step"), u + 1)
                mul(hid[par], sgt[par], bk(2 * par + 1, 2, TOK)).then_inc(sem("dense_hid"), 1)

            def select(p):
                place = ptab[:, :, bass.ds(p, 1)].to_broadcast([P, 2, P])
                gate = gtab[:, :, bass.ds(p, 1)].to_broadcast([P, 2, P])
                v.tensor_tensor(sel, over_streams(C("iota")), place, ALU.is_equal).then_inc(sem("moe_match"), 1)
                dve.wait_ge(sem("moe_match"), p + 1)
                mul(selg, sel, gate).then_inc(sem("moe_sel"), 1)

            def over_streams(a):
                return a.unsqueeze(1).to_broadcast([P, 2, P])

            def route():
                dve.wait_ge(sem("logits_done"), 1)
                for st in range(2):
                    last = v.tensor_copy(lg[:, st, :], bank[st][:, 0:NE])
                chained(last)
                for st in range(2):
                    last = v.max(top8[:, st, :], lg[:, st, :])
                chained(last)
                for st in range(2):
                    last = v.max_index(idxu[:, st, :], top8[:, st, :], lg[:, st, :])
                sub(gap[:, 0, :], top8[:, :, 1], top8[:, :, 0]).then_inc(sem("gap_ready"), 1)
                dve.wait_ge(sem("gap_ready"), 1)
                chained(v.tensor_copy(idxf, idxu[:]))
                for st in range(2):
                    v.tensor_scalar(lg[:, st, :], C("iota8"), idxf[:, st, 0:1], None, ALU.is_equal)
                    last = v.tensor_scalar(pick2[:, st, :], C("iota8"), idxf[:, st, 1:2], None, ALU.is_equal)
                chained(last)
                add(member, lg, pick2).then_inc(sem("member_ready"), 1)
                dve.wait_ge(sem("gap_exp"), 1)
                chained(v.tensor_scalar(gap[:, 1, :], gap[:, 0, :], 1.0, None, ALU.add))
                chained(v.reciprocal(gap[:, 1, :], gap[:, 1, :]))
                chained(mul(gap[:, 0, :], gap[:, 0, :], gap[:, 1, :]))
                chained(mul(gts, lg, over_last(gap[:, 1, :])))
                chained(mul(pick2, pick2, over_last(gap[:, 0, :])))
                chained(add(gts, gts, pick2))
                v.memset(ptab, -1.0)
                chained(v.memset(gtab, 0.0))
                v.tensor_copy(gtab[:, :, 0:NE], gts)
                dve.wait_ge(sem("slots_done"), 1)
                slots = bk(2, 3, NE)
                v.scalar_tensor_tensor(slotno, slots[:, 0:2, :], 1.0, member, ALU.add, ALU.mult)
                chained(v.tensor_scalar(crowded, slots[:, 2, :], float(P), None, ALU.is_gt))
                chained(v.tensor_scalar(ptab[:, :, 0:NE], slotno, -1.0, None, ALU.add))
                select(0)
                chained(v.memset(rank, 0.0))
                for e in range(1, NE):
                    chained(add(rank[:, e:e + 1], rank[:, e - 1:e], crowded[:, e - 1:e]))
                chained(v.tensor_reduce(evf[:, 0:1], crowded, AX.X, ALU.add))
                chained(v.scalar_tensor_tensor(slotno, member, -float(P), slotno, ALU.mult, ALU.add))
                for j in range(OVER):
                    chained(v.scalar_tensor_tensor(onehot, rank, float(j), crowded, ALU.is_equal, ALU.mult))
                    for table, source in ((ptab, slotno), (gtab, gts)):
                        chained(mul(rtab, source, onehot.unsqueeze(1).to_broadcast([P, 2, NE])))
                        chained(v.tensor_reduce(table[:, :, NE + j], rtab, AX.X, ALU.add))
                    chained(v.tensor_scalar(ptab[:, :, NE + j], ptab[:, :, NE + j], -1.0, None, ALU.add))
                    chained(mul(rtab[:, 0, :], C("iota8"), onehot))
                    chained(v.tensor_reduce(evf[:, j + 1:j + 2], rtab[:, 0, :], AX.X, ALU.add))
                v.tensor_copy(passes_i[:], evf).then_inc(sem("passes_known"), 1)

            def over_last(a):
                return a.unsqueeze(2).to_broadcast([P, 2, NE])

            def experts():
                v.memset(accT, 0.0).then_inc(sem("moe_acc"), 1)
                dve.sem_inc(sem("moe_hid"), 2)
                dve.sem_inc(sem("moe_y"), 1)

                def hidden(par, u):
                    dve.wait_ge(sem("moe_sig"), u + 1)
                    dve.wait_ge(sem("moe_hidT"), u + 1)
                    mul(msig[par], msig[par], bank[par][:, 0:TW]).then_inc(sem("moe_silu"), 1)
                    dve.wait_ge(sem("moe_silu"), u + 1)
                    mul(mhid[par], msig[par], bank[par][:, TW:2 * TW]).then_inc(sem("moe_hid"), 1)

                n_pass = second_passes(dve) + NE
                with dve.Fori(0, n_pass) as p:
                    dve.wait_ge(sem("moe_selT_done"), p + 1)
                    select(p + 1)
                    with dve.Fori(0, EXPERT_UNITS // 2) as i:
                        for par in range(2):
                            hidden(par, p * EXPERT_UNITS + i * 2 + par)
                    dve.wait_ge(sem("moe_d_used"), (p + 1) * EXPERT_UNITS + 2)
                    v.tensor_copy(ysb[:, 0:512], bank[4][:, :])
                    v.tensor_copy(ysb[:, 512:1024], bank[5][:, :]).then_inc(sem("moe_y"), 1)
                    dve.wait_ge(sem("moe_acc"), p * 4 + 1)
                    for b in range(4):
                        dve.wait_ge(sem("moe_back"), p * 4 + (b + 1))
                        add(accT[:, 2 * b:2 * b + 2, :], accT[:, 2 * b:2 * b + 2, :], bk([2, 3, 6, 7][b], 2, TOK))\
                            .then_inc(sem("moe_acc"), 1)
                dve.wait_ge(sem("moe_acc"), n_pass * 4 + 1)
                dve.wait_ge(sem("moe_selT"), n_pass + 1)

            for l in range(L):
                if l == 0:
                    modulate_input()
                project(l, ["q0", "q1", "kv"])
                attention(l)
                rwkv_inputs(l)
                for st in range(2):
                    rwkv_stream(l, st)
                if l == 0:
                    dve.wait_ge(sem("ada_turned"), L * ADA_TILES)
                    take_modulations(0, 24, 48, 0)
                    take_modulations(1, 0, 48, 48)
                    v.memset(zeros[:, 0:1], 0.0).then_inc(sem("mod_read"), 1)
                    fuse_modulations()
                norm_and_gla(l)
                merge(l)
                dve.wait_ge(sem("tile_used"), tile_number(l, "out3"))
                layer_norm(2 * l)
                if l == 0:
                    dense_loop(dve, dense_hidden)
                    dve.wait_ge(sem("dense_d_used"), DENSE_UNITS)
                    layer_norm(1)
                else:
                    route()
                    experts()
                    layer_norm(3, last_norm=True)


def lay_out(x):
    def chunks(a):
        a = np.asarray(a)
        a = a.reshape(a.shape[:-1] + (a.shape[-1] // P, P))
        return np.ascontiguousarray(np.moveaxis(a, -1, 0))

    g = {}
    xs = np.concatenate([x["x_prompt"][0], x["x_sample"][0]], 0)
    g["xT"] = np.ascontiguousarray(chunks(xs).transpose(0, 2, 1))
    cc = np.stack([x["c_ctx"], x["c"][0]], 0)
    g["cT"] = np.ascontiguousarray(chunks(cc).transpose(0, 2, 1))
    g["bada"] = chunks(x["b_ada"])
    g["lnp"] = chunks(np.stack([x["ln1_g"], x["ln1_b"], x["ln2_g"], x["ln2_b"]], 1))
    rows = [chunks(x["rwkv_a0"]).reshape(P, L, 4)]
    for n in ["rwkv_k_k", "rwkv_k_a"]:
        rows.append(chunks(x[n]))
    rows.append(chunks(x["rwkv_r_k"].reshape(L, 256)))
    for n in ["rwkv_ln_g", "rwkv_ln_b"]:
        rows.append(chunks(x[n]))
    rows.append(chunks(np.concatenate([x["gla_norm_g"], x["gla_norm_g"]], 1)))
    g["rv"] = np.ascontiguousarray(np.concatenate(rows, 2))
    g["w0row"] = np.ascontiguousarray(x["rwkv_w0"].reshape(1, L, 512))
    g["glbrow"] = np.ascontiguousarray(x["gla_gate_bias"].reshape(1, L, 256))
    sink = x["attn_sink"].reshape(L, 2, 4).transpose(0, 2, 1).reshape(1, L, 8)
    g["sinkB"] = np.ascontiguousarray(np.broadcast_to(sink, (P, L, 8)))

    def on_diagonal(a):
        _, nd, r, n = a.shape
        out = np.zeros((nd * r, L, nd * n), a.dtype)
        for d in range(nd):
            out[d * r:(d + 1) * r, :, d * n:(d + 1) * n] = a[:, d].transpose(1, 0, 2)
        return out

    g["wbB"] = on_diagonal(x["rwkv_w_b"])
    g["abB"] = on_diagonal(x["rwkv_a_b"])
    g["glb"] = on_diagonal(x["gla_gate_b"])
    g["gbw"] = np.ascontiguousarray(x["rwkv_g_b"].transpose(1, 0, 2))
    s = x["state_rwkv"][0].reshape(L, 2, 2, 2, 64, 64)
    g["s0r"] = np.ascontiguousarray(s.transpose(3, 5, 0, 1, 2, 4)).reshape(P, L, 4, 64)
    g["s0g"] = np.ascontiguousarray(x["state_gla"][0].transpose(2, 3, 0, 1, 4)).reshape(P, L, 2, 64)
    g["kcT"] = np.ascontiguousarray(x["cache_attn_k"][0].transpose(2, 3, 0, 1)).reshape(P, L, P)
    g["vc"] = np.ascontiguousarray(x["cache_attn_v"][0].transpose(1, 0, 2, 3)).reshape(P, L, P)
    g["router"] = np.ascontiguousarray(x["moe_router"][0].reshape(KC, P, NE).transpose(1, 0, 2))
    g["cst"] = build_constants()
    for n in ["w_ada", "w_in", "rwkv_w_a", "rwkv_a_a", "rwkv_g_a", "gla_gate_a", "w_up_a", "w_up_b", "w_up_c",
              "w_out", "ffn_w_gate", "ffn_w_up", "ffn_w_down", "moe_w_gate", "moe_w_up", "moe_w_down"]:
        g[n] = np.ascontiguousarray(x[n])
    return g


OUTS = {"yT": (P, KC, TOK), "kT": (L, P, P), "v": (L, P, P), "rwkv": (1, L, 2, 4, 64, 64), "gla": (1, L, 2, 4, 32, 64)}


def kernel(**inputs):
    import concourse.bacc as bacc
    from concourse.bass_utils import run_bass_kernel_spmd

    x = {n: np.asarray(a) for n, a in inputs.items()}
    arrays = lay_out(x)
    nc = bacc.Bacc("TRN2", target_bir_lowering=False, num_devices=1)
    ins = {n: nc.dram_tensor(f"in_{n}", a.shape, mybir.dt.from_np(a.dtype), kind="ExternalInput").ap()
           for n, a in arrays.items()}
    outs = {n: nc.dram_tensor(f"out_{n}", s, F32, kind="ExternalOutput").ap() for n, s in OUTS.items()}
    build_program(nc, ins, outs)
    r = run_bass_kernel_spmd(nc, [{f"in_{n}": a for n, a in arrays.items()}], core_ids=[0]).results[0]
    y = r["out_yT"].transpose(2, 1, 0).reshape(TOK, D)
    k = r["out_kT"].transpose(0, 2, 1).reshape(1, L, P, 2, 64)
    val = r["out_v"].reshape(1, L, P, 2, 64)
    return (np.ascontiguousarray(y[None, 0:P]), np.ascontiguousarray(y[None, P:]), np.ascontiguousarray(k),
            val, r["out_rwkv"], r["out_gla"])
```
